# Optimizing a Trainium2 kernel written in Bass

```python
import jax
import jax.numpy as jnp
from jax import lax
import numpy as np

D_MODEL = 1024
BATCH = 1
SEQ = 1024
DEPTH = 1

N_MIXERS = 4
GROUP_W = D_MODEL // N_MIXERS
D_MIX = N_MIXERS * GROUP_W
NORM_EPS = 1e-6
POOL_WINDOWS = (2, 4, 8, 16)
POOL_CG = GROUP_W // 4
HEAD_DIM = 64
ATT_HEADS = GROUP_W // HEAD_DIM
ATT_KV_HEADS = 2
ATT_WINDOW = 128
ATT_BLOCK = 128
CONV_W = 3
RWKV_HEAD = 64
RWKV_HEADS = GROUP_W // RWKV_HEAD
LORA_W = 32
LORA_A = 32
LORA_V = 32
LORA_G = 64
RWKV_GN_EPS = 64e-5
N_A = GROUP_W
N_B = (ATT_HEADS + 2 * ATT_KV_HEADS) * HEAD_DIM
N_C = 3 * GROUP_W
N_D = 3 * GROUP_W + LORA_W + LORA_A + LORA_G
N_IN = N_A + N_B + N_C + N_D
N_GROUPS = 4
EXP_PER_GROUP = 8
N_EXPERTS = N_GROUPS * EXP_PER_GROUP
TOP_K_IN_GROUP = 2
D_EXPERT = 128

kernel_name = 'hybrid_parallel_heads_hmoe'

def rms_norm(x, g):
    xf = x.astype(jnp.float32)
    y = xf * lax.rsqrt(jnp.mean(xf * xf, axis=-1, keepdims=True) + NORM_EPS)
    return (y * g.astype(jnp.float32)).astype(x.dtype)

def pool_mixer(u, w_pool, scale):
    B, T, _ = u.shape
    uf = u.astype(jnp.float32).reshape(B, T, len(POOL_WINDOWS), POOL_CG)
    cs = jnp.cumsum(uf, axis=1)
    count = jnp.arange(1, T + 1, dtype=jnp.float32)[None, :, None]
    diffs = []
    for j, w in enumerate(POOL_WINDOWS):
        cj = cs[:, :, j]
        prev = jnp.pad(cj, ((0, 0), (w, 0), (0, 0)))[:, :T]
        diffs.append((cj - prev) / jnp.minimum(count, w) - uf[:, :, j])
    d = jnp.stack(diffs, axis=2)
    y = jnp.einsum('btgc,gce->btge', d, w_pool.astype(jnp.float32)).reshape(B, T, GROUP_W)
    return (y * scale.astype(jnp.float32)).astype(u.dtype)

def swa_sink_attention(q, k, v, sinks):
    B, T, H, hd = q.shape
    KVH = k.shape[2]
    G = H // KVH
    nb = T // ATT_BLOCK
    f32 = jnp.float32
    qb = q.astype(f32).reshape(B, nb, ATT_BLOCK, KVH, G, hd) * (hd ** -0.5)

    def band(z):
        zp = jnp.pad(z.astype(f32), ((0, 0), (ATT_BLOCK, 0), (0, 0), (0, 0)))
        zp = zp.reshape(B, nb + 1, ATT_BLOCK, KVH, hd)
        return jnp.concatenate([zp[:, :-1], zp[:, 1:]], axis=2)

    kb, vb = band(k), band(v)
    s = jnp.einsum('bnqhgd,bnkhd->bnhgqk', qb, kb)
    qi = jnp.arange(ATT_BLOCK)[:, None]
    ki = jnp.arange(2 * ATT_BLOCK)[None, :]
    dist = qi + ATT_BLOCK - ki
    kpos = (jnp.arange(nb)[:, None, None] - 1) * ATT_BLOCK + ki
    valid = (dist >= 0) & (dist < ATT_WINDOW) & (kpos >= 0)
    slopes = (2.0 ** (-8.0 * jnp.arange(1, H + 1, dtype=f32) / H)).reshape(KVH, G)
    s = s - slopes[:, :, None, None] * dist.astype(f32)
    s = jnp.where(valid[None, :, None, None], s, -jnp.inf)
    sink = sinks.astype(f32).reshape(KVH, G)[None, None, :, :, None, None]
    m = jnp.maximum(jnp.max(s, axis=-1, keepdims=True), sink)
    p = jnp.exp(s - m)
    p = p / (jnp.sum(p, axis=-1, keepdims=True) + jnp.exp(sink - m))
    o = jnp.einsum('bnhgqk,bnkhd->bnqhgd', p, vb)
    return o.reshape(B, T, H * hd).astype(q.dtype)

def short_gated_conv(bg, cg, xin, conv_w):
    z = cg * xin
    y = lax.conv_general_dilated(z, conv_w[:, None, :], window_strides=(1,),
                                 padding=[(CONV_W - 1, 0)],
                                 dimension_numbers=('NWC', 'WIO', 'NWC'),
                                 feature_group_count=GROUP_W)
    return bg * y

def rwkv7_time_mix(p, v_first, mu, w0, w2, a0, a2, g2, k_k, k_a, r_k, ln_g, ln_b, v_res):
    f32 = jnp.float32
    B, T, _ = p.shape
    H, N = RWKV_HEADS, RWKV_HEAD
    p = p.astype(f32)
    prev = jnp.pad(p, ((0, 0), (1, 0), (0, 0)))[:, :-1]
    z = p + (prev - p) * mu.astype(f32)
    cuts = [GROUP_W, 2 * GROUP_W, 3 * GROUP_W, 3 * GROUP_W + LORA_W, 3 * GROUP_W + LORA_W + LORA_A]
    r, k, v, wd, ad, gd = jnp.split(z, cuts, axis=-1)
    w = -jax.nn.softplus(-(w0.astype(f32) + jnp.tanh(wd) @ w2.astype(f32))) - 0.5
    decay = jnp.exp(-jnp.exp(w))
    a = jax.nn.sigmoid(a0.astype(f32) + ad @ a2.astype(f32))
    g = jax.nn.sigmoid(gd) @ g2.astype(f32)
    if v_res is None:
        v_first = v
    else:
        v0, v1, v2 = v_res
        v = v + (v_first - v) * jax.nn.sigmoid(v0.astype(f32) + (v @ v1.astype(f32)) @ v2.astype(f32))

    def heads(t):
        return t.reshape(B, T, H, N)

    kk = heads(k * k_k.astype(f32))
    kk = kk / jnp.maximum(jnp.sqrt(jnp.sum(kk * kk, axis=-1, keepdims=True)), 1e-12)
    k = k * (1.0 + (a - 1.0) * k_a.astype(f32))

    def step(S, inp):
        r_t, w_t, k_t, v_t, kk_t, a_t = inp
        sa = jnp.einsum('bhij,bhj->bhi', S, -kk_t)
        S = (S * w_t[:, :, None, :] + sa[..., :, None] * (kk_t * a_t)[:, :, None, :]
             + v_t[..., :, None] * k_t[..., None, :])
        return S, jnp.einsum('bhij,bhj->bhi', S, r_t)

    def tm(t):
        return jnp.moveaxis(heads(t), 1, 0)

    S0 = jnp.zeros((B, H, N, N), f32)
    _, y = lax.scan(step, S0, (tm(r), tm(decay), tm(k), tm(v), jnp.moveaxis(kk, 1, 0), tm(a)))
    y = jnp.moveaxis(y, 0, 1)
    mean = jnp.mean(y, axis=-1, keepdims=True)
    var = jnp.mean(jnp.square(y - mean), axis=-1, keepdims=True)
    y = ((y - mean) * lax.rsqrt(var + RWKV_GN_EPS)).reshape(B, T, GROUP_W)
    y = y * ln_g.astype(f32) + ln_b.astype(f32)
    bonus = (jnp.sum(heads(r * k * r_k.astype(f32)), axis=-1, keepdims=True) * heads(v)).reshape(B, T, GROUP_W)
    return (y + bonus) * g, v_first

def hier_moe(h, w_grp, b_grp, w_exp, b_exp, w_gate, w_up, w_down):
    B, T, D = h.shape
    f32 = jnp.float32
    hf = h.reshape(B * T, D)
    grp_prob = jax.nn.softmax((hf @ w_grp).astype(f32) + b_grp.astype(f32), axis=-1)
    gp, gi = lax.top_k(grp_prob, 1)
    exp_logits = ((hf @ w_exp).astype(f32) + b_exp.astype(f32)).reshape(-1, N_GROUPS, EXP_PER_GROUP)
    in_grp = jnp.take_along_axis(exp_logits, gi[:, :, None], axis=1)[:, 0]
    ev, ei = lax.top_k(in_grp, TOP_K_IN_GROUP)
    wts = jax.nn.softmax(ev, axis=-1) * gp
    eidx = gi * EXP_PER_GROUP + ei
    gates = jnp.einsum('nk,nke->ne', wts, jax.nn.one_hot(eidx, N_EXPERTS, dtype=f32))
    hg = jnp.einsum('nd,edf->nef', hf, w_gate)
    hu = jnp.einsum('nd,edf->nef', hf, w_up)
    act = jax.nn.silu(hg) * hu * gates[:, :, None].astype(h.dtype)
    y = jnp.einsum('nef,efd->nd', act, w_down)
    return y.reshape(B, T, D)

def setup_inputs(seed: int = 0) -> dict:
    key = jax.random.key(seed)
    keys = jax.random.split(key, 48)
    counter = [0]
    f32 = jnp.float32
    L, D = DEPTH, D_MODEL

    def nxt():
        kk = keys[counter[0]]
        counter[0] += 1
        return kk

    def nrm(shape, scale):
        return jax.random.normal(nxt(), shape, f32) * scale

    def unif(shape, lo, hi):
        return jax.random.uniform(nxt(), shape, f32, lo, hi)

    return {
        'x': nrm((BATCH, SEQ, D), 1.0),
        'c': nrm((BATCH, D), 1.0),
        'w_ada': nrm((L, D, 6 * D), 0.5 * D ** -0.5),
        'b_ada': nrm((L, 6 * D), 0.02),
        'norm1_g': 1.0 + nrm((L, D), 0.05),
        'norm2_g': 1.0 + nrm((L, D), 0.05),
        'w_in': nrm((L, D, N_IN), D ** -0.5),
        'w_out': nrm((L, D_MIX, D), D_MIX ** -0.5),
        'pool_w': nrm((L, len(POOL_WINDOWS), POOL_CG, POOL_CG), POOL_CG ** -0.5),
        'pool_scale': unif((L, GROUP_W), 0.5, 1.5),
        'attn_sinks': nrm((L, ATT_HEADS), 0.5),
        'conv_w': nrm((L, CONV_W, GROUP_W), CONV_W ** -0.5),
        'rwkv_mu': unif((L, N_D), 0.0, 1.0),
        'rwkv_w0': unif((L, GROUP_W), -6.0, -0.5),
        'rwkv_w2': nrm((L, LORA_W, GROUP_W), 0.5 * LORA_W ** -0.5),
        'rwkv_a0': nrm((L, GROUP_W), 0.1),
        'rwkv_a2': nrm((L, LORA_A, GROUP_W), 0.5 * LORA_A ** -0.5),
        'rwkv_g2': nrm((L, LORA_G, GROUP_W), LORA_G ** -0.5),
        'rwkv_k_k': 0.85 + nrm((L, GROUP_W), 0.05),
        'rwkv_k_a': 1.0 + nrm((L, GROUP_W), 0.05),
        'rwkv_r_k': nrm((L, GROUP_W), 0.1),
        'rwkv_ln_g': 1.0 + nrm((L, GROUP_W), 0.05),
        'rwkv_ln_b': nrm((L, GROUP_W), 0.02),
        'rwkv_v0': nrm((L - 1, GROUP_W), 0.1),
        'rwkv_v1': nrm((L - 1, GROUP_W, LORA_V), GROUP_W ** -0.5),
        'rwkv_v2': nrm((L - 1, LORA_V, GROUP_W), 0.5 * LORA_V ** -0.5),
        'moe_w_grp': nrm((L, D, N_GROUPS), D ** -0.5),
        'moe_b_grp': nrm((L, N_GROUPS), 0.01),
        'moe_w_exp': nrm((L, D, N_EXPERTS), D ** -0.5),
        'moe_b_exp': nrm((L, N_EXPERTS), 0.01),
        'moe_w_gate': nrm((L, N_EXPERTS, D, D_EXPERT), D ** -0.5),
        'moe_w_up': nrm((L, N_EXPERTS, D, D_EXPERT), D ** -0.5),
        'moe_w_down': nrm((L, N_EXPERTS, D_EXPERT, D), D_EXPERT ** -0.5),
        'final_g': 1.0 + nrm((D,), 0.05),
    }

def reference(x, c, w_ada, b_ada, norm1_g, norm2_g, w_in, w_out, pool_w, pool_scale, attn_sinks,
              conv_w, rwkv_mu, rwkv_w0, rwkv_w2, rwkv_a0, rwkv_a2, rwkv_g2, rwkv_k_k, rwkv_k_a,
              rwkv_r_k, rwkv_ln_g, rwkv_ln_b, rwkv_v0, rwkv_v1, rwkv_v2, moe_w_grp, moe_b_grp,
              moe_w_exp, moe_b_exp, moe_w_gate, moe_w_up, moe_w_down, final_g):
    B, T, _ = x.shape
    cond = jax.nn.silu(c)
    v_first = None
    for l in range(DEPTH):
        mod = cond @ w_ada[l] + b_ada[l]
        sh1, sc1, gt1, sh2, sc2, gt2 = [m[:, None, :] for m in jnp.split(mod, 6, axis=-1)]
        h = rms_norm(x, norm1_g[l]) * (1.0 + sc1) + sh1
        p = h @ w_in[l]
        pa, pb, pc, pd = jnp.split(p, [N_A, N_A + N_B, N_A + N_B + N_C], axis=-1)
        ya = pool_mixer(pa, pool_w[l], pool_scale[l])
        q, k, v = jnp.split(pb, [ATT_HEADS * HEAD_DIM, (ATT_HEADS + ATT_KV_HEADS) * HEAD_DIM], axis=-1)
        yb = swa_sink_attention(q.reshape(B, T, ATT_HEADS, HEAD_DIM),
                                k.reshape(B, T, ATT_KV_HEADS, HEAD_DIM),
                                v.reshape(B, T, ATT_KV_HEADS, HEAD_DIM), attn_sinks[l])
        bg, cg, xin = jnp.split(pc, 3, axis=-1)
        yc = short_gated_conv(bg, cg, xin, conv_w[l])
        v_res = None if l == 0 else (rwkv_v0[l - 1], rwkv_v1[l - 1], rwkv_v2[l - 1])
        yd, v_first = rwkv7_time_mix(pd, v_first, rwkv_mu[l], rwkv_w0[l], rwkv_w2[l], rwkv_a0[l],
                                     rwkv_a2[l], rwkv_g2[l], rwkv_k_k[l], rwkv_k_a[l], rwkv_r_k[l],
                                     rwkv_ln_g[l], rwkv_ln_b[l], v_res)
        y = jnp.concatenate([ya, yb, yc, yd.astype(x.dtype)], axis=-1) @ w_out[l]
        x = x + gt1 * y
        h2 = rms_norm(x, norm2_g[l]) * (1.0 + sc2) + sh2
        x = x + gt2 * hier_moe(h2, moe_w_grp[l], moe_b_grp[l], moe_w_exp[l], moe_b_exp[l],
                               moe_w_gate[l], moe_w_up[l], moe_w_down[l])
    return rms_norm(x, final_g)


_drawn_inputs = setup_inputs


def setup_inputs(seed=0):
    import zlib

    import numpy as np

    out = dict(_drawn_inputs(seed))
    spreads = {}
    factors = {'norm2_g': 3.069,
     'attn_sinks': 8.0,
     'rwkv_w2': 8.0,
     'rwkv_a0': 8.0,
     'rwkv_a2': 2.999,
     'rwkv_k_k': 7.026,
     'rwkv_k_a': 7.224,
     'rwkv_ln_g': 8.0,
     'rwkv_ln_b': 8.0,
     'moe_b_grp': 8.0,
     'moe_b_exp': 8.0}
    for name, (base, spread) in spreads.items():
        noise = np.random.default_rng([zlib.crc32(name.encode()), seed]).standard_normal(out[name].shape)
        drawn = base * np.exp(spread * noise) if base else spread * noise
        out[name] = jnp.asarray(drawn.astype(out[name].dtype))
    for name, factor in factors.items():
        out[name] = (out[name] * factor).astype(out[name].dtype)
    return out
```

```python
from contextlib import ExitStack

import numpy as np

import concourse.bass as bass
from concourse import mybir

F32 = mybir.dt.float32
I32 = mybir.dt.int32
U32 = mybir.dt.uint32
ALU = mybir.AluOpType
ACT = mybir.ActivationFunctionType
AX = mybir.AxisListType
ds = bass.ds

P = 128
D = 1024
T = 1024
KD = D // P
NT = T // P
HD = 64
CH = 64
PAD = 16
TW = T + PAD
EPS = 1e-6
GN_EPS = 64e-5
E = 32
GROUPS = 4
EPG = E // GROUPS
FE = 128
CAP = P
OVT = (2 * T - 1) // CAP
TILES = E + OVT
OOB = 1 << 20
NEG = -1e30

B_R, B_K, B_V, B_LORA, B_POOL, B_Q, B_KEY, B_VAL, B_BG, B_CG, B_XI = 0, 2, 4, 6, 7, 9, 11, 12, 13, 15, 17
NB = 19
COL_POOL, COL_ATT, COL_CONV, COL_RWKV = 0, 256, 768, 1536
ZB = 7

R_ADA, R_G1, R_G2, R_MU, R_W0, R_A0, R_KK, R_KA, R_RK, R_LNG, R_LNB, R_PS, R_CW, NR = \
    0, 48, 56, 64, 71, 73, 75, 77, 79, 81, 83, 85, 87, 93
M_SH1, M_SC1, M_GT1, M_SH2, M_SC2, M_GT2 = 0, 8, 16, 24, 32, 40


class Chain:

    def __init__(self, eng, sem):
        self.eng, self.sem, self.base, self.n, self.loop = eng, sem, 0, 0, None

    def at(self):
        return self.base + self.n if self.loop is None else self.loop[0] * self.loop[1] + (self.base + self.n)

    def note(self, ins):
        ins.then_inc(self.sem, 1)
        self.n += 1

    def wait(self):
        self.eng.wait_ge(self.sem, self.at())

    def step(self, ins):
        self.note(ins)
        self.wait()

    def enter(self, reg, per):
        self.base, self.n, self.loop = self.base + self.n, 0, (reg, per)

    def leave(self, turns):
        per = self.loop[1]
        assert self.n == per, (self.n, per)
        self.base, self.n, self.loop = self.base + per * turns, 0, None


def build(nc, w, out):
    ctx = ExitStack()
    with ctx:
        def sb(name, shape, dt=F32):
            return ctx.enter_context(nc.sbuf_tensor(name, shape, dt))

        def sem(name):
            return ctx.enter_context(nc.semaphore(name))

        PS = [ctx.enter_context(nc.psum_tensor(f"bank{i}", [P, 512], F32)) for i in range(8)]

        xn2_d = nc.dram_tensor("xn2_d", [T, D], F32, kind="Internal")
        tbl_d = nc.dram_tensor("tbl_d", [TILES * CAP, 4], I32, kind="Internal")
        y_d = nc.dram_tensor("y_d", [2 * T, D], F32, kind="Internal")

        REG_P = sb("REG_P", [P, NB * TW])
        REG_W = sb("REG_W", [P, 15360])
        REG_Y = sb("REG_Y", [P, 8192])

        def area(reg, at, *shape):
            n = int(np.prod(shape))
            v = reg[:, at:at + n]
            names = "abcd"[:len(shape)]
            if len(shape) > 1:
                v = v.rearrange(f"p ({' '.join(names)}) -> p {' '.join(names)}", **dict(zip(names, shape)))
            return v, at + n

        pT = REG_P[:, :].rearrange("p (b t) -> p b t", b=NB)
        hT, o = area(REG_W, 0, KD, T)
        xin, o = area(REG_W, o, 2, D)
        xn, o = area(REG_W, o, 2, D)
        win, o = area(REG_W, o, 3, KD, P)
        ada, _ = area(REG_Y, 0, 2, KD, 512)
        yT = REG_Y[:, :].rearrange("p (k t) -> p k t", k=KD)
        qz, o = area(REG_W, 0, 4, P)
        vs, o = area(REG_W, o, 2 * P)
        vt, o = area(REG_W, o, 2, P)
        sc, o = area(REG_W, o, 4, 2 * P)
        ptT, o = area(REG_W, o, 4, 2, P)
        pm1, o = area(REG_W, o, TW)
        pm2, o = area(REG_W, o, TW)
        pmd, o = area(REG_W, o, 2, T)
        cvt, o = area(REG_W, o, T)
        W2 = 2 * P
        z, o = area(REG_W, 0, ZB, W2)
        df, o = area(REG_W, o, ZB, W2)
        R1_DF = o
        lw, o = area(REG_W, o, 2, W2)
        Lc, o = area(REG_W, o, 2, W2)
        Lm, o = area(REG_W, o, 2, W2)
        Pc, o = area(REG_W, o, 2, W2)
        Pm = Lm
        iP = Lc
        aa, o = area(REG_W, o, 2, W2)
        gg, o = area(REG_W, o, 2, W2)
        kkr, o = area(REG_W, o, 2, W2)
        rk, o = area(REG_W, o, 2, W2)
        yb, o = area(REG_W, o, 2, W2)
        lt, o = area(REG_W, o, W2)
        KR, o = area(REG_W, o, 2, 2, W2)
        Bt, _ = area(df.rearrange("p a b -> p (a b)"), 0, 2, W2)
        Kt, _ = area(df.rearrange("p a b -> p (a b)"), 2 * W2, 2, W2)
        sq, _ = area(df.rearrange("p a b -> p (a b)"), 4 * W2, 2, W2)
        del R1_DF
        rw, rw_at = [], []
        for n in range(2):
            reg, o = (REG_P, TW * 7) if n == 0 else (REG_P, o)
            t = {}
            rw_at.append(o)
            for name, shape in (("bt", (4, HD)), ("kt", (4, HD)), ("vt", (4, HD)), ("wk", (4, 2, HD)), ("uz", (2, 4, HD)),
                                ("ab", (4, 2, P)), ("ak", (4, 2, P)), ("x", (4, P)), ("xt", (4, P)), ("t1", (4, P)),
                                ("bl", (4, P)), ("re", (2, P))):
                t[name], o = area(reg, o, *shape)
            rw.append(t)
        assert o <= NB * TW
        wo, o = area(REG_P, 0, KD, D)
        x1, o = area(REG_P, o, NT, D)
        xn2, o = area(REG_P, o, 2, D)
        h2T, o = area(REG_P, o, KD, P)
        wg, o = area(REG_W, 0, 4, KD, FE)
        wu, o = area(REG_W, o, 4, KD, FE)
        wd, o = area(REG_W, o, 4, D)
        xg, o = area(REG_Y, 0, 2, D)
        xt, o = area(REG_Y, o, 2, KD, P)
        yo, o = area(REG_Y, o, 2, D)
        th, o = area(REG_Y, o, 2, P)
        a1, o = area(REG_Y, o, 2, P)
        ac, o = area(REG_Y, o, 2, P)
        fg, o = area(REG_Y, o, D)
        disti, _ = area(REG_W, 0, 2 * P)
        disti = disti.bitcast(I32)
        o = 4 * (2 * KD * FE + D)
        rt = {}
        for name, shape in (("ga", (NT, GROUPS)), ("gb", (NT, GROUPS)), ("goh", (NT, GROUPS)), ("xm", (NT, E)), ("ky", (NT, E)),
                            ("oh1", (NT, E)), ("oh2", (NT, E)), ("pos", (NT, E)), ("pre", (NT + 1, E)), ("tmp", (NT, E)),
                            ("cmp", (E * OVT,)), ("i32", (E,)), ("thr", (OVT,)), ("nov", (E,)), ("ci", (E,)), ("ob", (E,))):
            rt[name], o = area(REG_W, o, *shape)
        small = {}
        for name in ("gm", "gi", "gp", "m1", "i1", "m2", "i2", "e2", "q1", "q2", "b1", "b2", "c1", "c2", "g1", "g2"):
            small[name], o = area(REG_W, o, NT)
        assert o <= 15360
        yab, _ = area(REG_W, 0, 2, 2, D)
        fo, _ = area(REG_W, 4096, 2, D)

        ident = sb("ident", [P, P])
        bones = sb("bones", [P, P])
        tri = sb("tri", [P, P])
        ones = sb("ones", [P, P])
        msk = sb("msk", [P, 2, P])
        lmask = sb("lmask", [P, 6, P])
        adist = sb("adist", [P, 2 * P])
        sel = sb("sel", [8, 4, P])
        rmask = sb("rmask", [P, 512])
        rc16 = sb("rc16", [P, 2, PAD])
        cnti = sb("cnti", [P, PAD], I32)
        mhalf = sb("mhalf", [P, 8])
        prow = sb("prow", [NR, P])
        pc = sb("pc", [P, NR])
        pw = sb("pw", [P, 2, P])
        lor = sb("lor", [P, 256])
        wr = sb("wr", [P, KD, GROUPS + E])
        rbias = sb("rbias", [P, GROUPS + E])
        sink = sb("sink", [P, 4])
        cc = sb("cc", [P, KD])
        ct = sb("ct", [P, KD])
        mod = sb("mod", [P, 48])
        s1 = sb("s1", [P, KD])
        s2 = sb("s2", [P, KD])
        hp = sb("hp", [P, 8])
        brk = sb("brk", [P, 2, P])
        gtb = sb("gtb", [P, 2, D])
        ss = sb("ss", [P, 2])
        rs = sb("rs", [P, 2])
        mx = sb("mx", [P, 4])
        nm = sb("nm", [P, 4])
        es = sb("es", [P, 4])
        sm = sb("sm", [P, 4])
        rd = sb("rd", [P, 4])
        nrm = sb("nrm", [P, 8])
        nrp = sb("nrp", [P, 8])
        nrT = sb("nrT", [8, P])
        S = sb("S", [P, 5, 2, HD])
        G = sb("G", [P, 8, P])
        lg = sb("lg", [P, NT, GROUPS + E])
        dg = sb("dg", [P, 2, P])
        tbl = sb("tbl", [P, TILES, 4], I32)
        idx = sb("idx", [P, 4], I32)
        idy = sb("idy", [P, 4], I32)
        junk = sb("junk", [P, 1])

        eidt = sb("eidt", [P, OVT], I32)
        ent = sb("ent", [P, 2 * NT, 4], I32)
        slot = sb("slot", [P, 2 * NT], I32)

        def eid_view(i):
            return eidt[0:1, ds(i, 1)]

        def both(n):
            at = rw_at[n]
            return REG_P[:, at:at + 512]

        def mskb():
            return msk[:, :, :].rearrange("p a t -> p (a t)").unsqueeze(1).to_broadcast([P, 2, 2 * P])

        v = {n: w[n] for n in w}
        xd = v["x"].rearrange("b t d -> (b t) d")
        outd = out.rearrange("b t d -> (b t) d")

        names = ("ld_c ld_prm ld_misc ld_wr const_ready sel_ready chain_pool chain_dve  "
                 "prm_t prm_ready silu_t silu_ready mod1_ps mod1_ready mod2_ps mod2_ready "
                 "ss_ready ms_ready rstd_ready xn_ready hT_tr hT_act hT_dve "
                 "proj_ps proj_act proj_dve pad_ready gt_diag gt_ps gt_ready "
                 "att_q att_qk att_vps att_v  att_nm att_p att_pn att_tp att_tpa att_tpd att_o att_y "
                 "pool_d pool_ps pool_y conv_y  "
                 "w_df w_z w_tanh w_lora w_th w_tha w_sg  w_gg w_L w_exp w_kkr w_sq w_ss w_nrm w_nrp w_nrt w_nrT w_nrb "
                 "w_ops w_tok w_tka w_tkd w_abp w_ab w_akp w_ak w_bl w_xt w_xp w_xa w_t1p w_t1 w_x2p w_w1p w_w1 w_uzp w_uz "
                 "w_gp w_G w_rep w_re w_hp w_S w_yp w_y w_mean w_yc w_bonp  w_yT  "
                 "wo_ld xr_ld op_ps op_x1 op_xn op_tp op_ta op_td op_lg op_lgd "
                 "rt_pos  rt_ent rt_init rt_sc rt_ld rt_n "
                 " m_tx m_xa m_xd m_gu m_th m_act m_dn m_ya m_yd "
                 "ov_w ov_g ov_sc "
                 "rt_c rt_e1 rt_e2 rt_oh ld_fg f_go ov_go f_c att_zero f_x2 f_o").split()
        s = {n: sem(n) for n in names}
        s_ada = [sem(f"ld_ada{i}") for i in range(2)]
        s_x = [sem(f"ld_x{i}") for i in range(2)]
        s_win = [sem(f"ld_win{i}") for i in range(3)]
        s_w = [sem(f"ld_expert{i}") for i in range(4)]
        s_gx = [sem(f"gathered{i}") for i in range(2)]
        s_sc = [sem(f"scattered{i}") for i in range(2)]
        s_st = [sem(f"st_xn2_{i}") for i in range(2)]
        s_fy = [sem(f"ld_y{i}") for i in range(2)]
        s_fo = [sem(f"st_out{i}") for i in range(2)]
        block = ctx.enter_context(nc.Block())

        ada_v = v["w_ada"].rearrange("l (p k) n -> (l p) k n", k=KD)
        win_v = v["w_in"].rearrange("l (k p) n -> (l p) k n", p=P)
        wo_v = v["w_out"].rearrange("l (k p) n -> (l p) k n", p=P)
        wg_v = v["moe_w_gate"].rearrange("l e (k p) f -> p (l e) k f", p=P)
        wu_v = v["moe_w_up"].rearrange("l e (k p) f -> p (l e) k f", p=P)
        wd_v = v["moe_w_down"].rearrange("l e f d -> f (l e) d")

        @block.sync
        def _(sp):
            def row(n, r, k):
                return sp.dma_start(prow[r:r + k, :], v[n])

            sp.dma_start(cc[:, :], v["c"].rearrange("b (p k) -> (b p) k", k=KD)).then_inc(s["ld_c"], 16)

            def load_ada(b):
                sp.dma_start(ada[:, b % 2], ada_v[:, :, b * 512:(b + 1) * 512]).then_inc(s_ada[b % 2], 16)

            load_ada(0)
            rows = [("b_ada", R_ADA, 48), ("norm1_g", R_G1, 8), ("norm2_g", R_G2, 8), ("rwkv_mu", R_MU, 7),
                    ("rwkv_w0", R_W0, 2), ("rwkv_a0", R_A0, 2), ("rwkv_k_k", R_KK, 2), ("rwkv_k_a", R_KA, 2),
                    ("rwkv_r_k", R_RK, 2), ("rwkv_ln_g", R_LNG, 2), ("rwkv_ln_b", R_LNB, 2), ("pool_scale", R_PS, 2)]
            for name, r, k in rows:
                sp.dma_start(prow[r:r + k, :], v[name].rearrange("l (r n) -> (l r) n", n=P)).then_inc(s["ld_prm"], 16)
            sp.dma_start(prow[R_CW:R_CW + 6, :], v["conv_w"].rearrange("l c (r n) -> (l c r) n", n=P)).then_inc(s["ld_prm"], 16)
            load_ada(1)

            def load_x(j):
                sp.dma_start(xin[:, j % 2], xd[j * P:(j + 1) * P, :]).then_inc(s_x[j % 2], 16)

            def load_win(b):
                if b < B_POOL:
                    src = win_v[:, :, COL_RWKV + b * P:COL_RWKV + (b + 1) * P]
                elif b < B_Q:
                    src = win_v[:, :, COL_POOL + (b - B_POOL) * P:COL_POOL + (b - B_POOL + 1) * P]
                elif b < B_KEY:
                    for n in range(2):
                        c0 = COL_ATT + (b - B_Q + 2 * n) * HD
                        sp.dma_start(win[:, b % 3, :, n * HD:(n + 1) * HD], win_v[:, :, c0:c0 + HD]).then_inc(s_win[b % 3], 16)
                    return
                elif b < B_BG:
                    c0 = COL_ATT + 256 + (b - B_KEY) * P
                    src = win_v[:, :, c0:c0 + P]
                else:
                    src = win_v[:, :, COL_CONV + (b - B_BG) * P:COL_CONV + (b - B_BG + 1) * P]
                sp.dma_start(win[:, b % 3], src).then_inc(s_win[b % 3], 32)

            load_x(0)
            load_x(1)
            for b in (2, 3):
                sp.wait_ge(s["mod1_ps"], b - 1)
                load_ada(b)
            for b in range(3):
                load_win(b)
            sp.wait_ge(s["const_ready"], 1)
            for g in range(4):
                h = 64 * (g % 2)
                sp.dma_start(pw[h:h + 64, g // 2, h:h + 64], v["pool_w"][0, g]).then_inc(s["ld_misc"], 16)
            sp.dma_start(lor[0:32, :], v["rwkv_w2"][0]).then_inc(s["ld_misc"], 16)
            sp.dma_start(lor[32:64, :], v["rwkv_a2"][0]).then_inc(s["ld_misc"], 16)
            sp.dma_start(lor[64:128, :], v["rwkv_g2"][0]).then_inc(s["ld_misc"], 16)
            sp.dma_start(sink[:, :], v["attn_sinks"].to_broadcast([P, 4])).then_inc(s["ld_misc"], 16)
            for j in range(2, NT):
                sp.wait_ge(s["xn_ready"], j - 1)
                load_x(j)

            for b in (4, 5):
                sp.wait_ge(s["mod1_ps"], b - 1)
                load_ada(b)
            for b in range(3, NB):
                sp.wait_ge(s["proj_ps"], b - 2)
                load_win(b)
                if b % 3 == 2 and b >= 5 or b == 18:
                    a = {5: 6, 8: 7, 11: 8, 14: 9, 17: 10, 18: 11}[b]
                    sp.wait_ge(s["mod2_ps"], a - 5)
                    load_ada(a)
            sp.dma_start(rbias[:, 0:GROUPS], v["moe_b_grp"].to_broadcast([P, GROUPS])).then_inc(s["ld_wr"], 16)
            sp.dma_start(rbias[:, GROUPS:], v["moe_b_exp"].to_broadcast([P, E])).then_inc(s["ld_wr"], 16)
            sp.dma_start(wr[:, :, 0:GROUPS], v["moe_w_grp"].rearrange("l (k p) n -> (l p) k n", p=P)).then_inc(s["ld_wr"], 16)
            sp.dma_start(wr[:, :, GROUPS:], v["moe_w_exp"].rearrange("l (k p) n -> (l p) k n", p=P)).then_inc(s["ld_wr"], 16)

            sp.wait_ge(s["w_yT"], 5)
            sp.wait_ge(s["conv_y"], 2)
            sp.wait_ge(s["att_y"], NT)
            sp.wait_ge(s["pool_y"], 4)
            sp.dma_start(wo, wo_v).then_inc(s["wo_ld"], 16)
            for j in range(NT):
                sp.dma_start(x1[:, j], xd[j * P:(j + 1) * P, :]).then_inc(s["xr_ld"], 16)

            def load_expert(u, e):
                for dst, src in ((wg, wg_v), (wu, wu_v), (wd, wd_v)):
                    view = src[:, e] if isinstance(e, int) else src[:, ds(e, 1)]
                    d_ = dst[:, u] if isinstance(e, int) else dst[:, u:u + 1]
                    sp.dma_start(d_, view).then_inc(s_w[u], 16)

            for e in range(4):
                load_expert(e, e)
            for j in range(NT):
                sp.wait_ge(s["op_xn"], j + 1)
                sp.dma_start(xn2_d[j * P:(j + 1) * P, :], xn2[:, j % 2]).then_inc(s_st[j % 2], 16)
            sp.wait_ge(s["op_ps"], NT)
            sp.dma_start(fg, v["final_g"].rearrange("(o n) -> o n", o=1).to_broadcast([P, D])).then_inc(s["ld_fg"], 16)
            with sp.Fori(1, E // 4) as g:
                for u in range(4):
                    sp.wait_ge(s["m_dn"], g * 4 + (u - 3))
                    load_expert(u, g * 4 + u)
            sp.wait_ge(s["rt_n"], 1)
            n_ov = sp.value_load(idy[0:1, 0:1], min_val=1, max_val=OVT)
            with sp.Fori(0, n_ov) as i:
                sp.wait_ge(s["ov_go"], i + 1)
                e = sp.value_load(eid_view(i), min_val=0, max_val=E - 1)
                for dst, src in ((wg, wg_v), (wu, wu_v), (wd, wd_v)):
                    sp.dma_start(dst[:, 0:1], src[:, ds(e, 1)]).then_inc(s["ov_w"], 16)
            sp.wait_ge(s["f_go"], 1)
            for j in range(NT):
                if j >= 2:
                    sp.wait_ge(s["f_x2"], j - 1)
                sp.dma_start(yab[:, j % 2, 0], y_d[j * P:(j + 1) * P, :]).then_inc(s_fy[j % 2], 16)
                sp.dma_start(yab[:, j % 2, 1], y_d[T + j * P:T + (j + 1) * P, :]).then_inc(s_fy[j % 2], 16)
                if j >= 1:
                    sp.wait_ge(s["f_o"], j)
                    sp.dma_start(outd[(j - 1) * P:j * P, :], fo[:, (j - 1) % 2]).then_inc(s_fo[(j - 1) % 2], 16)
            sp.wait_ge(s["f_o"], NT)
            sp.dma_start(outd[(NT - 1) * P:, :], fo[:, (NT - 1) % 2]).then_inc(s_fo[(NT - 1) % 2], 16)
            for n in range(2):
                sp.wait_ge(s_fo[n], 16 * NT // 2)


        @block.gpsimd
        def _(gp):
            ch = Chain(gp, s["chain_pool"])

            def keep(o_, in_, pattern, base, cm, op=ALU.is_ge, fill=0.0):
                ch.step(gp.affine_select(out=o_, in_=in_, compare_op=op, fill=fill, base=base, pattern=pattern,
                                         channel_multiplier=cm))

            ch.note(gp.memset(ident[:, :], 0.0))
            ch.note(gp.memset(pw[:, :, :], 0.0))
            ch.note(gp.memset(bones[:, :], 0.0))
            ch.step(gp.memset(ones[:, :], 1.0))
            keep(ident[:, :], ident[:, :], [[-1, P]], 0, 1, ALU.not_equal, 1.0)
            gp.memset(mhalf[:, :], -0.5).then_inc(s["const_ready"], 1)
            keep(tri[:, :], ones[:, :], [[1, P]], -1, -1)
            keep(msk[:, 1, :], ones[:, :], [[1, P]], 0, -1)
            ch.note(gp.memset(bones[0:64, 0:64], 1.0))
            ch.step(gp.memset(bones[64:P, 64:P], 1.0))
            ch.note(gp.tensor_tensor(msk[:, 0, :], tri[:, :], bones[:, :], ALU.mult))
            ch.step(gp.tensor_tensor(msk[:, 1, :], msk[:, 1, :], bones[:, :], ALU.mult))
            ch.step(gp.memset(lmask[:, :, :], 0.0))
            for l in range(6):
                b = 1 << l
                half = lmask[:, l, :].rearrange("p (n h b) -> p n h b", h=2, b=b)[:, :, 1, :]
                ch.step(gp.memset(half, 1.0))
                keep(half, half, [[-2 * b, P // (2 * b)], [0, b]], 0, 1)
                keep(half, half, [[2 * b, P // (2 * b)], [0, b]], b - 1, -1)
            ch.step(gp.iota(disti, pattern=[[1, 2 * P]], base=-P, channel_multiplier=-1))
            ch.step(gp.tensor_copy(adist[:, :], disti))
            keep(adist[:, :], adist[:, :], [[-1, 2 * P]], P, 1, fill=NEG)
            keep(adist[:, :], adist[:, :], [[1, 2 * P]], -1, -1, fill=NEG)
            ch.step(gp.memset(sel[:, :, :], 0.0))
            sv = sel[:, :, :].rearrange("p a (h d) -> p a h d", h=2)
            keep(sv, sv, [[-2, 4], [-1, 2], [0, HD]], 0, 1, ALU.not_equal, 1.0)
            ch.step(gp.memset(rmask[:, :], 1.0))
            ch.step(gp.memset(rmask[:, 0:512:CH], 0.0))
            ch.step(gp.iota(cnti[:, :], pattern=[[1, PAD]], base=1, channel_multiplier=0))
            for c in range(2):
                ch.step(gp.tensor_copy(rc16[:, c, :], cnti[:, :]))
                for h in range(2):
                    rows = rc16[64 * h:64 * h + 64, c, :]
                    ch.step(gp.tensor_scalar(rows, rows, float(2 << (2 * c + h)), None, ALU.min))
            gp.memset(S[:, 4], 0.0)
            gp.memset(G[:, :, :], 0.0)
            ch.note(gp.iota(ent[:, :, 0], pattern=[[P, 2 * NT]], base=0, channel_multiplier=1))
            ch.note(gp.iota(ent[:, :, 1], pattern=[[0, 2], [P, NT]], base=0, channel_multiplier=1))
            ch.note(gp.iota(ent[:, :, 3], pattern=[[0, 2 * NT]], base=0, channel_multiplier=0))
            gp.memset(tbl[:, :, :], OOB).then_inc(s["sel_ready"], 1)

            def power(out_, in_, n, ready, done, count):
                gp.wait_ge(s[ready], count)
                gp.tensor_tensor(out_, in_, mhalf[:, 0:n], ALU.pow).then_inc(s[done], 1)

            gp.wait_ge(s["sel_ready"], 1)
            gp.dma_start(tbl_d[:, :].rearrange("(t p) f -> p t f", p=P), tbl[:, :, :]).then_inc(s["rt_init"], 16)
            for j in range(NT):
                power(rs[:, j % 2:j % 2 + 1], ss[:, j % 2:j % 2 + 1], 1, "ms_ready", "rstd_ready", j + 1)

            gp.memset(pT[:, :, 0:PAD], 0.0).then_inc(s["pad_ready"], 1)

            gp.wait_ge(s["proj_act"], NB)
            gp.wait_ge(s["proj_dve"], NB)
            gp.wait_ge(s["pad_ready"], 1)
            gp.wait_ge(s["rt_c"], 1)
            ch.step(gp.memset(pm1[:, 0:PAD], 0.0))
            ch.step(gp.memset(pm2[:, 0:PAD], 0.0))
            for c in range(2):
                u = pT[:, B_POOL + c]
                src, dst, steps = u, pm1, 2 + 2 * c
                for n in range(steps):
                    sh = 1 << n
                    ch.step(gp.tensor_tensor(dst[:, PAD:], src[:, PAD:], src[:, PAD - sh:TW - sh], ALU.add))
                    if n >= steps - 2:
                        h = n - (steps - 2)
                        r = slice(64 * h, 64 * h + 64)
                        wdt = float(2 * sh)
                        ch.note(gp.tensor_scalar(pmd[r, c, PAD:], dst[r, 2 * PAD:], 1.0 / wdt, None, ALU.mult))
                        ch.step(gp.tensor_tensor(pmd[r, c, 0:PAD], dst[r, PAD:2 * PAD], rc16[r, c, :], ALU.mult))
                    src, dst = dst, (pm2 if dst is pm1 else pm1)
                gp.tensor_tensor(pmd[:, c, :], pmd[:, c, :], u[:, PAD:], ALU.subtract).then_inc(s["pool_d"], 1)
            gp.wait_ge(s["prm_ready"], 1)
            gp.wait_ge(s["mod2_ps"], 8)
            for c in range(2):
                ch.step(gp.tensor_tensor(pm1[:, :], pT[:, B_CG + c], pT[:, B_XI + c], ALU.mult))
                ch.step(gp.tensor_scalar(pm2[:, PAD:], pm1[:, PAD - 2:TW - 2], pc[:, R_CW + c:R_CW + c + 1], None, ALU.mult))
                for n in (1, 2):
                    ch.step(gp.tensor_scalar(cvt, pm1[:, PAD - 2 + n:TW - 2 + n],
                                             pc[:, R_CW + 2 * n + c:R_CW + 2 * n + c + 1], None, ALU.mult))
                    ch.step(gp.tensor_tensor(pm2[:, PAD:], pm2[:, PAD:], cvt, ALU.add))
                gp.tensor_tensor(yT[:, 4 + c, :], pm2[:, PAD:], pT[:, B_BG + c, PAD:], ALU.mult).then_inc(s["conv_y"], 1)
                gp.wait_ge(s["conv_y"], c + 1)

            LB = 6
            with gp.Fori(0, NT // 2) as m:
                prev, at = gp.snap(m * W2 + (PAD - 1)), gp.snap(m * W2 + PAD)
                gp.wait_ge(s["w_yT"], m + 1)
                gp.tensor_tensor(df, pT[:, 0:ZB, ds(prev, W2)], pT[:, 0:ZB, ds(at, W2)], ALU.subtract).then_inc(s["w_df"], 1)
                power(nrp[:, :], nrm[:, :], 8, "w_nrm", "w_nrp", m * 2 + 1)
                for l in range(LB):
                    for n in range(2):
                        if l == 0:
                            gp.wait_ge(s["w_ab"], m * 2 + (n + 1))
                        elif l == 1:
                            gp.wait_ge(s["w_xt"], m * 12 + (n + 1))
                        else:
                            gp.wait_ge(s["w_t1p"], m * 10 + (2 * (l - 2) + n + 1))
                        gp.tensor_tensor(rw[n]["bl"], rw[n]["ab"][:, :, 0, :],
                                         lmask[:, l:l + 1, :].to_broadcast([P, 4, P]), ALU.mult).then_inc(s["w_bl"], 1)
                power(nrp[:, :], nrm[:, :], 8, "w_nrm", "w_nrp", m * 2 + 2)

            for j in range(NT):
                power(rs[:, j % 2:j % 2 + 1], ss[:, j % 2:j % 2 + 1], 1, "ms_ready", "rstd_ready", NT + j + 1)
            gp.wait_ge(s["rt_init"], 16)
            gp.wait_ge(s["rt_ent"], 1)
            for a in range(2 * NT):
                gp.indirect_dma_start(out=tbl_d[:, :], out_offset=bass.IndirectOffsetOnAxis(ap=slot[:, a:a + 1], axis=0),
                                      in_=ent[:, a, :], in_offset=None, bounds_check=TILES * CAP - 1,
                                      oob_is_err=False).then_inc(s["rt_sc"], 16)
            gp.wait_ge(s["rt_sc"], 16 * 2 * NT)
            gp.dma_start(tbl[:, :, :], tbl_d[:, :].rearrange("(t p) f -> p t f", p=P)).then_inc(s["rt_ld"], 16)
            gp.wait_ge(s["op_ps"], NT)
            ch.step(gp.memset(xg, 0.0))
            gp.wait_ge(s["rt_ld"], 16)
            gp.wait_ge(s_st[0], 16 * NT // 2)
            gp.wait_ge(s_st[1], 16 * NT // 2)

            def tview(e, c):
                if isinstance(e, int):
                    return tbl[:, e, c:c + 1]
                return tbl[:, ds(e, 1), c:c + 1].rearrange("p o f -> p (o f)")

            last_row, last_out = gp.to_reg(T - 1), gp.to_reg(2 * T - 1)

            def pause():
                ch.note(gp.tensor_tensor(junk[:, :], mhalf[:, 0:1], mhalf[:, 0:1], ALU.mult))

            def gather(e, par):
                row_ = e if isinstance(e, int) else gp.snap(e)
                if not isinstance(e, int) or e >= 2:
                    gp.wait_ge(s["m_tx"], e - 1)
                ch.step(gp.tensor_copy(idx[:, par:par + 1], tview(row_, 1)))
                pause()
                gp.indirect_dma_start(out=xg[:, par], out_offset=None, in_=xn2_d[:, :],
                                      in_offset=bass.IndirectOffsetOnAxis(ap=idx[:, par:par + 1], axis=0),
                                      bounds_check=last_row, oob_is_err=False).then_inc(s_gx[par], 16)

            def scatter(e, par):
                row_ = e if isinstance(e, int) else gp.snap(e)
                gp.wait_ge(s["m_ya"], e + 1)
                gp.wait_ge(s["m_yd"], e + 1)
                ch.step(gp.tensor_copy(idx[:, 2 + par:3 + par], tview(row_, 0)))
                pause()
                gp.indirect_dma_start(out=y_d[:, :], out_offset=bass.IndirectOffsetOnAxis(ap=idx[:, 2 + par:3 + par], axis=0),
                                      in_=yo[:, par], in_offset=None, bounds_check=last_out,
                                      oob_is_err=False).then_inc(s_sc[par], 16)

            gather(0, 0)
            gather(1, 1)
            gather(2, 0)
            with gp.Fori(0, 7) as g:
                ch.enter(g, 16)
                for u in range(4):
                    gather(g * 4 + (3 + u), (1 + u) % 2)
                    scatter(g * 4 + u, u % 2)
            ch.leave(7)
            gather(31, 1)
            for e in (28, 29, 30, 31):
                scatter(e, e % 2)
            for par in range(2):
                gp.wait_ge(s_sc[par], 16 * E // 2)

            n_ov = gp.value_load(idy[0:1, 0:1], min_val=1, max_val=OVT)
            gp.sem_inc(s["ov_go"], 1)
            with gp.Fori(0, n_ov) as i:
                ch.enter(i, 4)
                row_ = gp.snap(i + E)
                ch.step(gp.tensor_copy(idx[:, 0:1], tview(row_, 1)))
                pause()
                gp.indirect_dma_start(out=xg[:, 0], out_offset=None, in_=xn2_d[:, :],
                                      in_offset=bass.IndirectOffsetOnAxis(ap=idx[:, 0:1], axis=0),
                                      bounds_check=last_row, oob_is_err=False).then_inc(s["ov_g"], 16)
                ch.step(gp.tensor_copy(idx[:, 2:3], tview(row_, 0)))
                gp.wait_ge(s["m_ya"], i + (E + 1))
                gp.wait_ge(s["m_yd"], i + (E + 1))
                pause()
                gp.indirect_dma_start(out=y_d[:, :], out_offset=bass.IndirectOffsetOnAxis(ap=idx[:, 2:3], axis=0),
                                      in_=yo[:, 0], in_offset=None, bounds_check=last_out,
                                      oob_is_err=False).then_inc(s["ov_sc"], 16)
                gp.wait_ge(s["ov_sc"], i * 16 + 16)
                gp.sem_inc(s["ov_go"], 1)
            gp.sem_inc(s["f_go"], 1)
            for j in range(NT):
                power(rs[:, j % 2:j % 2 + 1], ss[:, j % 2:j % 2 + 1], 1, "ms_ready", "rstd_ready", 2 * NT + j + 1)

        @block.tensor
        def _(pe):
            def mm(o_, l, r, start=True, stop=True):
                return pe.matmul(o_, l, r, start=start, stop=stop, skip_group_check=True)

            pe.wait_ge(s["sel_ready"], 1)
            pe.wait_ge(s["ld_prm"], 16 * 13)
            pe.transpose(PS[7][:, 0:NR], prow[:, :], ident[0:NR, 0:NR]).then_inc(s["prm_t"], 1)

            def ada_block(par, col, count, done):
                pe.wait_ge(s_ada[par], count)
                for q in range(4):
                    for k in range(KD):
                        last = mm(PS[6][:, col + q:col + q + 1], ada[:, par, k, q * P:(q + 1) * P], cc[:, k:k + 1],
                                  k == 0, k == KD - 1)
                last.then_inc(s[done], 1)

            pe.wait_ge(s["silu_ready"], 1)
            for b in range(4):
                ada_block(b % 2, 4 * b, 16 * (b // 2 + 1), "mod1_ps")

            for j in range(NT):
                pe.wait_ge(s["xn_ready"], j + 1)
                if j >= 2:
                    pe.wait_ge(s["hT_act"], j - 1)
                    pe.wait_ge(s["hT_dve"], j - 1)
                for k in range(KD):
                    last = pe.transpose(PS[2 * (j % 2) + k // 4][:, (k % 4) * P:(k % 4 + 1) * P],
                                        xn[:, j % 2, k * P:(k + 1) * P], ident[:, :])
                last.then_inc(s["hT_tr"], 1)
            pe.wait_ge(s["hT_act"], NT)
            pe.wait_ge(s["hT_dve"], NT)
            pe.wait_ge(s["mod1_ready"], 1)

            def project(u, waits, done):
                pe.wait_ge(s_win[u], waits)
                if done is not None:
                    pe.wait_ge(s["proj_act"], done)
                    pe.wait_ge(s["proj_dve"], done)
                for k in range(KD):
                    for h in range(2):
                        last = mm(PS[2 * u + h][:, :], win[:, u, k, :], hT[:, k, h * 512:(h + 1) * 512], k == 0, k == KD - 1)
                last.then_inc(s["proj_ps"], 1)

            for r in range(2):
                for u in range(3):
                    project(u, 32 * (r + 1), None if r == 0 else u + 1)
                if r == 1:
                    ada_block(0, 0, 16 * 3, "mod2_ps")
                    ada_block(1, 4, 16 * 3, "mod2_ps")
            with pe.Fori(0, 2) as m:
                for r in range(2):
                    for u in range(3):
                        project(u, m * 64 + 32 * (3 + r), m * 6 + (3 * r + u + 4))
                    pe.wait_ge(s["mod2_ready"], m + 1)
                    ada_block(r, 4 * r, m * 16 + 16 * 4, "mod2_ps")
            project(0, 32 * 7, 16)
            pe.wait_ge(s["mod2_ready"], 3)
            ada_block(0, 0, 16 * 6, "mod2_ps")
            ada_block(1, 4, 16 * 6, "mod2_ps")

            for i in range(16):
                pe.wait_ge(s["gt_diag"], i + 1)
                if i % 4 == 0 and i >= 4:
                    pe.wait_ge(s["gt_ready"], i // 4)
                mm(PS[7][:, (i % 4) * P:(i % 4 + 1) * P], ones[:, :], dg[:, i % 2, :]).then_inc(s["gt_ps"], 1)

            def attend(nb, first):
                k0 = 1 if first else 0
                at = PAD if first else nb * P + (PAD - P)
                ks = slice(at, 2 * P + at - P * k0) if first else ds(at, 2 * P)
                pe.wait_ge(s["att_q"], nb + 1)
                for h in range(4):
                    last = mm(PS[h // 2][:, (h % 2) * 256 + k0 * P:(h % 2) * 256 + 256], qz[:, h, :], pT[:, B_KEY, ks])
                last.then_inc(s["att_qk"], 1)
                for kb in range(k0, 2):
                    last = pe.transpose(PS[2][:, kb * P:(kb + 1) * P], vs[:, kb * P:(kb + 1) * P], ident[:, :])
                last.then_inc(s["att_vps"], 1)
                pe.wait_ge(s["att_pn"], nb + 1)
                for h in range(4):
                    for kb in range(k0, 2):
                        last = pe.transpose(PS[3 + h // 2][:, ((h % 2) * 2 + kb) * P:((h % 2) * 2 + kb + 1) * P],
                                            sc[:, h, kb * P:(kb + 1) * P], ident[:, :])
                last.then_inc(s["att_tp"], 1)
                pe.wait_ge(s["att_v"], nb + 1)
                pe.wait_ge(s["att_tpa"], nb + 1)
                pe.wait_ge(s["att_tpd"], nb + 1)
                for h in range(4):
                    r = 64 * (h % 2)
                    for kb in range(k0, 2):
                        last = mm(PS[5][r:r + 64, (h // 2) * P:(h // 2 + 1) * P], vt[:, kb, (h // 2) * HD:(h // 2 + 1) * HD],
                                  ptT[:, h, kb, :], kb == k0, kb == 1)
                last.then_inc(s["att_o"], 1)

            attend(0, True)
            with pe.Fori(1, NT) as nb:
                attend(nb, False)

            pe.wait_ge(s["ld_misc"], 16 * 8)
            for c in range(2):
                pe.wait_ge(s["pool_d"], c + 1)
                for h in range(2):
                    last = mm(PS[6 + h][:, :], pw[:, c, :], pmd[:, c, h * 512:(h + 1) * 512])
                    if c == 0 and h == 0:
                        pass
                last.then_inc(s["pool_ps"], 1)
                if c == 0:
                    pe.wait_ge(s["pool_y"], 2)
            pe.wait_ge(s["pool_y"], 4)

            with pe.Fori(0, NT // 2) as m:
                def wait(name, per, k):
                    pe.wait_ge(s[name], m * per + k)

                def hb(h):
                    return slice(64 * (h % 2), 64 * (h % 2) + 64)

                wait("w_tanh", 1, 1)
                for p in range(2):
                    last = mm(PS[0][:, p * W2:(p + 1) * W2], lor[0:32, p * P:(p + 1) * P], lt[0:32, :])
                last.then_inc(s["w_lora"], 1)
                for p in range(2):
                    last = mm(PS[1][:, p * W2:(p + 1) * W2], lor[32:64, p * P:(p + 1) * P], z[32:64, B_LORA, :])
                last.then_inc(s["w_lora"], 1)
                wait("w_sg", 1, 1)
                for p in range(2):
                    last = mm(PS[2][:, p * W2:(p + 1) * W2], lor[64:128, p * P:(p + 1) * P], lt[64:128, :])
                last.then_inc(s["w_lora"], 1)

                def head_norms(bank, k):
                    wait("w_sq", 2, k)
                    for n in range(2):
                        for p in range(2):
                            c = n * 4 + p * 2
                            last = mm(PS[3][:, c:c + 2], sq[:, p, n * P:(n + 1) * P], bones[:, 0:P:64])
                    last.then_inc(s["w_ss"], 1)
                    wait("w_nrp", 2, k)
                    pe.transpose(PS[3][0:8, P:2 * P], nrp[:, :], ident[:, :]).then_inc(s["w_nrt"], 1)
                    wait("w_nrT", 2, k)
                    for p in range(2):
                        for n in range(2):
                            last = mm(PS[bank][:, p * W2 + n * P:p * W2 + (n + 1) * P], sel[:, n * 2 + p, :], nrT[:, :])
                    last.then_inc(s["w_nrb"], 1)

                head_norms(4, 1)
                wait("w_ops", 1, 1)
                wait("w_gg", 1, 1)
                for n in range(2):
                    tk = slice(n * P, (n + 1) * P)
                    for i, src in enumerate((Bt, Kt)):
                        for p in range(2):
                            pe.transpose(PS[4 * n][:, (2 * i + p) * P:(2 * i + p + 1) * P], src[:, p, tk], ident[:, :])
                    for p in range(2):
                        pe.transpose(PS[4 * n + 1][:, p * P:(p + 1) * P], z[:, B_V + p, tk], ident[:, :])
                        last = pe.transpose(PS[4 * n + 1][:, (2 + p) * P:(3 + p) * P], KR[:, p, 0, tk], ident[:, :])
                    last.then_inc(s["w_tok"], 1)
                    for h in range(4):
                        last = mm(PS[4 * n + 2 + h % 2][:, (h // 2) * 256:(h // 2) * 256 + 256].rearrange("p (a t) -> p a t", a=2),
                                  Bt[hb(h), h // 2, tk], KR[hb(h), h // 2, :, tk])
                    last.then_inc(s["w_abp"], 1)
                for n in range(2):
                    tk = slice(n * P, (n + 1) * P)
                    wait("w_tka", 2, n + 1)
                    wait("w_tkd", 2, n + 1)
                    for h in range(4):
                        last = mm(PS[4 * n + h % 2][:, (h // 2) * 256:(h // 2) * 256 + 256].rearrange("p (a t) -> p a t", a=2),
                                  Kt[hb(h), h // 2, tk], KR[hb(h), h // 2, :, tk])
                    last.then_inc(s["w_akp"], 1)

                def four(n, bank, l, r, sem_name):
                    for h in range(4):
                        last = mm(PS[4 * n + bank][:, h * P:(h + 1) * P], l[:, h, :], r[:, h, :])
                    last.then_inc(s[sem_name], 1)

                def flip(n, bank):
                    for h in range(4):
                        last = pe.transpose(PS[4 * n + bank][:, h * P:(h + 1) * P], rw[n]["xt"][:, h, :], ident[:, :])
                    last.then_inc(s["w_xp"], 1)

                for n in range(2):
                    wait("w_xt", 12, n + 1)
                    flip(n, 2)
                for n in range(2):
                    wait("w_ak", 2, n + 1)
                    for h in range(4):
                        last = mm(PS[4 * n][:, h * HD:(h + 1) * HD], rw[n]["ak"][:, h, 0, :], rw[n]["vt"][:, h, :])
                    last.then_inc(s["w_w1p"], 1)
                for l in range(1, 6):
                    for n in range(2):
                        wait("w_xa", 10, 2 * (l - 1) + n + 1)
                        wait("w_bl", 12, 2 * l + n + 1)
                        four(n, 3, rw[n]["bl"], rw[n]["x"], "w_t1p")
                    for n in range(2):
                        wait("w_t1", 10, 2 * (l - 1) + n + 1)
                        four(n, 2, rw[n]["t1"], rw[n]["xt"], "w_x2p")
                    if l < 5:
                        for n in range(2):
                            wait("w_xt", 12, 2 * l + n + 1)
                            flip(n, 3)
                for n in range(2):
                    wait("w_xt", 12, 10 + n + 1)
                    wait("w_w1", 2, n + 1)
                    for h in range(4):
                        last = mm(PS[4 * n + 1][:, h * P:(h + 1) * P], rw[n]["xt"][:, h, :],
                                  rw[n]["wk"][:, h].rearrange("p a d -> p (a d)"))
                    last.then_inc(s["w_uzp"], 1)
                for n in range(2):
                    wait("w_uz", 2, n + 1)
                    uz, bt = rw[n]["uz"], rw[n]["bt"]
                    for h in range(4):
                        last = mm(PS[4 * n + 3][hb(h), (h // 2) * P:(h // 2 + 1) * P], uz[:, 1, h, :], rw[n]["ab"][:, h, 1, :])
                    last.then_inc(s["w_rep"], 1)
                    for c in range(2):
                        rr = slice(64 * c, 64 * c + 64)
                        for h in range(4):
                            last = mm(PS[4 * n + 2 - c][hb(h), (h // 2) * HD:(h // 2 + 1) * HD], uz[rr, 1, h, :], bt[rr, h, :])
                    last.then_inc(s["w_gp"], 1)
                for n in range(2):
                    t = rw[n]
                    for c in range(2):
                        rr = slice(64 * c, 64 * c + 64)
                        for p in range(2):
                            o_ = PS[4 * n + 3 * c][:, p * HD:(p + 1) * HD]
                            for h in (2 * p, 2 * p + 1):
                                mm(o_[hb(h), :], t["bt"][rr, h, :], t["uz"][rr, 0, h, :], True, False)
                                mm(o_[hb(h), :], t["kt"][rr, h, :], t["vt"][rr, h, :], False, False)
                            if p == 0:
                                if c == 0:
                                    wait("w_G", 2, n + 1)
                                wait("w_S", 5, 2 * n + c + 1)
                            last = mm(o_, G[:, 4 * n + c * 2 + p, :], S[:, 2 * n + c, p, :], False, True)
                        last.then_inc(s["w_hp"], 1)
                for n in range(2):
                    wait("w_re", 2, n + 1)
                    t = rw[n]
                    for h in range(4):
                        p = h // 2
                        o_ = PS[4 * n + 1][hb(h), p * P:(p + 1) * P]
                        mm(o_, t["uz"][:, 0, h, :], t["ab"][:, h, 1, :], True, False)
                        mm(o_, t["vt"][:, h, :], t["ak"][:, h, 1, :], False, False)
                        for c in range(2):
                            cs = slice(64 * c, 64 * c + 64)
                            last = mm(o_[:, cs], S[hb(h), 2 * n + c, p, :], t["re"][hb(h), p, cs], False, c == 1)
                    last.then_inc(s["w_yp"], 1)
                wait("w_y", 2, 2)
                mm(PS[2][:, :], bones[:, :], yb.rearrange("p a t -> p (a t)")).then_inc(s["w_mean"], 1)
                for p in range(2):
                    last = mm(PS[5][:, p * W2:(p + 1) * W2], brk[:, p, :], rk[:, p, :])
                last.then_inc(s["w_bonp"], 1)
                head_norms(4, 2)

            pe.wait_ge(s["w_yT"], 5)
            pe.wait_ge(s["wo_ld"], 16)
            pe.wait_ge(s["ld_wr"], 16 * 4)

            def out_main(j):
                if j >= 2:
                    pe.wait_ge(s["op_x1"], j - 1)
                for k in range(KD):
                    for h in range(2):
                        last = mm(PS[2 * (j % 2) + h][:, :], yT[:, k, j * P:(j + 1) * P], wo[:, k, h * 512:(h + 1) * 512],
                                  k == 0, k == KD - 1)
                last.then_inc(s["op_ps"], 1)

            out_main(0)
            for j in range(NT):
                if j + 1 < NT:
                    out_main(j + 1)
                pe.wait_ge(s["op_xn"], j + 1)
                if j >= 1:
                    pe.wait_ge(s["op_ta"], j)
                    pe.wait_ge(s["op_td"], j)
                for k in range(KD):
                    last = pe.transpose(PS[4 + k // 4][:, (k % 4) * P:(k % 4 + 1) * P], xn2[:, j % 2, k * P:(k + 1) * P],
                                        ident[:, :])
                last.then_inc(s["op_tp"], 1)
                pe.wait_ge(s["op_ta"], j + 1)
                pe.wait_ge(s["op_td"], j + 1)
                if j >= 1:
                    pe.wait_ge(s["op_lgd"], j)
                for k in range(KD):
                    last = mm(PS[6][:, 0:GROUPS + E], h2T[:, k, :], wr[:, k, :], k == 0, k == KD - 1)
                last.then_inc(s["op_lg"], 1)

            pe.wait_ge(s["rt_oh"], 1)
            flat = rt["tmp"].rearrange("p a b -> p (a b)")
            mm(PS[7][:, 0:NT * E], tri[:, :], flat)
            mm(PS[7][:, 256:256 + NT * E], ones[:, :], flat).then_inc(s["rt_pos"], 1)

            def ex_t(e, par, pre="m_", gsem=None, gcount=None, wait_free=True):
                pe.wait_ge(gsem, gcount)
                if wait_free:
                    pe.wait_ge(s[pre + "xa"], e)
                    pe.wait_ge(s[pre + "xd"], e)
                for k in range(KD):
                    last = pe.transpose(PS[k // 4][:, (k % 4) * P:(k % 4 + 1) * P], xg[:, par, k * P:(k + 1) * P], ident[:, :])
                last.then_inc(s[pre + "tx"], 1)

            def ex_gu(e, par, u, pre="m_", wsem=None, wcount=None, wait_free=True):
                pe.wait_ge(s[pre + "xa"], e + 1)
                pe.wait_ge(s[pre + "xd"], e + 1)
                pe.wait_ge(wsem, wcount)
                if wait_free:
                    pe.wait_ge(s[pre + "act"], e - 1)
                for i, wt in enumerate((wg, wu)):
                    for k in range(KD):
                        last = mm(PS[2 + par][:, i * P:(i + 1) * P], wt[:, u, k, :], xt[:, par, k, :], k == 0, k == KD - 1)
                last.then_inc(s[pre + "gu"], 1)

            def ex_dn(e, par, u, pre="m_", wait_free=True):
                pe.wait_ge(s[pre + "act"], e + 1)
                if wait_free:
                    pe.wait_ge(s[pre + "ya"], e - 1)
                    pe.wait_ge(s[pre + "yd"], e - 1)
                for h in range(2):
                    last = mm(PS[4 + 2 * par + h][:, :], ac[:, par, :], wd[:, u, h * 512:(h + 1) * 512])
                last.then_inc(s[pre + "dn"], 1)

            ex_t(0, 0, gsem=s_gx[0], gcount=16, wait_free=False)
            ex_t(1, 1, gsem=s_gx[1], gcount=16)
            ex_gu(0, 0, 0, wsem=s_w[0], wcount=48, wait_free=False)

            def turn(e, u1, gcount_, wcount_, first):
                ex_t(e + 1, (u1 + 1) % 2, gsem=s_gx[(u1 + 1) % 2], gcount=gcount_)
                ex_gu(e, u1 % 2, u1 % 4, wsem=s_w[u1 % 4], wcount=wcount_, wait_free=not first)
                ex_dn(e - 1, (u1 - 1) % 2, (u1 - 1) % 4, wait_free=not first)

            turn(1, 1, 32, 48, True)
            ex_t(3, 1, gsem=s_gx[1], gcount=32)
            ex_gu(2, 0, 2, wsem=s_w[2], wcount=48)
            ex_dn(1, 1, 1, wait_free=False)
            with pe.Fori(0, 7) as g:
                for u in range(4):
                    turn(g * 4 + (3 + u), 3 + u, g * 32 + 16 * ((4 + u) // 2 + 1), g * 48 + 48 * ((3 + u) // 4 + 1), False)
            ex_gu(31, 1, 3, wsem=s_w[3], wcount=48 * 8)
            ex_dn(30, 0, 2)
            ex_dn(31, 1, 3)

            n_ov = pe.value_load(idy[0:1, 0:1], min_val=1, max_val=OVT)
            pe.wait_ge(s["m_ya"], E)
            pe.wait_ge(s["m_yd"], E)
            with pe.Fori(0, n_ov) as i:
                ex_t(i + E, 0, "m_", s["ov_g"], i * 16 + 16, False)
                ex_gu(i + E, 0, 0, "m_", s["ov_w"], i * 48 + 48, False)
                ex_dn(i + E, 0, 0, "m_", False)

        @block.scalar
        def _(act):
            def fn(o_, i_, f=ACT.Copy, **kw):
                return act.activation(o_, i_, f, **kw)

            act.wait_ge(s["ld_c"], 16)
            fn(ct[:, :], cc[:, :], ACT.Tanh, scale=0.5).then_inc(s["silu_t"], 1)
            act.wait_ge(s["sel_ready"], 1)

            def square(j):
                act.wait_ge(s_x[j % 2], 16 * (j // 2 + 1))
                fn(xn[:, j % 2], xin[:, j % 2], ACT.Square, accum_out=ss[:, j % 2:j % 2 + 1]).then_inc(s["ss_ready"], 1)

            square(0)
            square(1)
            act.wait_ge(s["mod1_ready"], 1)
            for j in range(NT):
                act.wait_ge(s["hT_tr"], j + 1)
                for k in range(4):
                    last = fn(hT[:, k, j * P:(j + 1) * P], PS[2 * (j % 2)][:, k * P:(k + 1) * P], ACT.Identity,
                              scale=s1[:, k:k + 1], bias=mod[:, M_SH1 + k:M_SH1 + k + 1])
                last.then_inc(s["hT_act"], 1)
                if j + 2 < NT:
                    square(j + 2)

            def projected(b, u):
                act.wait_ge(s["proj_ps"], b + 1)
                dst = pT[:, b, PAD:PAD + 512] if isinstance(b, int) else \
                    pT[:, ds(b, 1), PAD:PAD + 512].rearrange("p o t -> p (o t)")
                fn(dst, PS[2 * u][:, :]).then_inc(s["proj_act"], 1)

            with act.Fori(0, 6) as m:
                for u in range(3):
                    projected(m * 3 + u, u)
            projected(18, 0)

            for q in range(4):
                act.wait_ge(s["gt_ps"], 4 * (q + 1))
                fn(gtb[:, q // 2, (q % 2) * 512:(q % 2 + 1) * 512], PS[7][:, :]).then_inc(s["gt_ready"], 1)

            act.wait_ge(s["proj_dve"], NB)
            act.wait_ge(s["proj_act"], NB)
            act.wait_ge(s["att_zero"], 1)

            def attend(nb, first):
                k0 = 1 if first else 0
                tok = slice(PAD, PAD + P) if first else ds(nb * P + PAD, P)
                at = slice(PAD, PAD + P) if first else ds(nb * P + (PAD - P), 2 * P)
                for kv in range(2):
                    r = slice(64 * kv, 64 * kv + 64)
                    fn(qz[r, 2 * kv:2 * kv + 2, :], pT[r, B_Q:B_Q + 2, tok], scale=float(HD) ** -0.5)
                fn(vs[:, k0 * P:], pT[:, B_VAL, at]).then_inc(s["att_q"], 1)
                act.wait_ge(s["att_vps"], nb + 1)
                fn(vt[:, k0:, :], PS[2][:, k0 * P:256].rearrange("p (a b) -> p a b", b=P)).then_inc(s["att_v"], 1)
                act.wait_ge(s["att_nm"], nb + 1)
                for h in range(4):
                    fn(sc[:, h, k0 * P:], sc[:, h, k0 * P:], ACT.Exp, bias=nm[:, h:h + 1], accum_out=sm[:, h:h + 1])
                fn(es[:, :], es[:, :], ACT.Exp).then_inc(s["att_p"], 1)
                act.wait_ge(s["att_tp"], nb + 1)
                fn(ptT[:, 0:2, k0:, :], PS[3][:, :].rearrange("p (h a b) -> p h a b", h=2, b=P)[:, :, k0:, :])\
                    .then_inc(s["att_tpa"], 1)

            attend(0, True)
            with act.Fori(1, NT) as nb:
                attend(nb, False)

            for i in range(4):
                c, h = i // 2, i % 2
                act.wait_ge(s["pool_ps"], c + 1)
                fn(yT[:, c, h * 512:(h + 1) * 512], PS[6 + h][:, :], scale=pc[:, R_PS + c:R_PS + c + 1]).then_inc(s["pool_y"], 1)

            with act.Fori(0, NT // 2) as m:
                def wait(name, per, k):
                    act.wait_ge(s[name], m * per + k)

                wait("w_yT", 1, 1)
                fn(S[:, 0], S[:, 4]).then_inc(s["w_S"], 1)
                wait("w_z", 1, 1)
                fn(lt[0:32, :], z[0:32, B_LORA, :], ACT.Tanh)
                fn(lt[64:128, :], z[64:128, B_LORA, :], ACT.Tanh, scale=0.5).then_inc(s["w_tanh"], 1)
                wait("w_kkr", 1, 1)
                fn(sq, kkr, ACT.Square).then_inc(s["w_sq"], 1)
                wait("w_lora", 3, 1)
                for p in range(2):
                    last = fn(lw[:, p], PS[0][:, p * W2:(p + 1) * W2], ACT.Tanh, scale=0.5, bias=hp[:, p:p + 1])
                last.then_inc(s["w_th"], 1)
                wait("w_lora", 3, 2)
                for p in range(2):
                    last = fn(aa[:, p], PS[1][:, p * W2:(p + 1) * W2], ACT.Tanh, scale=0.5, bias=hp[:, 2 + p:3 + p])
                last.then_inc(s["w_tha"], 1)
                wait("w_lora", 3, 3)
                fn(gg.rearrange("p a t -> p (a t)"), PS[2][:, :]).then_inc(s["w_gg"], 1)
                wait("w_L", 1, 1)
                fn(Pc, Lc, ACT.Exp)
                fn(Pm, Lm, ACT.Exp)
                fn(iP, Lc, ACT.Exp, scale=-1.0).then_inc(s["w_exp"], 1)
                for n in range(2):
                    wait("w_tok", 2, n + 1)
                    fn(both(n), PS[4 * n][:, :]).then_inc(s["w_tka"], 1)
                for n in range(2):
                    wait("w_xp", 10, n + 1)
                    fn(rw[n]["x"], PS[4 * n + 2][:, :].rearrange("p (h t) -> p h t", h=4)).then_inc(s["w_xa"], 1)
                for n in range(2):
                    wait("w_w1p", 2, n + 1)
                    fn(rw[n]["wk"][:, :, 0, :], PS[4 * n][:, 0:256].rearrange("p (h d) -> p h d", h=4)).then_inc(s["w_w1"], 1)
                for l in range(1, 6):
                    for n in range(2):
                        wait("w_t1p", 10, 2 * (l - 1) + n + 1)
                        fn(rw[n]["t1"], PS[4 * n + 3][:, :].rearrange("p (h t) -> p h t", h=4)).then_inc(s["w_t1"], 1)
                    if l < 5:
                        for n in range(2):
                            wait("w_xp", 10, 2 * l + n + 1)
                            fn(rw[n]["x"], PS[4 * n + 3][:, :].rearrange("p (h t) -> p h t", h=4)).then_inc(s["w_xa"], 1)
                for n in range(2):
                    wait("w_uzp", 2, n + 1)
                    fn(rw[n]["uz"].rearrange("p a h d -> p h a d"),
                       PS[4 * n + 1][:, :].rearrange("p (h a d) -> p h a d", h=4, a=2), scale=-1.0).then_inc(s["w_uz"], 1)
                for n in range(2):
                    for c in range(2):
                        wait("w_hp", 4, 2 * n + c + 1)
                        end = n * P + c * CH + CH - 1
                        for p in range(2):
                            last = fn(S[:, 2 * n + c + 1, p, :], PS[4 * n + 3 * c][:, p * HD:(p + 1) * HD],
                                      scale=Pc[:, p, end:end + 1])
                        last.then_inc(s["w_S"], 1)
                wait("w_yc", 1, 1)
                fn(sq, yb, ACT.Square).then_inc(s["w_sq"], 1)

            def modulated(dst, j, count, tr, done, bank=4):
                act.wait_ge(s[tr], count)
                for k in range(4):
                    last = fn(dst[:, k, :], PS[bank][:, k * P:(k + 1) * P], ACT.Identity, scale=s2[:, k:k + 1],
                              bias=mod[:, M_SH2 + k:M_SH2 + k + 1])
                last.then_inc(s[done], 1)

            for j in range(NT):
                act.wait_ge(s["op_x1"], j + 1)
                fn(xn2[:, j % 2], x1[:, j], ACT.Square, accum_out=ss[:, j % 2:j % 2 + 1]).then_inc(s["ss_ready"], 1)
                modulated(h2T, j, j + 1, "op_tp", "op_ta")

            act.wait_ge(s["rt_e1"], 1)
            fn(rt["gb"], rt["ga"], ACT.Exp).then_inc(s["rt_e2"], 1)
            act.wait_ge(s["rt_e1"], 2)
            fn(small["e2"], small["e2"], ACT.Exp).then_inc(s["rt_e2"], 1)

            act.wait_ge(s["rt_n"], 1)
            act.wait_ge(s["rt_ld"], 16)

            def gate(e):
                if isinstance(e, int):
                    return tbl[:, e, 2:3].bitcast(F32)
                return tbl[:, ds(e, 1), 2:3].rearrange("p o f -> p (o f)").bitcast(F32)

            def hidden(e, par, pre="m_", free=True):
                act.wait_ge(s[pre + "gu"], e + 1)
                if free:
                    act.wait_ge(s[pre + "act"], e - 1)
                fn(th[:, par, :], PS[2 + par][:, 0:P], ACT.Tanh, scale=0.5).then_inc(s[pre + "th"], 1)

            def result(e, par, pre="m_", free=None):
                act.wait_ge(s[pre + "dn"], e + 1)
                if free is not None:
                    act.wait_ge(s_sc[par], free)
                fn(yo[:, par, 0:512], PS[4 + 2 * par][:, :], scale=gate(e)).then_inc(s[pre + "ya"], 1)

            act.wait_ge(s["op_ps"], NT)
            modulated(xt[:, 0], 0, 1, "m_tx", "m_xa", 0)
            modulated(xt[:, 1], 1, 2, "m_tx", "m_xa", 0)
            hidden(0, 0, free=False)
            modulated(xt[:, 0], 2, 3, "m_tx", "m_xa", 0)
            hidden(1, 1, free=False)
            result(0, 0)
            modulated(xt[:, 1], 3, 4, "m_tx", "m_xa", 0)
            hidden(2, 0)
            result(1, 1)
            with act.Fori(0, 7) as g:
                for u in range(4):
                    modulated(xt[:, (4 + u) % 2], 0, g * 4 + (5 + u), "m_tx", "m_xa", 0)
                    hidden(g * 4 + (3 + u), (3 + u) % 2)
                    result(g * 4 + (2 + u), u % 2, free=g * 32 + 16 * ((2 + u) // 2))
            hidden(31, 1)
            result(30, 0, free=16 * 15)
            result(31, 1, free=16 * 15)
            n_ov = act.value_load(idy[0:1, 0:1], min_val=1, max_val=OVT)
            with act.Fori(0, n_ov) as i:
                modulated(xt[:, 0], 0, i + (E + 1), "m_tx", "m_xa", 0)
                hidden(i + E, 0, free=False)
                result(i + E, 0)

            for j in range(NT):
                act.wait_ge(s["f_x2"], j + 1)
                if j >= 2:
                    act.wait_ge(s_fo[j % 2], 16 * (j // 2))
                fn(fo[:, j % 2], x1[:, j], ACT.Square, accum_out=ss[:, j % 2:j % 2 + 1]).then_inc(s["ss_ready"], 1)

        @block.vector
        def _(dve):
            ch = Chain(dve, s["chain_dve"])
            tt, ts, stt = dve.tensor_tensor, dve.tensor_scalar, dve.scalar_tensor_tensor

            def flat3(ap):
                return ap.rearrange("p a t -> p (a t)")

            dve.wait_ge(s["ld_c"], 16)
            dve.wait_ge(s["silu_t"], 1)
            ch.step(ts(ct[:, :], ct[:, :], 0.5, 0.5, ALU.mult, ALU.add))
            tt(cc[:, :], cc[:, :], ct[:, :], ALU.mult).then_inc(s["silu_ready"], 1)
            dve.wait_ge(s["sel_ready"], 1)
            dve.reciprocal(rc16[:, :, :], rc16[:, :, :]).then_inc(s["rt_c"], 1)
            dve.wait_ge(s["prm_t"], 1)
            dve.tensor_copy(pc[:, :], PS[7][:, 0:NR]).then_inc(s["prm_ready"], 1)
            dve.wait_ge(s["prm_ready"], 1)
            ch.note(ts(hp[:, 0:4], pc[:, R_W0:R_W0 + 4], 0.5, None, ALU.mult))
            ch.note(ts(hp[:, 4:6], pc[:, R_KA:R_KA + 2], 0.5, None, ALU.mult))
            ch.note(ts(hp[:, 6:8], pc[:, R_KA:R_KA + 2], -0.5, 1.0, ALU.mult, ALU.add))
            for p in range(2):
                ch.note(ts(brk[:, p, :], bones[:, :], pc[:, R_RK + p:R_RK + p + 1], None, ALU.mult))

            def mean_square(j, phase):
                dve.wait_ge(s["ss_ready"], phase * NT + j + 1)
                ts(ss[:, j % 2:j % 2 + 1], ss[:, j % 2:j % 2 + 1], 1.0 / D, EPS, ALU.mult, ALU.add).then_inc(s["ms_ready"], 1)

            def normed(j):
                mean_square(j, 0)
                dve.wait_ge(s["rstd_ready"], j + 1)
                dve.wait_ge(s_x[j % 2], 16 * (j // 2 + 1))
                ts(xn[:, j % 2], xin[:, j % 2], rs[:, j % 2:j % 2 + 1], None, ALU.mult).then_inc(s["xn_ready"], 1)

            normed(0)
            normed(1)
            dve.wait_ge(s["mod1_ps"], 4)
            ch.step(tt(mod[:, 0:16], PS[6][:, 0:16], pc[:, 0:16], ALU.add))
            stt(s1[:, :], mod[:, M_SC1:M_SC1 + 8], 1.0, pc[:, R_G1:R_G1 + 8], ALU.add, ALU.mult).then_inc(s["mod1_ready"], 1)
            dve.wait_ge(s["mod1_ready"], 1)
            for j in range(NT):
                dve.wait_ge(s["hT_tr"], j + 1)
                for k in range(4, KD):
                    last = ts(hT[:, k, j * P:(j + 1) * P], PS[2 * (j % 2) + 1][:, (k - 4) * P:(k - 3) * P],
                              s1[:, k:k + 1], mod[:, M_SH1 + k:M_SH1 + k + 1], ALU.mult, ALU.add)
                last.then_inc(s["hT_dve"], 1)
                if j + 2 < NT:
                    normed(j + 2)

            def projected(b, u):
                dve.wait_ge(s["proj_ps"], b + 1)
                dst = pT[:, b, PAD + 512:PAD + 1024] if isinstance(b, int) else \
                    pT[:, ds(b, 1), PAD + 512:PAD + 1024].rearrange("p o t -> p (o t)")
                dve.tensor_copy(dst, PS[2 * u + 1][:, :]).then_inc(s["proj_dve"], 1)

            def modded(c, count):
                dve.wait_ge(s["mod2_ps"], count)
                cols = slice(16 + 8 * c, 24 + 8 * c) if isinstance(c, int) else ds(c * 8 + 16, 8)
                tt(mod[:, cols], PS[6][:, 0:8], pc[:, cols], ALU.add).then_inc(s["mod2_ready"], 1)

            for b in range(6):
                projected(b, b % 3)
            modded(0, 2)
            with dve.Fori(0, 2) as m:
                for u in range(6):
                    projected(m * 6 + (6 + u), u % 3)
                modded(m + 1, m * 2 + 4)
            projected(18, 0)
            modded(3, 8)
            dve.wait_ge(s["mod2_ready"], 4)
            ch.step(stt(s2[:, :], mod[:, M_SC2:M_SC2 + 8], 1.0, pc[:, R_G2:R_G2 + 8], ALU.add, ALU.mult))
            for i in range(16):
                if i >= 2:
                    dve.wait_ge(s["gt_ps"], i - 1)
                col = (M_GT1 if i < 8 else M_GT2) + i % 8
                ts(dg[:, i % 2, :], ident[:, :], mod[:, col:col + 1], None, ALU.mult).then_inc(s["gt_diag"], 1)

            dve.wait_ge(s["proj_act"], NB)
            dve.memset(qz, 0.0).then_inc(s["att_zero"], 1)
            dve.wait_ge(s["ld_misc"], 16 * 8)

            def attend(nb, first):
                k0 = 1 if first else 0
                dve.wait_ge(s["att_qk"], nb + 1)
                for h in range(4):
                    slope = 2.0 ** (-8.0 * (h + 1) / 4)
                    ch.note(stt(sc[:, h, k0 * P:], adist[:, k0 * P:], slope, PS[h // 2][:, (h % 2) * 256 + k0 * P:(h % 2 + 1) * 256],
                                ALU.mult, ALU.add))
                ch.wait()
                ch.step(dve.tensor_reduce(mx[:, :], sc[:, :, k0 * P:], AX.X, ALU.max))
                ch.step(tt(mx[:, :], mx[:, :], sink[:, :], ALU.max))
                ch.note(tt(es[:, :], sink[:, :], mx[:, :], ALU.subtract))
                ts(nm[:, :], mx[:, :], -1.0, None, ALU.mult).then_inc(s["att_nm"], 1)
                dve.wait_ge(s["att_p"], nb + 1)
                ch.step(tt(rd[:, :], sm[:, :], es[:, :], ALU.add))
                ch.step(dve.reciprocal(rd[:, :], rd[:, :]))
                for h in range(4):
                    last = ts(sc[:, h, k0 * P:], sc[:, h, k0 * P:], rd[:, h:h + 1], None, ALU.mult)
                last.then_inc(s["att_pn"], 1)
                dve.wait_ge(s["att_tp"], nb + 1)
                dve.tensor_copy(ptT[:, 2:4, k0:, :], PS[4][:, :].rearrange("p (h a b) -> p h a b", h=2, b=P)[:, :, k0:, :])\
                    .then_inc(s["att_tpd"], 1)
                dve.wait_ge(s["att_o"], nb + 1)
                tok = slice(0, P) if first else ds(nb * P, P)
                dve.tensor_copy(yT[:, 2:4, tok], PS[5][:, 0:2 * P].rearrange("p (a t) -> p a t", a=2)).then_inc(s["att_y"], 1)

            attend(0, True)
            with dve.Fori(1, NT) as nb:
                ch.enter(nb - 1, 9)
                attend(nb, False)
            ch.leave(NT - 1)

            dve.wait_ge(s["pool_y"], 4)
            dve.wait_ge(s["conv_y"], 2)
            dve.wait_ge(s["att_y"], NT)
            dve.wait_ge(s["pad_ready"], 1)
            dve.memset(ct[:, :], 0.0).then_inc(s["w_yT"], 1)
            with dve.Fori(0, NT // 2) as m:
                ch.enter(m, 18)

                def wait(name, per, k):
                    dve.wait_ge(s[name], m * per + k)

                wait("w_yT", 1, 1)
                wait("w_df", 1, 1)
                for b in range(ZB):
                    last = stt(z[:, b, :], df[:, b, :], pc[:, R_MU + b:R_MU + b + 1],
                               pT[:, b, ds(m * W2 + PAD, W2)], ALU.mult, ALU.add)
                last.then_inc(s["w_z"], 1)
                wait("w_z", 1, 1)
                for p in range(2):
                    last = ts(kkr[:, p], z[:, B_K + p, :], pc[:, R_KK + p:R_KK + p + 1], None, ALU.mult)
                last.then_inc(s["w_kkr"], 1)
                wait("w_tanh", 1, 1)
                ts(lt[64:128, :], lt[64:128, :], 0.5, 0.5, ALU.mult, ALU.add).then_inc(s["w_sg"], 1)
                wait("w_ss", 2, 1)
                ts(nrm[:, :], PS[3][:, 0:8], 1e-24, None, ALU.max).then_inc(s["w_nrm"], 1)
                wait("w_th", 1, 1)
                c = -0.5 * float(np.exp(-0.5))
                ch.step(ts(lw, lw, 1.0, c, ALU.add, ALU.mult))
                ch.step(dve.tensor_tensor_scan(flat3(Lc), rmask[:, :], flat3(lw), 0.0, ALU.mult, ALU.add))
                tt(Lm, Lc, lw, ALU.subtract).then_inc(s["w_L"], 1)
                wait("w_nrt", 2, 1)
                dve.tensor_copy(nrT[:, :], PS[3][0:8, P:2 * P]).then_inc(s["w_nrT"], 1)
                wait("w_tha", 1, 1)
                for p in range(2):
                    ch.note(ts(rk[:, p], aa[:, p], hp[:, 4 + p:5 + p], hp[:, 6 + p:7 + p], ALU.mult, ALU.add))
                ch.wait()
                ch.note(tt(z[:, B_K:B_K + 2, :], z[:, B_K:B_K + 2, :], rk, ALU.mult))
                ch.step(ts(aa, aa, 0.5, 0.5, ALU.mult, ALU.add))
                wait("w_nrb", 2, 1)
                ch.step(tt(flat3(kkr), flat3(kkr), PS[4][:, :], ALU.mult))
                wait("w_exp", 1, 1)
                ch.note(tt(KR[:, :, 0, :], kkr, Pm, ALU.mult))
                ch.note(tt(KR[:, :, 1, :], z[:, B_R:B_R + 2, :], Pc, ALU.mult))
                ch.note(tt(Kt, z[:, B_K:B_K + 2, :], iP, ALU.mult))
                ch.note(tt(rk, z[:, B_R:B_R + 2, :], z[:, B_K:B_K + 2, :], ALU.mult))
                ch.step(tt(aa, kkr, aa, ALU.mult))
                tt(Bt, aa, iP, ALU.mult).then_inc(s["w_ops"], 1)
                for n in range(2):
                    t = rw[n]
                    wait("w_tok", 2, n + 1)
                    ch.note(dve.tensor_copy(t["vt"], PS[4 * n + 1][:, 0:256].rearrange("p (h d) -> p h d", h=4)))
                    dve.tensor_copy(t["wk"][:, :, 1, :], PS[4 * n + 1][:, 256:512].rearrange("p (h d) -> p h d", h=4))\
                        .then_inc(s["w_tkd"], 1)
                    wait("w_abp", 2, n + 1)
                    for q in range(2):
                        last = tt(t["ab"][:, q::2].rearrange("p h a t -> p h (a t)"),
                                  PS[4 * n + 2 + q][:, :].rearrange("p (h x) -> p h x", h=2),
                                  mskb(), ALU.mult)
                    last.then_inc(s["w_ab"], 1)
                for n in range(2):
                    wait("w_bl", 12, n + 1)
                    tt(rw[n]["xt"], ident[:, :].unsqueeze(1).to_broadcast([P, 4, P]), rw[n]["bl"], ALU.subtract)\
                        .then_inc(s["w_xt"], 1)
                for n in range(2):
                    wait("w_akp", 2, n + 1)
                    for q in range(2):
                        last = tt(rw[n]["ak"][:, q::2].rearrange("p h a t -> p h (a t)"),
                                  PS[4 * n + q][:, :].rearrange("p (h x) -> p h x", h=2), mskb(), ALU.mult)
                    last.then_inc(s["w_ak"], 1)
                for l in range(1, 6):
                    for n in range(2):
                        wait("w_x2p", 10, 2 * (l - 1) + n + 1)
                        tt(rw[n]["xt"], rw[n]["xt"], PS[4 * n + 2][:, :].rearrange("p (h t) -> p h t", h=4), ALU.subtract)\
                            .then_inc(s["w_xt"], 1)
                for n in range(2):
                    wait("w_rep", 2, n + 1)
                    tt(rw[n]["re"], PS[4 * n + 3][:, 0:256].rearrange("p (a t) -> p a t", a=2),
                       KR[:, :, 1, n * P:(n + 1) * P], ALU.add).then_inc(s["w_re"], 1)
                    wait("w_gp", 2, n + 1)
                    for c in range(2):
                        for h in range(2):
                            r = slice(64 * h, 64 * h + 64)
                            last = tt(G[r, 4 * n + 2 * c:4 * n + 2 * c + 2, r],
                                      PS[4 * n + 2 - c][r, 0:128].rearrange("p (q d) -> p q d", q=2),
                                      ident[r, r].unsqueeze(1).to_broadcast([64, 2, 64]), ALU.add)
                    last.then_inc(s["w_G"], 1)
                for n in range(2):
                    wait("w_yp", 2, n + 1)
                    dve.tensor_copy(yb[:, :, n * P:(n + 1) * P], PS[4 * n + 1][:, 0:256].rearrange("p (a t) -> p a t", a=2))\
                        .then_inc(s["w_y"], 1)
                wait("w_mean", 1, 1)
                stt(flat3(yb), PS[2][:, :], -1.0 / HD, flat3(yb), ALU.mult, ALU.add).then_inc(s["w_yc"], 1)
                wait("w_bonp", 1, 1)
                ch.note(tt(flat3(Lm), PS[5][:, :], flat3(z[:, B_V:B_V + 2, :]), ALU.mult))
                wait("w_ss", 2, 2)
                ts(nrm[:, :], PS[3][:, 0:8], 1.0 / HD, GN_EPS, ALU.mult, ALU.add).then_inc(s["w_nrm"], 1)
                wait("w_nrt", 2, 2)
                dve.tensor_copy(nrT[:, :], PS[3][0:8, P:2 * P]).then_inc(s["w_nrT"], 1)
                wait("w_nrb", 2, 2)
                ch.step(tt(flat3(yb), flat3(yb), PS[4][:, :], ALU.mult))
                for p in range(2):
                    last = ts(yb[:, p], yb[:, p], pc[:, R_LNG + p:R_LNG + p + 1], pc[:, R_LNB + p:R_LNB + p + 1], ALU.mult, ALU.add)
                ch.step(last)
                ch.step(tt(yb, yb, Lm, ALU.add))
                tt(yT[:, 6:8, ds(m * W2, W2)], yb, gg, ALU.mult).then_inc(s["w_yT"], 1)
            ch.leave(NT // 2)

            dve.wait_ge(s["xr_ld"], 16 * NT)

            def modulated(dst, count, tr, done, bank=5):
                dve.wait_ge(s[tr], count)
                for k in range(4, KD):
                    last = ts(dst[:, k, :], PS[bank][:, (k - 4) * P:(k - 3) * P], s2[:, k:k + 1],
                              mod[:, M_SH2 + k:M_SH2 + k + 1], ALU.mult, ALU.add)
                last.then_inc(s[done], 1)

            for j in range(NT):
                dve.wait_ge(s["op_ps"], j + 1)
                if j >= 2:
                    dve.wait_ge(s_st[j % 2], 16 * (j // 2))
                for h in range(2):
                    ch.note(tt(xn2[:, j % 2, h * 512:(h + 1) * 512], PS[2 * (j % 2) + h][:, :], gtb[:, 0, h * 512:(h + 1) * 512],
                               ALU.mult))
                ch.wait()
                tt(x1[:, j], x1[:, j], xn2[:, j % 2], ALU.add).then_inc(s["op_x1"], 1)
                mean_square(j, 1)
                dve.wait_ge(s["rstd_ready"], NT + j + 1)
                ts(xn2[:, j % 2], x1[:, j], rs[:, j % 2:j % 2 + 1], None, ALU.mult).then_inc(s["op_xn"], 1)
                modulated(h2T, j + 1, "op_tp", "op_td")
                dve.wait_ge(s["op_lg"], j + 1)
                tt(lg[:, j], PS[6][:, 0:GROUPS + E], rbias[:, :], ALU.add).then_inc(s["op_lgd"], 1)
            dve.wait_ge(s["op_lgd"], NT)

            q = small

            def b3(ap, n):
                return ap.unsqueeze(2).to_broadcast([P, NT, n])

            def row3(ap, n):
                return ap.unsqueeze(1).to_broadcast([P, NT, n])

            L = lg[:, :, 0:GROUPS]
            X = lg[:, :, GROUPS:]

            def pick(vals, n, top, where, hot):
                ch.step(dve.tensor_reduce(top, vals, AX.X, ALU.max))
                key = rt["ky"][:, :, 0:n]
                ch.step(tt(key, vals, b3(top, n), ALU.is_ge))
                ch.step(ts(key, key, -64.0, 64.0, ALU.mult, ALU.add))
                ch.step(tt(key, key, row3(rt["i32"][:, 0:n], n), ALU.add))
                ch.step(dve.tensor_reduce(where, key, AX.X, ALU.min))
                ch.step(tt(hot, row3(rt["i32"][:, 0:n], n), b3(where, n), ALU.is_equal))

            ch.step(dve.tensor_tensor_scan(rt["i32"], ones[:, 0:E], ones[:, 0:E], -1.0, ALU.mult, ALU.add))
            ch.step(ts(rt["thr"], rt["i32"][:, 0:OVT], float(CAP), float(CAP), ALU.mult, ALU.add))
            pick(L, GROUPS, q["gm"], q["gi"], rt["goh"])
            tt(rt["ga"], L, b3(q["gm"], GROUPS), ALU.subtract).then_inc(s["rt_e1"], 1)
            ch.step(ts(rt["goh"], rt["goh"], 1.0, -NEG, ALU.subtract, ALU.mult))
            for e in range(GROUPS):
                ch.note(tt(rt["xm"][:, :, e * EPG:(e + 1) * EPG], X[:, :, e * EPG:(e + 1) * EPG],
                           rt["goh"][:, :, e:e + 1].to_broadcast([P, NT, EPG]), ALU.add))
            ch.wait()
            pick(rt["xm"], E, q["m1"], q["i1"], rt["oh1"])
            ch.step(ts(rt["tmp"], rt["oh1"], 10 * NEG, None, ALU.mult))
            ch.step(tt(rt["xm"], rt["xm"], rt["tmp"], ALU.add))
            pick(rt["xm"], E, q["m2"], q["i2"], rt["oh2"])
            tt(q["e2"], q["m2"], q["m1"], ALU.subtract).then_inc(s["rt_e1"], 1)
            tt(rt["tmp"], rt["oh1"], rt["oh2"], ALU.add).then_inc(s["rt_oh"], 1)
            dve.wait_ge(s["rt_e2"], 1)
            ch.step(dve.tensor_reduce(q["gp"], rt["gb"], AX.X, ALU.add))
            dve.wait_ge(s["rt_e2"], 2)
            ch.step(ts(q["g1"], q["e2"], 1.0, None, ALU.add))
            ch.step(tt(q["g1"], q["g1"], q["gp"], ALU.mult))
            ch.step(dve.reciprocal(q["g1"], q["g1"]))
            ch.step(tt(q["g2"], q["g1"], q["e2"], ALU.mult))
            dve.wait_ge(s["rt_pos"], 1)
            ch.step(dve.memset(rt["pre"][:, 0], 0.0))
            for j in range(NT):
                ch.step(tt(rt["pre"][:, j + 1], rt["pre"][:, j], PS[7][:, 256 + j * E:256 + (j + 1) * E], ALU.add))
            ch.step(tt(rt["pos"], PS[7][:, 0:256].rearrange("p (j e) -> p j e", e=E), rt["pre"][:, 0:NT], ALU.add))
            n_e = rt["pre"][:, NT]
            cmp = rt["cmp"].rearrange("p (e i) -> p e i", i=OVT)
            ch.step(tt(cmp, n_e.unsqueeze(2).to_broadcast([P, E, OVT]), rt["thr"].unsqueeze(1).to_broadcast([P, E, OVT]), ALU.is_gt))
            ch.step(dve.tensor_reduce(rt["nov"], cmp, AX.X, ALU.add))
            ch.step(dve.tensor_tensor_scan(rt["ci"], ones[:, 0:E], rt["nov"], 0.0, ALU.mult, ALU.add))
            ch.note(tt(rt["ob"], rt["ci"], rt["nov"], ALU.subtract))
            cm2 = rt["cmp"].rearrange("p (i e) -> p i e", e=E)
            ch.step(tt(cm2, rt["ci"].unsqueeze(1).to_broadcast([P, OVT, E]),
                       rt["i32"][:, 0:OVT].unsqueeze(2).to_broadcast([P, OVT, E]), ALU.is_le))
            ch.step(dve.tensor_reduce(rt["thr"], cm2, AX.X, ALU.add))
            ch.note(ts(eidt[:, :], rt["thr"], float(E - 1), None, ALU.min))
            ts(idy[:, 0:1], rt["ci"][:, E - 1:E], 1.0, None, ALU.max).then_inc(s["rt_n"], 1)
            for n in range(2):
                hot, where, g_ = (rt["oh1"], q["i1"], q["g1"]) if n == 0 else (rt["oh2"], q["i2"], q["g2"])
                qq, bb, c_ = (q["q1"], q["b1"], q["c1"]) if n == 0 else (q["q2"], q["b2"], q["c2"])
                ch.step(tt(rt["tmp"], hot, rt["pos"], ALU.mult))
                ch.step(dve.tensor_reduce(qq, rt["tmp"], AX.X, ALU.add))
                ch.step(tt(rt["tmp"], hot, row3(rt["ob"], E), ALU.mult))
                ch.step(dve.tensor_reduce(bb, rt["tmp"], AX.X, ALU.add))
                ch.step(tt(bb, bb, where, ALU.subtract))
                ch.step(ts(bb, bb, float(CAP), float(CAP * (E - 1)), ALU.mult, ALU.add))
                ch.step(ts(c_, qq, float(CAP), None, ALU.is_ge))
                ch.step(tt(bb, bb, c_, ALU.mult))
                ch.step(tt(bb, bb, qq, ALU.add))
                ch.step(ts(c_, where, float(CAP), None, ALU.mult))
                ch.note(tt(slot[:, n * NT:(n + 1) * NT], bb, c_, ALU.add))
                ch.note(dve.tensor_copy(ent[:, n * NT:(n + 1) * NT, 2].bitcast(F32), g_))
            ch.wait()
            dve.memset(ct[:, :], 0.0).then_inc(s["rt_ent"], 1)

            dve.wait_ge(s["rt_n"], 1)
            dve.wait_ge(s["rt_ld"], 16)

            def gate(e):
                if isinstance(e, int):
                    return tbl[:, e, 2:3].bitcast(F32)
                return tbl[:, ds(e, 1), 2:3].rearrange("p o f -> p (o f)").bitcast(F32)

            def hidden(e, par, pre="m_", free=True):
                dve.wait_ge(s[pre + "th"], e + 1)
                ch.step(stt(a1[:, par, :], th[:, par, :], 1.0, PS[2 + par][:, 0:P], ALU.add, ALU.mult))
                if free:
                    dve.wait_ge(s[pre + "dn"], e - 1)
                stt(ac[:, par, :], a1[:, par, :], 0.5, PS[2 + par][:, P:2 * P], ALU.mult, ALU.mult).then_inc(s[pre + "act"], 1)

            def result(e, par, pre="m_", free=None):
                dve.wait_ge(s[pre + "dn"], e + 1)
                if free is not None:
                    dve.wait_ge(s_sc[par], free)
                ts(yo[:, par, 512:], PS[5 + 2 * par][:, :], gate(e), None, ALU.mult).then_inc(s[pre + "yd"], 1)

            modulated(xt[:, 0], 1, "m_tx", "m_xd", 1)
            modulated(xt[:, 1], 2, "m_tx", "m_xd", 1)
            hidden(0, 0, free=False)
            modulated(xt[:, 0], 3, "m_tx", "m_xd", 1)
            hidden(1, 1, free=False)
            result(0, 0)
            modulated(xt[:, 1], 4, "m_tx", "m_xd", 1)
            hidden(2, 0)
            result(1, 1)
            with dve.Fori(0, 7) as g:
                ch.enter(g, 4)
                for u in range(4):
                    modulated(xt[:, (4 + u) % 2], g * 4 + (5 + u), "m_tx", "m_xd", 1)
                    hidden(g * 4 + (3 + u), (3 + u) % 2)
                    result(g * 4 + (2 + u), u % 2, free=g * 32 + 16 * ((2 + u) // 2))
            ch.leave(7)
            hidden(31, 1)
            result(30, 0, free=16 * 15)
            result(31, 1, free=16 * 15)
            n_ov = dve.value_load(idy[0:1, 0:1], min_val=1, max_val=OVT)
            with dve.Fori(0, n_ov) as i:
                ch.enter(i, 1)
                modulated(xt[:, 0], i + (E + 1), "m_tx", "m_xd", 1)
                hidden(i + E, 0, free=False)
                result(i + E, 0)

            dve.wait_ge(s["ld_fg"], 16)
            for j in range(NT):
                dve.wait_ge(s_fy[j % 2], 32 * (j // 2 + 1))
                a_, b_ = yab[:, j % 2, 0], yab[:, j % 2, 1]
                tt(a_, a_, b_, ALU.add).then_inc(s["f_c"], 1)
                dve.wait_ge(s["f_c"], 2 * j + 1)
                tt(a_, a_, gtb[:, 1], ALU.mult).then_inc(s["f_c"], 1)
                dve.wait_ge(s["f_c"], 2 * j + 2)
                tt(x1[:, j], x1[:, j], a_, ALU.add).then_inc(s["f_x2"], 1)
                mean_square(j, 2)
                dve.wait_ge(s["rstd_ready"], 2 * NT + j + 1)
                stt(fo[:, j % 2], x1[:, j], rs[:, j % 2:j % 2 + 1], fg, ALU.mult, ALU.mult).then_inc(s["f_o"], 1)


_INS = ["x", "c", "w_ada", "b_ada", "norm1_g", "norm2_g", "w_in", "w_out", "pool_w", "pool_scale", "attn_sinks", "conv_w",
        "rwkv_mu", "rwkv_w0", "rwkv_w2", "rwkv_a0", "rwkv_a2", "rwkv_g2", "rwkv_k_k", "rwkv_k_a", "rwkv_r_k", "rwkv_ln_g",
        "rwkv_ln_b", "moe_w_grp", "moe_b_grp", "moe_w_exp", "moe_b_exp", "moe_w_gate", "moe_w_up", "moe_w_down", "final_g"]


def kernel(**inputs):
    import numpy as _np
    import concourse.bacc as _bacc
    from concourse import mybir as _mybir
    from concourse.bass_utils import run_bass_kernel_spmd as _run

    nc = _bacc.Bacc("TRN2", target_bir_lowering=False, num_devices=1)
    arrays, args = {}, {}
    for name in _INS:
        a = _np.ascontiguousarray(inputs[name])
        arrays[f"in_{name}"] = a
        args[name] = nc.dram_tensor(f"in_{name}", a.shape, _mybir.dt.from_np(a.dtype), kind="ExternalInput").ap()
    out = nc.dram_tensor("out_dram", (1, T, D), F32, kind="ExternalOutput").ap()
    build(nc, args, out)
    r = _run(nc, [arrays], core_ids=[0])
    return r.results[0]["out_dram"]
```

```python
from contextlib import ExitStack

import numpy as np

import concourse.bass as bass
from concourse import mybir

F32 = mybir.dt.float32
I32 = mybir.dt.int32
U32 = mybir.dt.uint32
ALU = mybir.AluOpType
ACT = mybir.ActivationFunctionType
AX = mybir.AxisListType
ds = bass.ds

P = 128
D = 1024
T = 1024
KD = D // P
NT = T // P
HD = 64
CH = 64
PAD = 16
TW = T + PAD
EPS = 1e-6
GN_EPS = 64e-5
E = 32
GROUPS = 4
EPG = E // GROUPS
FE = 128
CAP = P
OVT = (2 * T - 1) // CAP
TILES = E + OVT
OOB = 1 << 20
NEG = -1e30

B_R, B_K, B_V, B_LORA, B_POOL, B_Q, B_KEY, B_VAL, B_BG, B_CG, B_XI = 0, 2, 4, 6, 7, 9, 11, 12, 13, 15, 17
NB = 19
ORDER = [B_Q, B_Q + 1, B_KEY, B_VAL, B_POOL, B_POOL + 1, *range(B_BG, NB), *range(B_R, B_POOL)]
N_ATT, N_POOL, N_CONV = 4, 6, 12
SLOT0 = 5
COL_POOL, COL_ATT, COL_CONV, COL_RWKV = 0, 256, 768, 1536
ZB = 7

R_ADA, R_G1, R_G2, R_MU, R_W0, R_A0, R_KK, R_KA, R_RK, R_LNG, R_LNB, R_PS, R_CW, NR = \
    0, 48, 56, 64, 71, 73, 75, 77, 79, 81, 83, 85, 87, 93
M_SH1, M_SC1, M_GT1, M_SH2, M_SC2, M_GT2 = 0, 8, 16, 24, 32, 40


class Chain:

    def __init__(self, eng, sem):
        self.eng, self.sem, self.base, self.n, self.loop = eng, sem, 0, 0, None

    def at(self):
        return self.base + self.n if self.loop is None else self.loop[0] * self.loop[1] + (self.base + self.n)

    def note(self, ins):
        ins.then_inc(self.sem, 1)
        self.n += 1

    def wait(self):
        self.eng.wait_ge(self.sem, self.at())

    def step(self, ins):
        self.note(ins)
        self.wait()

    def enter(self, reg, per):
        self.base, self.n, self.loop = self.base + self.n, 0, (reg, per)

    def leave(self, turns):
        per = self.loop[1]
        assert self.n == per, (self.n, per)
        self.base, self.n, self.loop = self.base + per * turns, 0, None


def build(nc, w, out):
    ctx = ExitStack()
    with ctx:
        def sb(name, shape, dt=F32):
            return ctx.enter_context(nc.sbuf_tensor(name, shape, dt))

        def sem(name):
            return ctx.enter_context(nc.semaphore(name))

        PS = [ctx.enter_context(nc.psum_tensor(f"bank{i}", [P, 512], F32)) for i in range(8)]

        xn2_d = nc.dram_tensor("xn2_d", [T, D], F32, kind="Internal")
        tbl_d = nc.dram_tensor("tbl_d", [TILES * CAP, 4], I32, kind="Internal")
        y_d = nc.dram_tensor("y_d", [2 * T, D], F32, kind="Internal")

        REG_P = sb("REG_P", [P, NB * TW])
        REG_W = sb("REG_W", [P, 15360])
        REG_Y = sb("REG_Y", [P, 8192])

        def area(reg, at, *shape):
            n = int(np.prod(shape))
            v = reg[:, at:at + n]
            names = "abcd"[:len(shape)]
            if len(shape) > 1:
                v = v.rearrange(f"p ({' '.join(names)}) -> p {' '.join(names)}", **dict(zip(names, shape)))
            return v, at + n

        pT = REG_P[:, :].rearrange("p (b t) -> p b t", b=NB)
        hT, o = area(REG_W, 0, KD, T)
        A_ATT = o
        xin, o = area(REG_W, o, 2, D)
        xn, o = area(REG_W, o, 2, D)
        A_WIN = 15360 - 2 * KD * P
        win, _ = area(REG_W, A_WIN, 2, KD, P)
        ada, _ = area(REG_P, 0, 4, KD, 512)
        yT = REG_Y[:, :].rearrange("p (k t) -> p k t", k=KD)
        qz, o = area(REG_W, A_ATT, 4, P)
        vs, o = area(REG_W, o, 2 * P)
        vt, o = area(REG_W, o, 2, 2, P)
        sc, o = area(REG_W, o, 2, 4, 2 * P)
        assert o <= A_WIN
        ptT, _ = area(REG_Y, 7 * T, 4, 2, P)
        pm1, o = area(REG_Y, 4 * T, TW)
        pm2, o = area(REG_Y, o, TW)
        acb, o = area(REG_Y, o, 2, 256)
        assert o <= 7 * T
        adb, _ = area(REG_P, 0, 2, KD, 256)
        acc, _ = area(REG_Y, 0, 4, 512)
        pmd = yT[:, 0:2, :]
        W2 = 2 * P
        z, o = area(REG_W, 0, ZB, W2)
        df, o = area(REG_W, o, ZB, W2)
        R1_DF = o
        lw, o = area(REG_W, o, 2, W2)
        Lc, o = area(REG_W, o, 2, W2)
        Lm, o = area(REG_W, o, 2, W2)
        Pc, o = area(REG_W, o, 2, W2)
        Pm = Lm
        iP = Lc
        aa, o = area(REG_W, o, 2, W2)
        gg, o = area(REG_W, o, 2, W2)
        kkr, o = area(REG_W, o, 2, W2)
        rk, o = area(REG_W, o, 2, W2)
        yb, o = area(REG_W, o, 2, W2)
        KR, o = area(REG_W, o, 2, 2, W2)
        lt, o = area(REG_W, o, W2)
        Bt, _ = area(df.rearrange("p a b -> p (a b)"), 0, 2, W2)
        Kt, _ = area(df.rearrange("p a b -> p (a b)"), 2 * W2, 2, W2)
        sq, _ = area(df.rearrange("p a b -> p (a b)"), 4 * W2, 2, W2)
        del R1_DF
        rw, rw_at = [], []
        for n in range(2):
            reg, o = (REG_P, TW * 7) if n == 0 else (REG_P, o)
            t = {}
            rw_at.append(o)
            for name, shape in (("bt", (4, HD)), ("kt", (4, HD)), ("vt", (4, HD)), ("wk", (4, 2, HD)), ("uz", (2, 4, HD)),
                                ("ab", (4, 2, P)), ("ak", (4, 2, P)), ("x", (4, P)), ("xt", (4, P)), ("t1", (4, P)),
                                ("bl", (4, P)), ("re", (2, P))):
                t[name], o = area(reg, o, *shape)
            rw.append(t)
        assert o <= NB * TW
        wo, o = area(REG_P, 0, KD, D)
        x1, o = area(REG_P, o, NT, D)
        xn2, o = area(REG_P, o, 2, D)
        h2T, o = area(REG_P, o, KD, P)
        wg, o = area(REG_W, 0, 4, KD, FE)
        wu, o = area(REG_W, o, 4, KD, FE)
        wd, o = area(REG_W, o, 4, D)
        xg, o = area(REG_Y, 0, 2, D)
        xt, o = area(REG_Y, o, 2, KD, P)
        yo, o = area(REG_Y, o, 2, D)
        th, o = area(REG_Y, o, 2, P)
        a1, o = area(REG_Y, o, 2, P)
        ac, o = area(REG_Y, o, 2, P)
        fg, o = area(REG_Y, o, D)
        disti, _ = area(REG_W, 0, 2 * P)
        disti = disti.bitcast(I32)
        o = 4 * (2 * KD * FE + D)
        rt = {}
        for name, shape in (("ga", (NT, GROUPS)), ("gb", (NT, GROUPS)), ("goh", (NT, GROUPS)), ("xm", (NT, E)), ("ky", (NT, E)),
                            ("oh1", (NT, E)), ("oh2", (NT, E)), ("pos", (NT, E)), ("pre", (NT + 1, E)), ("tmp", (NT, E)),
                            ("cmp", (E * OVT,)), ("i32", (E,)), ("thr", (OVT,)), ("nov", (E,)), ("ci", (E,)), ("ob", (E,))):
            rt[name], o = area(REG_W, o, *shape)
        small = {}
        for name in ("gm", "gi", "gp", "m1", "i1", "m2", "i2", "e2", "q1", "q2", "b1", "b2", "c1", "c2", "g1", "g2"):
            small[name], o = area(REG_W, o, NT)
        assert o <= 15360
        yab, _ = area(REG_W, 0, 2, 2, D)
        fo, _ = area(REG_W, 4096, 2, D)

        ident = sb("ident", [P, P])
        bones = sb("bones", [P, P])
        tri = sb("tri", [P, P])
        ones = sb("ones", [P, P])
        msk = sb("msk", [P, 2, P])
        lmask = sb("lmask", [P, 6, P])
        adist = sb("adist", [P, 2 * P])
        sel = sb("sel", [8, 4, P])
        rmask = sb("rmask", [P, 512])
        rc16 = sb("rc16", [P, 2, PAD])
        cnti = sb("cnti", [P, PAD], I32)
        mhalf = sb("mhalf", [P, 8])
        prow = sb("prow", [NR, P])
        pc = sb("pc", [P, NR])
        pw = sb("pw", [P, 2, P])
        lor = sb("lor", [P, 256])
        wr = sb("wr", [P, KD, GROUPS + E])
        rbias = sb("rbias", [P, GROUPS + E])
        sink = sb("sink", [P, 4])
        cc = sb("cc", [P, KD])
        ct = sb("ct", [P, KD])
        mod = sb("mod", [P, 48])
        s1 = sb("s1", [P, KD])
        s2 = sb("s2", [P, KD])
        hp = sb("hp", [P, 8])
        brk = sb("brk", [P, 2, P])
        gtb = sb("gtb", [P, 2, D])
        ss = sb("ss", [P, 2])
        rs = sb("rs", [P, 2])
        mx = sb("mx", [P, 4])
        nm = sb("nm", [P, 4])
        es = sb("es", [P, 4])
        sm = sb("sm", [P, 4])
        rd = sb("rd", [P, 4])
        nrm = sb("nrm", [P, 8])
        nrp = sb("nrp", [P, 8])
        nrT = sb("nrT", [8, P])
        S = sb("S", [P, 5, 2, HD])
        G = sb("G", [P, 8, P])
        lg = sb("lg", [P, NT, GROUPS + E])
        tbl = sb("tbl", [P, TILES, 4], I32)
        idx = sb("idx", [P, 4], I32)
        idy = sb("idy", [P, 4], I32)
        junk = sb("junk", [P, 1])

        eidt = sb("eidt", [P, OVT], I32)
        ent = sb("ent", [P, 2 * NT, 4], I32)
        slot = sb("slot", [P, 2 * NT], I32)

        def eid_view(i):
            return eidt[0:1, ds(i, 1)]

        def both(n):
            at = rw_at[n]
            return REG_P[:, at:at + 512]

        def mskb():
            return msk[:, :, :].rearrange("p a t -> p (a t)").unsqueeze(1).to_broadcast([P, 2, 2 * P])

        v = {n: w[n] for n in w}
        xd = v["x"].rearrange("b t d -> (b t) d")
        outd = out.rearrange("b t d -> (b t) d")

        names = ("wo7_ld ld_c ld_prm ld_misc ld_wr const_ready sel_ready chain_pool chain_dve  "
                 "prm_t prm_ready silu_t silu_ready mod1_ps mod1_ready mod2_ps mod2_ready "
                 "ss_ready ms_ready rstd_ready xn_ready hT_tr hT_act hT_dve "
                 "proj_ps proj_act proj_dve pad_ready acc_ready acb_ready gtb_ld "
                 "att_q att_qk att_vps att_v  att_nm att_p att_pn att_tp att_tpa att_tpd att_o att_y "
                 "pool_d pool_ps pool_y conv_y  "
                 "w_df w_z w_tanh w_lora w_th w_tha w_sg  w_gg w_L w_exp w_kkr w_sq w_ss w_nrm w_nrp w_nrt w_nrT w_nrb "
                 "w_ops w_tok w_tka w_tkd w_abp w_ab w_akp w_ak w_bl w_xt w_xp w_xa w_t1p w_t1 w_x2p w_w1p w_w1 w_uzp w_uz "
                 "w_gp w_G w_rep w_re w_hp w_S w_yp w_y w_mean w_yc w_bonp  w_yT  "
                 "wo_ld xr_ld op_ps op_x1 op_xn op_tp op_ta op_td op_lg op_lgd "
                 "rt_pos  rt_ent rt_init rt_sc rt_ld rt_n "
                 " m_tx m_xa m_xd m_gu m_th m_act m_dn m_ya m_yd "
                 "ov_w ov_g ov_sc "
                 "rt_c rt_e1 rt_e2 rt_oh ld_fg f_go ov_go f_c att_zero f_x2 f_o").split()
        s = {n: sem(n) for n in names}
        s_ada = [sem(f"ld_ada{i}") for i in range(4)]
        s_x = [sem(f"ld_x{i}") for i in range(2)]
        s_win = [sem(f"ld_win{i}") for i in range(2)]
        s_w = [sem(f"ld_expert{i}") for i in range(4)]
        s_gx = [sem(f"gathered{i}") for i in range(2)]
        s_sc = [sem(f"scattered{i}") for i in range(2)]
        s_st = [sem(f"st_xn2_{i}") for i in range(2)]
        s_fy = [sem(f"ld_y{i}") for i in range(2)]
        s_fo = [sem(f"st_out{i}") for i in range(2)]
        block = ctx.enter_context(nc.Block())

        ada_v = v["w_ada"].rearrange("l (p k) n -> (l p) k n", k=KD)
        win_v = v["w_in"].rearrange("l (k p) n -> (l p) k n", p=P)
        wo_v = v["w_out"].rearrange("l (k p) n -> (l p) k n", p=P)
        wg_v = v["moe_w_gate"].rearrange("l e (k p) f -> p (l e) k f", p=P)
        wu_v = v["moe_w_up"].rearrange("l e (k p) f -> p (l e) k f", p=P)
        wd_v = v["moe_w_down"].rearrange("l e f d -> f (l e) d")

        @block.sync
        def _(sp):
            def row(n, r, k):
                return sp.dma_start(prow[r:r + k, :], v[n])

            sp.dma_start(cc[:, :], v["c"].rearrange("b (p k) -> (b p) k", k=KD)).then_inc(s["ld_c"], 16)

            def load_ada(b):
                sp.dma_start(ada[:, b], ada_v[:, :, b * 512:(b + 1) * 512]).then_inc(s_ada[b], 16)

            def load_x(j):
                sp.dma_start(xin[:, j % 2], xd[j * P:(j + 1) * P, :]).then_inc(s_x[j % 2], 16)

            load_ada(0)
            load_x(0)
            load_ada(1)
            load_x(1)
            rows = [("b_ada", R_ADA, 48), ("norm1_g", R_G1, 8), ("norm2_g", R_G2, 8), ("rwkv_mu", R_MU, 7),
                    ("rwkv_w0", R_W0, 2), ("rwkv_a0", R_A0, 2), ("rwkv_k_k", R_KK, 2), ("rwkv_k_a", R_KA, 2),
                    ("rwkv_r_k", R_RK, 2), ("rwkv_ln_g", R_LNG, 2), ("rwkv_ln_b", R_LNB, 2), ("pool_scale", R_PS, 2)]
            for name, r, k in rows:
                sp.dma_start(prow[r:r + k, :], v[name].rearrange("l (r n) -> (l r) n", n=P)).then_inc(s["ld_prm"], 16)
            sp.dma_start(prow[R_CW:R_CW + 6, :], v["conv_w"].rearrange("l c (r n) -> (l c r) n", n=P)).then_inc(s["ld_prm"], 16)
            load_ada(2)
            load_ada(3)

            def load_win(i):
                b, u = ORDER[i], i % 2
                if B_Q <= b < B_KEY:
                    for n in range(2):
                        c0 = COL_ATT + (b - B_Q + 2 * n) * HD
                        sp.dma_start(win[:, u, :, n * HD:(n + 1) * HD], win_v[:, :, c0:c0 + HD]).then_inc(s_win[u], 16)
                    return
                if b < B_POOL:
                    c0 = COL_RWKV + b * P
                elif b < B_Q:
                    c0 = COL_POOL + (b - B_POOL) * P
                elif b < B_BG:
                    c0 = COL_ATT + 256 + (b - B_KEY) * P
                else:
                    c0 = COL_CONV + (b - B_BG) * P
                sp.dma_start(win[:, u], win_v[:, :, c0:c0 + P]).then_inc(s_win[u], 32)

            load_win(0)
            load_win(1)
            sp.wait_ge(s["const_ready"], 1)
            for g in range(4):
                h = 64 * (g % 2)
                sp.dma_start(pw[h:h + 64, g // 2, h:h + 64], v["pool_w"][0, g]).then_inc(s["ld_misc"], 16)
            sp.dma_start(lor[0:32, :], v["rwkv_w2"][0]).then_inc(s["ld_misc"], 16)
            sp.dma_start(lor[32:64, :], v["rwkv_a2"][0]).then_inc(s["ld_misc"], 16)
            sp.dma_start(lor[64:128, :], v["rwkv_g2"][0]).then_inc(s["ld_misc"], 16)
            sp.dma_start(sink[:, :], v["attn_sinks"].to_broadcast([P, 4])).then_inc(s["ld_misc"], 16)
            for j in range(2, NT):
                sp.wait_ge(s["xn_ready"], j - 1)
                load_x(j)
            sp.dma_start(rbias[:, 0:GROUPS], v["moe_b_grp"].to_broadcast([P, GROUPS])).then_inc(s["ld_wr"], 16)
            sp.dma_start(rbias[:, GROUPS:], v["moe_b_exp"].to_broadcast([P, E])).then_inc(s["ld_wr"], 16)
            sp.dma_start(wr[:, :, 0:GROUPS], v["moe_w_grp"].rearrange("l (k p) n -> (l p) k n", p=P)).then_inc(s["ld_wr"], 16)
            sp.dma_start(wr[:, :, GROUPS:], v["moe_w_exp"].rearrange("l (k p) n -> (l p) k n", p=P)).then_inc(s["ld_wr"], 16)
            for i in range(2):
                sp.dma_start(gtb[:, i], v["b_ada"][:, (2 + 3 * i) * D:(3 + 3 * i) * D].to_broadcast([P, D])).then_inc(s["gtb_ld"], 16)
            sp.wait_ge(s["acc_ready"], 4)
            for i in range(2, NB):
                sp.wait_ge(s["proj_ps"], i - 1)
                load_win(i)
                for h in range(2 * (i - 4), 2 * (i - 4) + 2) if 4 <= i < 12 else ():
                    if h >= 2:
                        sp.wait_ge(s["acb_ready"], h - 1)
                    sp.dma_start(adb[:, h % 2], ada_v[:, :, 2048 + h * 256:2304 + h * 256]).then_inc(s_ada[h % 2], 16)


            sp.wait_ge(s["w_z"], 4)
            sp.dma_start(wo[:, 0:KD - 1], wo_v[:, 0:KD - 1]).then_inc(s["wo_ld"], 16)
            sp.wait_ge(s["w_yT"], 5)
            sp.dma_start(wo[:, KD - 1], wo_v[:, KD - 1]).then_inc(s["wo7_ld"], 16)
            for j in range(NT):
                sp.dma_start(x1[:, j], xd[j * P:(j + 1) * P, :]).then_inc(s["xr_ld"], 16)

            def load_expert(u, e):
                for dst, src in ((wg, wg_v), (wu, wu_v), (wd, wd_v)):
                    view = src[:, e] if isinstance(e, int) else src[:, ds(e, 1)]
                    d_ = dst[:, u] if isinstance(e, int) else dst[:, u:u + 1]
                    sp.dma_start(d_, view).then_inc(s_w[u], 16)

            for e in range(4):
                load_expert(e, e)
            for j in range(NT):
                sp.wait_ge(s["op_xn"], j + 1)
                sp.dma_start(xn2_d[j * P:(j + 1) * P, :], xn2[:, j % 2]).then_inc(s_st[j % 2], 16)
            sp.wait_ge(s["op_ps"], NT)
            sp.dma_start(fg, v["final_g"].rearrange("(o n) -> o n", o=1).to_broadcast([P, D])).then_inc(s["ld_fg"], 16)
            with sp.Fori(1, E // 4) as g:
                for u in range(4):
                    sp.wait_ge(s["m_dn"], g * 4 + (u - 3))
                    load_expert(u, g * 4 + u)
            sp.wait_ge(s["rt_n"], 1)
            n_ov = sp.value_load(idy[0:1, 0:1], min_val=1, max_val=OVT)
            with sp.Fori(0, n_ov) as i:
                sp.wait_ge(s["ov_go"], i + 1)
                e = sp.value_load(eid_view(i), min_val=0, max_val=E - 1)
                for dst, src in ((wg, wg_v), (wu, wu_v), (wd, wd_v)):
                    sp.dma_start(dst[:, 0:1], src[:, ds(e, 1)]).then_inc(s["ov_w"], 16)
            sp.wait_ge(s["f_go"], 1)
            for j in range(NT):
                if j >= 2:
                    sp.wait_ge(s["f_x2"], j - 1)
                sp.dma_start(yab[:, j % 2, 0], y_d[j * P:(j + 1) * P, :]).then_inc(s_fy[j % 2], 16)
                sp.dma_start(yab[:, j % 2, 1], y_d[T + j * P:T + (j + 1) * P, :]).then_inc(s_fy[j % 2], 16)
                if j >= 1:
                    sp.wait_ge(s["f_o"], j)
                    sp.dma_start(outd[(j - 1) * P:j * P, :], fo[:, (j - 1) % 2]).then_inc(s_fo[(j - 1) % 2], 16)
            sp.wait_ge(s["f_o"], NT)
            sp.dma_start(outd[(NT - 1) * P:, :], fo[:, (NT - 1) % 2]).then_inc(s_fo[(NT - 1) % 2], 16)
            for n in range(2):
                sp.wait_ge(s_fo[n], 16 * NT // 2)


        @block.gpsimd
        def _(gp):
            ch = Chain(gp, s["chain_pool"])

            def keep(o_, in_, pattern, base, cm, op=ALU.is_ge, fill=0.0):
                ch.step(gp.affine_select(out=o_, in_=in_, compare_op=op, fill=fill, base=base, pattern=pattern,
                                         channel_multiplier=cm))

            ch.note(gp.memset(ident[:, :], 0.0))
            ch.note(gp.memset(pw[:, :, :], 0.0))
            ch.note(gp.memset(bones[:, :], 0.0))
            ch.step(gp.memset(ones[:, :], 1.0))
            keep(ident[:, :], ident[:, :], [[-1, P]], 0, 1, ALU.not_equal, 1.0)
            gp.memset(mhalf[:, :], -0.5).then_inc(s["const_ready"], 1)
            keep(tri[:, :], ones[:, :], [[1, P]], -1, -1)
            keep(msk[:, 1, :], ones[:, :], [[1, P]], 0, -1)
            ch.note(gp.memset(bones[0:64, 0:64], 1.0))
            ch.step(gp.memset(bones[64:P, 64:P], 1.0))
            ch.note(gp.tensor_tensor(msk[:, 0, :], tri[:, :], bones[:, :], ALU.mult))
            ch.step(gp.tensor_tensor(msk[:, 1, :], msk[:, 1, :], bones[:, :], ALU.mult))
            ch.step(gp.memset(lmask[:, :, :], 0.0))
            for l in range(6):
                b = 1 << l
                half = lmask[:, l, :].rearrange("p (n h b) -> p n h b", h=2, b=b)[:, :, 1, :]
                ch.step(gp.memset(half, 1.0))
                keep(half, half, [[-2 * b, P // (2 * b)], [0, b]], 0, 1)
                keep(half, half, [[2 * b, P // (2 * b)], [0, b]], b - 1, -1)
            ch.step(gp.iota(disti, pattern=[[1, 2 * P]], base=-P, channel_multiplier=-1))
            ch.step(gp.tensor_copy(adist[:, :], disti))
            keep(adist[:, :], adist[:, :], [[-1, 2 * P]], P, 1, fill=NEG)
            keep(adist[:, :], adist[:, :], [[1, 2 * P]], -1, -1, fill=NEG)
            ch.step(gp.memset(sel[:, :, :], 0.0))
            sv = sel[:, :, :].rearrange("p a (h d) -> p a h d", h=2)
            keep(sv, sv, [[-2, 4], [-1, 2], [0, HD]], 0, 1, ALU.not_equal, 1.0)
            ch.step(gp.memset(rmask[:, :], 1.0))
            ch.step(gp.memset(rmask[:, 0:512:CH], 0.0))
            ch.step(gp.iota(cnti[:, :], pattern=[[1, PAD]], base=1, channel_multiplier=0))
            for c in range(2):
                ch.step(gp.tensor_copy(rc16[:, c, :], cnti[:, :]))
                for h in range(2):
                    rows = rc16[64 * h:64 * h + 64, c, :]
                    ch.step(gp.tensor_scalar(rows, rows, float(2 << (2 * c + h)), None, ALU.min))
            gp.memset(S[:, 4], 0.0)
            gp.memset(G[:, :, :], 0.0)
            ch.note(gp.iota(ent[:, :, 0], pattern=[[P, 2 * NT]], base=0, channel_multiplier=1))
            ch.note(gp.iota(ent[:, :, 1], pattern=[[0, 2], [P, NT]], base=0, channel_multiplier=1))
            ch.note(gp.iota(ent[:, :, 3], pattern=[[0, 2 * NT]], base=0, channel_multiplier=0))
            gp.memset(tbl[:, :, :], OOB).then_inc(s["sel_ready"], 1)

            def power(out_, in_, n, ready, done, count):
                gp.wait_ge(s[ready], count)
                gp.tensor_tensor(out_, in_, mhalf[:, 0:n], ALU.pow).then_inc(s[done], 1)

            for j in range(NT):
                power(rs[:, j % 2:j % 2 + 1], ss[:, j % 2:j % 2 + 1], 1, "ms_ready", "rstd_ready", j + 1)

            gp.wait_ge(s["sel_ready"], 1)
            gp.dma_start(tbl_d[:, :].rearrange("(p t) f -> p t f", p=P), tbl[:, :, :]).then_inc(s["rt_init"], 16)

            gp.wait_ge(s["acc_ready"], 4)
            gp.memset(pT[:, ZB:, 0:PAD], 0.0).then_inc(s["pad_ready"], 1)

            gp.wait_ge(s["proj_act"], N_POOL)
            gp.wait_ge(s["proj_dve"], N_POOL)
            gp.wait_ge(s["pad_ready"], 1)
            gp.wait_ge(s["rt_c"], 1)
            ch.step(gp.memset(pm1[:, 0:PAD], 0.0))
            ch.step(gp.memset(pm2[:, 0:PAD], 0.0))
            for c in range(2):
                u = pT[:, B_POOL + c]
                src, dst, steps = u, pm1, 2 + 2 * c
                for n in range(steps):
                    sh = 1 << n
                    ch.step(gp.tensor_tensor(dst[:, PAD:], src[:, PAD:], src[:, PAD - sh:TW - sh], ALU.add))
                    if n >= steps - 2:
                        h = n - (steps - 2)
                        r = slice(64 * h, 64 * h + 64)
                        wdt = float(2 * sh)
                        ch.note(gp.tensor_scalar(pmd[r, c, PAD:], dst[r, 2 * PAD:], 1.0 / wdt, None, ALU.mult))
                        ch.step(gp.tensor_tensor(pmd[r, c, 0:PAD], dst[r, PAD:2 * PAD], rc16[r, c, :], ALU.mult))
                    src, dst = dst, (pm2 if dst is pm1 else pm1)
                gp.tensor_tensor(pmd[:, c, :], pmd[:, c, :], u[:, PAD:], ALU.subtract).then_inc(s["pool_d"], 1)
            gp.wait_ge(s["prm_ready"], 1)
            gp.wait_ge(s["proj_act"], N_CONV)
            gp.wait_ge(s["proj_dve"], N_CONV)
            for c in range(2):
                zc, yc, tap = pT[:, B_CG + c], pT[:, B_XI + c], yT[:, 4 + c, :]
                ch.step(gp.tensor_tensor(zc, zc, yc, ALU.mult))
                ch.step(gp.tensor_scalar(yc[:, PAD:], zc[:, PAD - 2:TW - 2], pc[:, R_CW + c:R_CW + c + 1], None, ALU.mult))
                for n in (1, 2):
                    ch.step(gp.tensor_scalar(tap, zc[:, PAD - 2 + n:TW - 2 + n],
                                             pc[:, R_CW + 2 * n + c:R_CW + 2 * n + c + 1], None, ALU.mult))
                    ch.step(gp.tensor_tensor(yc[:, PAD:], yc[:, PAD:], tap, ALU.add))
                gp.tensor_tensor(tap, yc[:, PAD:], pT[:, B_BG + c, PAD:], ALU.mult).then_inc(s["conv_y"], 1)
                gp.wait_ge(s["conv_y"], c + 1)
            gp.wait_ge(s["acb_ready"], 16)
            gp.memset(pT[:, 0:ZB, 0:PAD], 0.0).then_inc(s["pad_ready"], 1)

            LB = 6
            with gp.Fori(0, NT // 2) as m:
                prev, at = gp.snap(m * W2 + (PAD - 1)), gp.snap(m * W2 + PAD)
                gp.wait_ge(s["w_yT"], m + 1)
                gp.tensor_tensor(df, pT[:, 0:ZB, ds(prev, W2)], pT[:, 0:ZB, ds(at, W2)], ALU.subtract).then_inc(s["w_df"], 1)
                power(nrp[:, :], nrm[:, :], 8, "w_nrm", "w_nrp", m * 2 + 1)
                for l in range(LB):
                    for n in range(2):
                        if l == 0:
                            gp.wait_ge(s["w_ab"], m * 2 + (n + 1))
                        elif l == 1:
                            gp.wait_ge(s["w_xt"], m * 12 + (n + 1))
                        else:
                            gp.wait_ge(s["w_t1p"], m * 10 + (2 * (l - 2) + n + 1))
                        gp.tensor_tensor(rw[n]["bl"], rw[n]["ab"][:, :, 0, :],
                                         lmask[:, l:l + 1, :].to_broadcast([P, 4, P]), ALU.mult).then_inc(s["w_bl"], 1)
                power(nrp[:, :], nrm[:, :], 8, "w_nrm", "w_nrp", m * 2 + 2)

            for j in range(NT):
                power(rs[:, j % 2:j % 2 + 1], ss[:, j % 2:j % 2 + 1], 1, "ms_ready", "rstd_ready", NT + j + 1)
            gp.wait_ge(s["rt_init"], 16)
            gp.wait_ge(s["rt_ent"], 1)
            for a in range(2 * NT):
                gp.indirect_dma_start(out=tbl_d[:, :], out_offset=bass.IndirectOffsetOnAxis(ap=slot[:, a:a + 1], axis=0),
                                      in_=ent[:, a, :], in_offset=None, bounds_check=TILES * CAP - 1,
                                      oob_is_err=False).then_inc(s["rt_sc"], 16)
            gp.wait_ge(s["rt_sc"], 16 * 2 * NT)
            gp.dma_start(tbl[:, :, :], tbl_d[:, :].rearrange("(t p) f -> p t f", p=P)).then_inc(s["rt_ld"], 16)
            gp.wait_ge(s["op_ps"], NT)
            ch.step(gp.memset(xg, 0.0))
            gp.wait_ge(s["rt_ld"], 16)
            gp.wait_ge(s_st[0], 16 * NT // 2)
            gp.wait_ge(s_st[1], 16 * NT // 2)

            def tview(e, c):
                if isinstance(e, int):
                    return tbl[:, e, c:c + 1]
                return tbl[:, ds(e, 1), c:c + 1].rearrange("p o f -> p (o f)")

            last_row, last_out = gp.to_reg(T - 1), gp.to_reg(2 * T - 1)

            def pause():
                ch.note(gp.tensor_tensor(junk[:, :], mhalf[:, 0:1], mhalf[:, 0:1], ALU.mult))

            def gather(e, par):
                row_ = e if isinstance(e, int) else gp.snap(e)
                if not isinstance(e, int) or e >= 2:
                    gp.wait_ge(s["m_tx"], e - 1)
                ch.step(gp.tensor_copy(idx[:, par:par + 1], tview(row_, 1)))
                pause()
                gp.indirect_dma_start(out=xg[:, par], out_offset=None, in_=xn2_d[:, :],
                                      in_offset=bass.IndirectOffsetOnAxis(ap=idx[:, par:par + 1], axis=0),
                                      bounds_check=last_row, oob_is_err=False).then_inc(s_gx[par], 16)

            def scatter(e, par):
                row_ = e if isinstance(e, int) else gp.snap(e)
                gp.wait_ge(s["m_ya"], e + 1)
                gp.wait_ge(s["m_yd"], e + 1)
                ch.step(gp.tensor_copy(idx[:, 2 + par:3 + par], tview(row_, 0)))
                pause()
                gp.indirect_dma_start(out=y_d[:, :], out_offset=bass.IndirectOffsetOnAxis(ap=idx[:, 2 + par:3 + par], axis=0),
                                      in_=yo[:, par], in_offset=None, bounds_check=last_out,
                                      oob_is_err=False).then_inc(s_sc[par], 16)

            gather(0, 0)
            gather(1, 1)
            gather(2, 0)
            with gp.Fori(0, 7) as g:
                ch.enter(g, 16)
                for u in range(4):
                    gather(g * 4 + (3 + u), (1 + u) % 2)
                    scatter(g * 4 + u, u % 2)
            ch.leave(7)
            gather(31, 1)
            for e in (28, 29, 30, 31):
                scatter(e, e % 2)
            for par in range(2):
                gp.wait_ge(s_sc[par], 16 * E // 2)

            n_ov = gp.value_load(idy[0:1, 0:1], min_val=1, max_val=OVT)
            gp.sem_inc(s["ov_go"], 1)
            with gp.Fori(0, n_ov) as i:
                ch.enter(i, 4)
                row_ = gp.snap(i + E)
                ch.step(gp.tensor_copy(idx[:, 0:1], tview(row_, 1)))
                pause()
                gp.indirect_dma_start(out=xg[:, 0], out_offset=None, in_=xn2_d[:, :],
                                      in_offset=bass.IndirectOffsetOnAxis(ap=idx[:, 0:1], axis=0),
                                      bounds_check=last_row, oob_is_err=False).then_inc(s["ov_g"], 16)
                ch.step(gp.tensor_copy(idx[:, 2:3], tview(row_, 0)))
                gp.wait_ge(s["m_ya"], i + (E + 1))
                gp.wait_ge(s["m_yd"], i + (E + 1))
                pause()
                gp.indirect_dma_start(out=y_d[:, :], out_offset=bass.IndirectOffsetOnAxis(ap=idx[:, 2:3], axis=0),
                                      in_=yo[:, 0], in_offset=None, bounds_check=last_out,
                                      oob_is_err=False).then_inc(s["ov_sc"], 16)
                gp.wait_ge(s["ov_sc"], i * 16 + 16)
                gp.sem_inc(s["ov_go"], 1)
            gp.sem_inc(s["f_go"], 1)
            for j in range(NT):
                power(rs[:, j % 2:j % 2 + 1], ss[:, j % 2:j % 2 + 1], 1, "ms_ready", "rstd_ready", 2 * NT + j + 1)

        @block.tensor
        def _(pe):
            def mm(o_, l, r, start=True, stop=True):
                return pe.matmul(o_, l, r, start=start, stop=stop, skip_group_check=True)

            def columns(out_, sums, n):
                for q in range(n):
                    last = mm(out_[:, q:q + 1], sums[:, q * P:(q + 1) * P], ones[:, 0:1])
                return last

            pe.wait_ge(s["sel_ready"], 1)
            pe.wait_ge(s["ld_prm"], 16 * 13)
            pe.transpose(PS[7][:, 0:NR], prow[:, :], ident[0:NR, 0:NR]).then_inc(s["prm_t"], 1)
            for b in range(4):
                pe.wait_ge(s["acc_ready"], b + 1)
                last = columns(PS[6][:, 4 * b:4 * b + 4], acc[:, b], 4)
            last.then_inc(s["mod1_ps"], 1)

            for j in range(NT):
                pe.wait_ge(s["xn_ready"], j + 1)
                if j >= 2:
                    pe.wait_ge(s["hT_act"], j - 1)
                    pe.wait_ge(s["hT_dve"], j - 1)
                for k in range(KD):
                    last = pe.transpose(PS[2 * (j % 2) + k // 4][:, (k % 4) * P:(k % 4 + 1) * P],
                                        xn[:, j % 2, k * P:(k + 1) * P], ident[:, :])
                last.then_inc(s["hT_tr"], 1)
            pe.wait_ge(s["hT_act"], NT)
            pe.wait_ge(s["hT_dve"], NT)
            pe.wait_ge(s["mod1_ready"], 1)

            def project(par, loads, done, mid=None):
                pe.wait_ge(s_win[par], loads)
                if done is not None:
                    pe.wait_ge(s["proj_act"], done)
                    pe.wait_ge(s["proj_dve"], done)
                for k in range(KD):
                    if k == KD // 2 and mid is not None:
                        mid()
                    for h in range(2):
                        last = mm(PS[2 * par + h][:, :], win[:, par, k, :], hT[:, k, h * 512:(h + 1) * 512], k == 0, k == KD - 1)
                last.then_inc(s["proj_ps"], 1)

            def scores(nb):
                first = isinstance(nb, int) and nb == 0
                k0 = 1 if first else 0
                ks = slice(nb * P + (PAD - P * (1 - k0)), nb * P + PAD + P) if isinstance(nb, int) else \
                    ds(nb * P + (PAD - P), 2 * P)
                pe.wait_ge(s["att_q"], nb + 1)
                if not isinstance(nb, int) or nb >= 2:
                    pe.wait_ge(s["att_tpa"], nb - 1)
                    pe.wait_ge(s["att_tpd"], nb - 1)
                for h in range(4):
                    last = mm(PS[4 + h // 2][:, (h % 2) * 256 + k0 * P:(h % 2) * 256 + 256], qz[:, h, :], pT[:, B_KEY, ks])
                last.then_inc(s["att_qk"], 1)
                if not first:
                    pe.wait_ge(s["mod2_ready"], nb)
                for kb in range(k0, 2):
                    last = pe.transpose(PS[6][:, kb * P:(kb + 1) * P], vs[:, kb * P:(kb + 1) * P], ident[:, :])
                last.then_inc(s["att_vps"], 1)

            def flip_probs(nb, par, nxt=True):
                k0 = 1 if isinstance(nb, int) and nb == 0 else 0
                pe.wait_ge(s["att_pn"], nb + 1)
                if nxt:
                    pe.wait_ge(s["att_nm"], nb + 2)
                for h in range(4):
                    for kb in range(k0, 2):
                        last = pe.transpose(PS[4 + h // 2][:, ((h % 2) * 2 + kb) * P:((h % 2) * 2 + kb + 1) * P],
                                            sc[:, par, h, kb * P:(kb + 1) * P], ident[:, :])
                last.then_inc(s["att_tp"], 1)

            def outputs(nb, par):
                k0 = 1 if isinstance(nb, int) and nb == 0 else 0
                pe.wait_ge(s["att_v"], nb + 1)
                pe.wait_ge(s["att_tpa"], nb + 1)
                pe.wait_ge(s["att_tpd"], nb + 1)
                if not isinstance(nb, int) or nb >= 1:
                    pe.wait_ge(s["att_y"], nb)
                for h in range(4):
                    r = 64 * (h % 2)
                    for kb in range(k0, 2):
                        last = mm(PS[7][r:r + 64, (h // 2) * P:(h // 2 + 1) * P], vt[:, par, kb, (h // 2) * HD:(h // 2 + 1) * HD],
                                  ptT[:, h, kb, :], kb == k0, kb == 1)
                last.then_inc(s["att_o"], 1)

            def sums(nb, gates):
                pe.wait_ge(s["acb_ready"], nb * 2 + 2)
                pe.wait_ge(s["att_v"], nb + 1)
                if gates:
                    last = mm(PS[6][:, :], ones[:, :], acb.rearrange("p a b -> p (a b)"))
                else:
                    last = columns(PS[6][:, 0:4], acb.rearrange("p a b -> p (a b)"), 4)
                last.then_inc(s["mod2_ps"], 1)

            for i in range(SLOT0):
                project(i % 2, 32 * (i // 2 + 1), i - 1 if i >= 2 else None)
            scores(0)
            project(1, 32 * 3, 4, lambda: sums(0, True))
            scores(1)
            project(0, 32 * 4, 5, lambda: (flip_probs(0, 0), sums(1, True)))

            def beside(g, u, gates):
                outputs(g * 2 + u, u)
                scores(g * 2 + (2 + u))
                project((1 + u) % 2, g * 32 + 32 * (4 + u), g * 2 + (6 + u),
                        lambda: (flip_probs(g * 2 + (1 + u), (1 + u) % 2), sums(g * 2 + (2 + u), gates)))

            with pe.Fori(0, 2) as g:
                for u in range(2):
                    beside(g, u, False)
            for u in range(2):
                beside(2, u, True)
            outputs(6, 0)
            project(1, 32 * 7, 12, lambda: flip_probs(7, 1, False))
            outputs(7, 1)
            project(0, 32 * 8, 13)
            pe.wait_ge(s["ld_misc"], 16 * 8)
            pe.wait_ge(s["att_y"], NT)
            for c in range(2):
                pe.wait_ge(s["pool_d"], c + 1)
                if c == 1:
                    pe.wait_ge(s["pool_y"], 2)
                for h in range(2):
                    last = mm(PS[6 + h][:, :], pw[:, c, :], pmd[:, c, h * 512:(h + 1) * 512])
                last.then_inc(s["pool_ps"], 1)
                project(1 - c, 32 * (8 + c), 14 + c)
            project(1, 32 * 9, 16)
            project(0, 32 * 10, 17)
            pe.wait_ge(s["proj_act"], NB)
            pe.wait_ge(s["proj_dve"], NB)
            pe.wait_ge(s["pool_y"], 4)

            with pe.Fori(0, NT // 2) as m:
                def wait(name, per, k):
                    pe.wait_ge(s[name], m * per + k)

                def hb(h):
                    return slice(64 * (h % 2), 64 * (h % 2) + 64)

                wait("w_tanh", 1, 1)
                for p in range(2):
                    last = mm(PS[0][:, p * W2:(p + 1) * W2], lor[0:32, p * P:(p + 1) * P], lt[0:32, :])
                last.then_inc(s["w_lora"], 1)
                for p in range(2):
                    last = mm(PS[1][:, p * W2:(p + 1) * W2], lor[32:64, p * P:(p + 1) * P], z[32:64, B_LORA, :])
                last.then_inc(s["w_lora"], 1)
                wait("w_sg", 1, 1)
                for p in range(2):
                    last = mm(PS[2][:, p * W2:(p + 1) * W2], lor[64:128, p * P:(p + 1) * P], lt[64:128, :])
                last.then_inc(s["w_lora"], 1)

                def head_norms(bank, k):
                    wait("w_sq", 2, k)
                    for n in range(2):
                        for p in range(2):
                            c = n * 4 + p * 2
                            last = mm(PS[3][:, c:c + 2], sq[:, p, n * P:(n + 1) * P], bones[:, 0:P:64])
                    last.then_inc(s["w_ss"], 1)
                    wait("w_nrp", 2, k)
                    pe.transpose(PS[3][0:8, P:2 * P], nrp[:, :], ident[:, :]).then_inc(s["w_nrt"], 1)
                    wait("w_nrT", 2, k)
                    for p in range(2):
                        for n in range(2):
                            last = mm(PS[bank][:, p * W2 + n * P:p * W2 + (n + 1) * P], sel[:, n * 2 + p, :], nrT[:, :])
                    last.then_inc(s["w_nrb"], 1)

                head_norms(4, 1)
                wait("w_ops", 1, 1)
                wait("w_gg", 1, 1)
                for n in range(2):
                    tk = slice(n * P, (n + 1) * P)
                    for i, src in enumerate((Bt, Kt)):
                        for p in range(2):
                            pe.transpose(PS[4 * n][:, (2 * i + p) * P:(2 * i + p + 1) * P], src[:, p, tk], ident[:, :])
                    for p in range(2):
                        pe.transpose(PS[4 * n + 1][:, p * P:(p + 1) * P], z[:, B_V + p, tk], ident[:, :])
                        last = pe.transpose(PS[4 * n + 1][:, (2 + p) * P:(3 + p) * P], KR[:, p, 0, tk], ident[:, :])
                    last.then_inc(s["w_tok"], 1)
                    for h in range(4):
                        last = mm(PS[4 * n + 2 + h % 2][:, (h // 2) * 256:(h // 2) * 256 + 256].rearrange("p (a t) -> p a t", a=2),
                                  Bt[hb(h), h // 2, tk], KR[hb(h), h // 2, :, tk])
                    last.then_inc(s["w_abp"], 1)
                for n in range(2):
                    tk = slice(n * P, (n + 1) * P)
                    wait("w_tka", 2, n + 1)
                    wait("w_tkd", 2, n + 1)
                    for h in range(4):
                        last = mm(PS[4 * n + h % 2][:, (h // 2) * 256:(h // 2) * 256 + 256].rearrange("p (a t) -> p a t", a=2),
                                  Kt[hb(h), h // 2, tk], KR[hb(h), h // 2, :, tk])
                    last.then_inc(s["w_akp"], 1)

                def four(n, bank, l, r, sem_name):
                    for h in range(4):
                        last = mm(PS[4 * n + bank][:, h * P:(h + 1) * P], l[:, h, :], r[:, h, :])
                    last.then_inc(s[sem_name], 1)

                def flip(n, bank):
                    for h in range(4):
                        last = pe.transpose(PS[4 * n + bank][:, h * P:(h + 1) * P], rw[n]["xt"][:, h, :], ident[:, :])
                    last.then_inc(s["w_xp"], 1)

                for n in range(2):
                    wait("w_xt", 12, n + 1)
                    flip(n, 2)
                for n in range(2):
                    wait("w_ak", 2, n + 1)
                    for h in range(4):
                        last = mm(PS[4 * n][:, h * HD:(h + 1) * HD], rw[n]["ak"][:, h, 0, :], rw[n]["vt"][:, h, :])
                    last.then_inc(s["w_w1p"], 1)
                for l in range(1, 6):
                    for n in range(2):
                        wait("w_xa", 10, 2 * (l - 1) + n + 1)
                        wait("w_bl", 12, 2 * l + n + 1)
                        four(n, 3, rw[n]["bl"], rw[n]["x"], "w_t1p")
                    for n in range(2):
                        wait("w_t1", 10, 2 * (l - 1) + n + 1)
                        four(n, 2, rw[n]["t1"], rw[n]["xt"], "w_x2p")
                    if l < 5:
                        for n in range(2):
                            wait("w_xt", 12, 2 * l + n + 1)
                            flip(n, 3)
                for n in range(2):
                    wait("w_xt", 12, 10 + n + 1)
                    wait("w_w1", 2, n + 1)
                    for h in range(4):
                        last = mm(PS[4 * n + 1][:, h * P:(h + 1) * P], rw[n]["xt"][:, h, :],
                                  rw[n]["wk"][:, h].rearrange("p a d -> p (a d)"))
                    last.then_inc(s["w_uzp"], 1)
                for n in range(2):
                    wait("w_uz", 2, n + 1)
                    uz, bt = rw[n]["uz"], rw[n]["bt"]
                    for h in range(4):
                        last = mm(PS[4 * n + 3][hb(h), (h // 2) * P:(h // 2 + 1) * P], uz[:, 1, h, :], rw[n]["ab"][:, h, 1, :])
                    last.then_inc(s["w_rep"], 1)
                    for c in range(2):
                        rr = slice(64 * c, 64 * c + 64)
                        for h in range(4):
                            last = mm(PS[4 * n + 2 - c][hb(h), (h // 2) * HD:(h // 2 + 1) * HD], uz[rr, 1, h, :], bt[rr, h, :])
                    last.then_inc(s["w_gp"], 1)
                for n in range(2):
                    t = rw[n]
                    for c in range(2):
                        rr = slice(64 * c, 64 * c + 64)
                        for p in range(2):
                            o_ = PS[4 * n + 3 * c][:, p * HD:(p + 1) * HD]
                            for h in (2 * p, 2 * p + 1):
                                mm(o_[hb(h), :], t["bt"][rr, h, :], t["uz"][rr, 0, h, :], True, False)
                                mm(o_[hb(h), :], t["kt"][rr, h, :], t["vt"][rr, h, :], False, False)
                            if p == 0:
                                if c == 0:
                                    wait("w_G", 2, n + 1)
                                wait("w_S", 5, 2 * n + c + 1)
                            last = mm(o_, G[:, 4 * n + c * 2 + p, :], S[:, 2 * n + c, p, :], False, True)
                        last.then_inc(s["w_hp"], 1)
                for n in range(2):
                    wait("w_re", 2, n + 1)
                    t = rw[n]
                    for h in range(4):
                        p = h // 2
                        o_ = PS[4 * n + 1][hb(h), p * P:(p + 1) * P]
                        mm(o_, t["uz"][:, 0, h, :], t["ab"][:, h, 1, :], True, False)
                        mm(o_, t["vt"][:, h, :], t["ak"][:, h, 1, :], False, False)
                        for c in range(2):
                            cs = slice(64 * c, 64 * c + 64)
                            last = mm(o_[:, cs], S[hb(h), 2 * n + c, p, :], t["re"][hb(h), p, cs], False, c == 1)
                    last.then_inc(s["w_yp"], 1)
                wait("w_y", 2, 2)
                mm(PS[2][:, :], bones[:, :], yb.rearrange("p a t -> p (a t)")).then_inc(s["w_mean"], 1)
                for p in range(2):
                    last = mm(PS[5][:, p * W2:(p + 1) * W2], brk[:, p, :], rk[:, p, :])
                last.then_inc(s["w_bonp"], 1)
                head_norms(4, 2)

            pe.wait_ge(s["w_yT"], 5)
            pe.wait_ge(s["wo_ld"], 16)
            pe.wait_ge(s["ld_wr"], 16 * 4)

            def out_main(j):
                if j >= 2:
                    pe.wait_ge(s["op_x1"], j - 1)
                for k in range(KD):
                    if j == 0 and k == KD - 1:
                        pe.wait_ge(s["wo7_ld"], 16)
                    for h in range(2):
                        last = mm(PS[2 * (j % 2) + h][:, :], yT[:, k, j * P:(j + 1) * P], wo[:, k, h * 512:(h + 1) * 512],
                                  k == 0, k == KD - 1)
                last.then_inc(s["op_ps"], 1)

            out_main(0)
            for j in range(NT):
                if j + 1 < NT:
                    out_main(j + 1)
                pe.wait_ge(s["op_xn"], j + 1)
                if j >= 1:
                    pe.wait_ge(s["op_ta"], j)
                    pe.wait_ge(s["op_td"], j)
                for k in range(KD):
                    last = pe.transpose(PS[4 + k // 4][:, (k % 4) * P:(k % 4 + 1) * P], xn2[:, j % 2, k * P:(k + 1) * P],
                                        ident[:, :])
                last.then_inc(s["op_tp"], 1)
                pe.wait_ge(s["op_ta"], j + 1)
                pe.wait_ge(s["op_td"], j + 1)
                if j >= 1:
                    pe.wait_ge(s["op_lgd"], j)
                for k in range(KD):
                    last = mm(PS[6][:, 0:GROUPS + E], h2T[:, k, :], wr[:, k, :], k == 0, k == KD - 1)
                last.then_inc(s["op_lg"], 1)

            pe.wait_ge(s["rt_oh"], 1)
            flat = rt["tmp"].rearrange("p a b -> p (a b)")
            mm(PS[7][:, 0:NT * E], tri[:, :], flat)
            mm(PS[7][:, 256:256 + NT * E], ones[:, :], flat).then_inc(s["rt_pos"], 1)

            def ex_t(e, par, pre="m_", gsem=None, gcount=None, wait_free=True):
                pe.wait_ge(gsem, gcount)
                if wait_free:
                    pe.wait_ge(s[pre + "xa"], e)
                    pe.wait_ge(s[pre + "xd"], e)
                for k in range(KD):
                    last = pe.transpose(PS[k // 4][:, (k % 4) * P:(k % 4 + 1) * P], xg[:, par, k * P:(k + 1) * P], ident[:, :])
                last.then_inc(s[pre + "tx"], 1)

            def ex_gu(e, par, u, pre="m_", wsem=None, wcount=None, wait_free=True):
                pe.wait_ge(s[pre + "xa"], e + 1)
                pe.wait_ge(s[pre + "xd"], e + 1)
                pe.wait_ge(wsem, wcount)
                if wait_free:
                    pe.wait_ge(s[pre + "act"], e - 1)
                for i, wt in enumerate((wg, wu)):
                    for k in range(KD):
                        last = mm(PS[2 + par][:, i * P:(i + 1) * P], wt[:, u, k, :], xt[:, par, k, :], k == 0, k == KD - 1)
                last.then_inc(s[pre + "gu"], 1)

            def ex_dn(e, par, u, pre="m_", wait_free=True):
                pe.wait_ge(s[pre + "act"], e + 1)
                if wait_free:
                    pe.wait_ge(s[pre + "ya"], e - 1)
                    pe.wait_ge(s[pre + "yd"], e - 1)
                for h in range(2):
                    last = mm(PS[4 + 2 * par + h][:, :], ac[:, par, :], wd[:, u, h * 512:(h + 1) * 512])
                last.then_inc(s[pre + "dn"], 1)

            ex_t(0, 0, gsem=s_gx[0], gcount=16, wait_free=False)
            ex_t(1, 1, gsem=s_gx[1], gcount=16)
            ex_gu(0, 0, 0, wsem=s_w[0], wcount=48, wait_free=False)

            def turn(e, u1, gcount_, wcount_, first):
                ex_t(e + 1, (u1 + 1) % 2, gsem=s_gx[(u1 + 1) % 2], gcount=gcount_)
                ex_gu(e, u1 % 2, u1 % 4, wsem=s_w[u1 % 4], wcount=wcount_, wait_free=not first)
                ex_dn(e - 1, (u1 - 1) % 2, (u1 - 1) % 4, wait_free=not first)

            turn(1, 1, 32, 48, True)
            ex_t(3, 1, gsem=s_gx[1], gcount=32)
            ex_gu(2, 0, 2, wsem=s_w[2], wcount=48)
            ex_dn(1, 1, 1, wait_free=False)
            with pe.Fori(0, 7) as g:
                for u in range(4):
                    turn(g * 4 + (3 + u), 3 + u, g * 32 + 16 * ((4 + u) // 2 + 1), g * 48 + 48 * ((3 + u) // 4 + 1), False)
            ex_gu(31, 1, 3, wsem=s_w[3], wcount=48 * 8)
            ex_dn(30, 0, 2)
            ex_dn(31, 1, 3)

            n_ov = pe.value_load(idy[0:1, 0:1], min_val=1, max_val=OVT)
            pe.wait_ge(s["m_ya"], E)
            pe.wait_ge(s["m_yd"], E)
            with pe.Fori(0, n_ov) as i:
                ex_t(i + E, 0, "m_", s["ov_g"], i * 16 + 16, False)
                ex_gu(i + E, 0, 0, "m_", s["ov_w"], i * 48 + 48, False)
                ex_dn(i + E, 0, 0, "m_", False)

        @block.scalar
        def _(act):
            def fn(o_, i_, f=ACT.Copy, **kw):
                return act.activation(o_, i_, f, **kw)

            act.wait_ge(s["ld_c"], 16)
            fn(ct[:, :], cc[:, :], ACT.Tanh, scale=0.5).then_inc(s["silu_t"], 1)

            def square(j):
                act.wait_ge(s_x[j % 2], 16 * (j // 2 + 1))
                fn(xn[:, j % 2], xin[:, j % 2], ACT.Square, accum_out=ss[:, j % 2:j % 2 + 1]).then_inc(s["ss_ready"], 1)

            square(0)
            square(1)
            act.wait_ge(s["mod1_ready"], 1)
            for j in range(NT):
                act.wait_ge(s["hT_tr"], j + 1)
                for k in range(4):
                    last = fn(hT[:, k, j * P:(j + 1) * P], PS[2 * (j % 2)][:, k * P:(k + 1) * P], ACT.Identity,
                              scale=s1[:, k:k + 1], bias=mod[:, M_SH1 + k:M_SH1 + k + 1])
                last.then_inc(s["hT_act"], 1)
                if j + 2 < NT:
                    square(j + 2)

            def projected(i, par, blk=None):
                act.wait_ge(s["proj_ps"], i + 1)
                dst = pT[:, ORDER[i], PAD:PAD + 512] if blk is None else \
                    pT[:, ds(blk, 1), PAD:PAD + 512].rearrange("p o t -> p (o t)")
                fn(dst, PS[2 * par][:, :]).then_inc(s["proj_act"], 1)

            def queries(nb):
                first = isinstance(nb, int) and nb == 0
                k0 = 1 if first else 0
                tok = slice(nb * P + PAD, nb * P + PAD + P) if isinstance(nb, int) else ds(nb * P + PAD, P)
                at = slice(nb * P + PAD - P * (1 - k0), nb * P + PAD + P) if isinstance(nb, int) else ds(nb * P + (PAD - P), 2 * P)
                if not first:
                    act.wait_ge(s["att_qk"], nb)
                    act.wait_ge(s["att_vps"], nb)
                for kv in range(2):
                    r = slice(64 * kv, 64 * kv + 64)
                    fn(qz[r, 2 * kv:2 * kv + 2, :], pT[r, B_Q:B_Q + 2, tok], scale=float(HD) ** -0.5)
                fn(vs[:, k0 * P:], pT[:, B_VAL, at]).then_inc(s["att_q"], 1)

            def values(nb, par):
                k0 = 1 if isinstance(nb, int) and nb == 0 else 0
                act.wait_ge(s["att_vps"], nb + 1)
                fn(vt[:, par, k0:, :], PS[6][:, k0 * P:256].rearrange("p (a b) -> p a b", b=P)).then_inc(s["att_v"], 1)

            def exps(nb, par):
                k0 = 1 if isinstance(nb, int) and nb == 0 else 0
                act.wait_ge(s["att_nm"], nb + 1)
                for h in range(4):
                    fn(sc[:, par, h, k0 * P:], sc[:, par, h, k0 * P:], ACT.Exp, bias=nm[:, h:h + 1], accum_out=sm[:, h:h + 1])
                fn(es[:, :], es[:, :], ACT.Exp).then_inc(s["att_p"], 1)

            def flipped(nb):
                k0 = 1 if isinstance(nb, int) and nb == 0 else 0
                act.wait_ge(s["att_tp"], nb + 1)
                fn(ptT[:, 0:2, k0:, :], PS[4][:, :].rearrange("p (h a b) -> p h a b", h=2, b=P)[:, :, k0:, :])\
                    .then_inc(s["att_tpa"], 1)

            act.wait_ge(s["pad_ready"], 1)
            for i in range(N_ATT):
                projected(i, i % 2)
            act.wait_ge(s["att_zero"], 1)
            act.wait_ge(s["proj_dve"], N_ATT)
            act.wait_ge(s["proj_act"], N_ATT)
            for n in range(2):
                queries(n)
                projected(SLOT0 - 1 + n, n)
                values(n, n)
                exps(n, n)
                if n == 1:
                    flipped(0)
            with act.Fori(0, 3) as g:
                for u in range(2):
                    queries(g * 2 + (2 + u))
                    projected(g * 2 + (6 + u), u, g * 2 + (B_BG + u))
                    values(g * 2 + (2 + u), u)
                    exps(g * 2 + (2 + u), u)
                    flipped(g * 2 + (1 + u))
            projected(12, 0)
            flipped(7)
            for i in (13, 14):
                projected(i, i % 2)

            for i in range(4):
                c, h = i // 2, i % 2
                act.wait_ge(s["pool_ps"], c + 1)
                fn(yT[:, c, h * 512:(h + 1) * 512], PS[6 + h][:, :], scale=pc[:, R_PS + c:R_PS + c + 1]).then_inc(s["pool_y"], 1)
                if h == 1:
                    projected(15 + c, 1 - c)
            projected(17, 1)
            projected(18, 0)

            with act.Fori(0, NT // 2) as m:
                def wait(name, per, k):
                    act.wait_ge(s[name], m * per + k)

                wait("w_yT", 1, 1)
                fn(S[:, 0], S[:, 4]).then_inc(s["w_S"], 1)
                wait("w_z", 1, 1)
                fn(lt[0:32, :], z[0:32, B_LORA, :], ACT.Tanh)
                fn(lt[64:128, :], z[64:128, B_LORA, :], ACT.Tanh, scale=0.5).then_inc(s["w_tanh"], 1)
                wait("w_kkr", 1, 1)
                fn(sq, kkr, ACT.Square).then_inc(s["w_sq"], 1)
                wait("w_lora", 3, 1)
                for p in range(2):
                    last = fn(lw[:, p], PS[0][:, p * W2:(p + 1) * W2], ACT.Tanh, scale=0.5, bias=hp[:, p:p + 1])
                last.then_inc(s["w_th"], 1)
                wait("w_lora", 3, 2)
                for p in range(2):
                    last = fn(aa[:, p], PS[1][:, p * W2:(p + 1) * W2], ACT.Tanh, scale=0.5, bias=hp[:, 2 + p:3 + p])
                last.then_inc(s["w_tha"], 1)
                wait("w_lora", 3, 3)
                fn(gg.rearrange("p a t -> p (a t)"), PS[2][:, :]).then_inc(s["w_gg"], 1)
                wait("w_L", 1, 1)
                fn(Pc, Lc, ACT.Exp)
                fn(Pm, Lm, ACT.Exp)
                fn(iP, Lc, ACT.Exp, scale=-1.0).then_inc(s["w_exp"], 1)
                for n in range(2):
                    wait("w_tok", 2, n + 1)
                    fn(both(n), PS[4 * n][:, :]).then_inc(s["w_tka"], 1)
                for n in range(2):
                    wait("w_xp", 10, n + 1)
                    fn(rw[n]["x"], PS[4 * n + 2][:, :].rearrange("p (h t) -> p h t", h=4)).then_inc(s["w_xa"], 1)
                for n in range(2):
                    wait("w_w1p", 2, n + 1)
                    fn(rw[n]["wk"][:, :, 0, :], PS[4 * n][:, 0:256].rearrange("p (h d) -> p h d", h=4)).then_inc(s["w_w1"], 1)
                for l in range(1, 6):
                    for n in range(2):
                        wait("w_t1p", 10, 2 * (l - 1) + n + 1)
                        fn(rw[n]["t1"], PS[4 * n + 3][:, :].rearrange("p (h t) -> p h t", h=4)).then_inc(s["w_t1"], 1)
                    if l < 5:
                        for n in range(2):
                            wait("w_xp", 10, 2 * l + n + 1)
                            fn(rw[n]["x"], PS[4 * n + 3][:, :].rearrange("p (h t) -> p h t", h=4)).then_inc(s["w_xa"], 1)
                for n in range(2):
                    wait("w_uzp", 2, n + 1)
                    fn(rw[n]["uz"].rearrange("p a h d -> p h a d"),
                       PS[4 * n + 1][:, :].rearrange("p (h a d) -> p h a d", h=4, a=2), scale=-1.0).then_inc(s["w_uz"], 1)
                for n in range(2):
                    for c in range(2):
                        wait("w_hp", 4, 2 * n + c + 1)
                        end = n * P + c * CH + CH - 1
                        for p in range(2):
                            last = fn(S[:, 2 * n + c + 1, p, :], PS[4 * n + 3 * c][:, p * HD:(p + 1) * HD],
                                      scale=Pc[:, p, end:end + 1])
                        last.then_inc(s["w_S"], 1)
                wait("w_yc", 1, 1)
                fn(sq, yb, ACT.Square).then_inc(s["w_sq"], 1)

            def modulated(dst, j, count, tr, done, bank=4):
                act.wait_ge(s[tr], count)
                for k in range(4):
                    last = fn(dst[:, k, :], PS[bank][:, k * P:(k + 1) * P], ACT.Identity, scale=s2[:, k:k + 1],
                              bias=mod[:, M_SH2 + k:M_SH2 + k + 1])
                last.then_inc(s[done], 1)

            for j in range(NT):
                act.wait_ge(s["op_x1"], j + 1)
                fn(xn2[:, j % 2], x1[:, j], ACT.Square, accum_out=ss[:, j % 2:j % 2 + 1]).then_inc(s["ss_ready"], 1)
                modulated(h2T, j, j + 1, "op_tp", "op_ta")

            act.wait_ge(s["rt_e1"], 1)
            fn(rt["gb"], rt["ga"], ACT.Exp).then_inc(s["rt_e2"], 1)
            act.wait_ge(s["rt_e1"], 2)
            fn(small["e2"], small["e2"], ACT.Exp).then_inc(s["rt_e2"], 1)

            act.wait_ge(s["rt_n"], 1)
            act.wait_ge(s["rt_ld"], 16)

            def gate(e):
                if isinstance(e, int):
                    return tbl[:, e, 2:3].bitcast(F32)
                return tbl[:, ds(e, 1), 2:3].rearrange("p o f -> p (o f)").bitcast(F32)

            def hidden(e, par, pre="m_", free=True):
                act.wait_ge(s[pre + "gu"], e + 1)
                if free:
                    act.wait_ge(s[pre + "act"], e - 1)
                fn(th[:, par, :], PS[2 + par][:, 0:P], ACT.Tanh, scale=0.5).then_inc(s[pre + "th"], 1)

            def result(e, par, pre="m_", free=None):
                act.wait_ge(s[pre + "dn"], e + 1)
                if free is not None:
                    act.wait_ge(s_sc[par], free)
                fn(yo[:, par, 0:512], PS[4 + 2 * par][:, :], scale=gate(e)).then_inc(s[pre + "ya"], 1)

            act.wait_ge(s["op_ps"], NT)
            modulated(xt[:, 0], 0, 1, "m_tx", "m_xa", 0)
            modulated(xt[:, 1], 1, 2, "m_tx", "m_xa", 0)
            hidden(0, 0, free=False)
            modulated(xt[:, 0], 2, 3, "m_tx", "m_xa", 0)
            hidden(1, 1, free=False)
            result(0, 0)
            modulated(xt[:, 1], 3, 4, "m_tx", "m_xa", 0)
            hidden(2, 0)
            result(1, 1)
            with act.Fori(0, 7) as g:
                for u in range(4):
                    modulated(xt[:, (4 + u) % 2], 0, g * 4 + (5 + u), "m_tx", "m_xa", 0)
                    hidden(g * 4 + (3 + u), (3 + u) % 2)
                    result(g * 4 + (2 + u), u % 2, free=g * 32 + 16 * ((2 + u) // 2))
            hidden(31, 1)
            result(30, 0, free=16 * 15)
            result(31, 1, free=16 * 15)
            n_ov = act.value_load(idy[0:1, 0:1], min_val=1, max_val=OVT)
            with act.Fori(0, n_ov) as i:
                modulated(xt[:, 0], 0, i + (E + 1), "m_tx", "m_xa", 0)
                hidden(i + E, 0, free=False)
                result(i + E, 0)

            for j in range(NT):
                act.wait_ge(s["f_x2"], j + 1)
                if j >= 2:
                    act.wait_ge(s_fo[j % 2], 16 * (j // 2))
                fn(fo[:, j % 2], x1[:, j], ACT.Square, accum_out=ss[:, j % 2:j % 2 + 1]).then_inc(s["ss_ready"], 1)

        @block.vector
        def _(dve):
            ch = Chain(dve, s["chain_dve"])
            tt, ts, stt = dve.tensor_tensor, dve.tensor_scalar, dve.scalar_tensor_tensor

            def flat3(ap):
                return ap.rearrange("p a t -> p (a t)")

            dve.wait_ge(s["ld_c"], 16)
            dve.wait_ge(s["silu_t"], 1)
            ch.step(ts(ct[:, :], ct[:, :], 0.5, 0.5, ALU.mult, ALU.add))
            tt(cc[:, :], cc[:, :], ct[:, :], ALU.mult).then_inc(s["silu_ready"], 1)
            def mean_square(j, phase):
                dve.wait_ge(s["ss_ready"], phase * NT + j + 1)
                ts(ss[:, j % 2:j % 2 + 1], ss[:, j % 2:j % 2 + 1], 1.0 / D, EPS, ALU.mult, ALU.add).then_inc(s["ms_ready"], 1)

            def normed(j):
                mean_square(j, 0)
                dve.wait_ge(s["rstd_ready"], j + 1)
                dve.wait_ge(s_x[j % 2], 16 * (j // 2 + 1))
                ts(xn[:, j % 2], xin[:, j % 2], rs[:, j % 2:j % 2 + 1], None, ALU.mult).then_inc(s["xn_ready"], 1)

            def summed(dst, src, done):
                ch.step(ts(dst, src[:, 0], cc[:, 0:1], None, ALU.mult))
                for k in range(1, KD):
                    last = stt(dst, src[:, k], cc[:, k:k + 1], dst, ALU.mult, ALU.add)
                    if k < KD - 1:
                        ch.step(last)
                last.then_inc(s[done], 1)

            dve.wait_ge(s["silu_ready"], 1)
            for b in range(4):
                dve.wait_ge(s_ada[b], 16)
                summed(acc[:, b], ada[:, b], "acc_ready")
            dve.wait_ge(s["sel_ready"], 1)
            dve.reciprocal(rc16[:, :, :], rc16[:, :, :]).then_inc(s["rt_c"], 1)
            normed(0)
            normed(1)
            dve.wait_ge(s["prm_t"], 1)
            dve.tensor_copy(pc[:, :], PS[7][:, 0:NR]).then_inc(s["prm_ready"], 1)
            dve.wait_ge(s["prm_ready"], 1)
            ch.note(ts(hp[:, 0:4], pc[:, R_W0:R_W0 + 4], 0.5, None, ALU.mult))
            ch.note(ts(hp[:, 4:6], pc[:, R_KA:R_KA + 2], 0.5, None, ALU.mult))
            ch.note(ts(hp[:, 6:8], pc[:, R_KA:R_KA + 2], -0.5, 1.0, ALU.mult, ALU.add))
            for p in range(2):
                ch.note(ts(brk[:, p, :], bones[:, :], pc[:, R_RK + p:R_RK + p + 1], None, ALU.mult))
            dve.wait_ge(s["mod1_ps"], 1)
            ch.step(tt(mod[:, 0:16], PS[6][:, 0:16], pc[:, 0:16], ALU.add))
            stt(s1[:, :], mod[:, M_SC1:M_SC1 + 8], 1.0, pc[:, R_G1:R_G1 + 8], ALU.add, ALU.mult).then_inc(s["mod1_ready"], 1)
            dve.wait_ge(s["mod1_ready"], 1)
            for j in range(NT):
                dve.wait_ge(s["hT_tr"], j + 1)
                for k in range(4, KD):
                    last = ts(hT[:, k, j * P:(j + 1) * P], PS[2 * (j % 2) + 1][:, (k - 4) * P:(k - 3) * P],
                              s1[:, k:k + 1], mod[:, M_SH1 + k:M_SH1 + k + 1], ALU.mult, ALU.add)
                last.then_inc(s["hT_dve"], 1)
                if j + 2 < NT:
                    normed(j + 2)

            def projected(i, par, blk=None):
                dve.wait_ge(s["proj_ps"], i + 1)
                dst = pT[:, ORDER[i], PAD + 512:PAD + 1024] if blk is None else \
                    pT[:, ds(blk, 1), PAD + 512:PAD + 1024].rearrange("p o t -> p (o t)")
                dve.tensor_copy(dst, PS[2 * par + 1][:, :]).then_inc(s["proj_dve"], 1)

            def attended(nb):
                dve.wait_ge(s["att_o"], nb + 1)
                tok = slice(nb * P, nb * P + P) if isinstance(nb, int) else ds(nb * P, P)
                dve.tensor_copy(yT[:, 2:4, tok], PS[7][:, 0:2 * P].rearrange("p (a t) -> p a t", a=2)).then_inc(s["att_y"], 1)

            def softmax(nb, par):
                k0 = 1 if isinstance(nb, int) and nb == 0 else 0
                dve.wait_ge(s["att_qk"], nb + 1)
                for h in range(4):
                    slope = 2.0 ** (-8.0 * (h + 1) / 4)
                    ch.note(stt(sc[:, par, h, k0 * P:], adist[:, k0 * P:], slope,
                                PS[4 + h // 2][:, (h % 2) * 256 + k0 * P:(h % 2 + 1) * 256], ALU.mult, ALU.add))
                ch.wait()
                ch.step(dve.tensor_reduce(mx[:, :], sc[:, par, :, k0 * P:], AX.X, ALU.max))
                ch.step(tt(mx[:, :], mx[:, :], sink[:, :], ALU.max))
                ch.note(tt(es[:, :], sink[:, :], mx[:, :], ALU.subtract))
                ts(nm[:, :], mx[:, :], -1.0, None, ALU.mult).then_inc(s["att_nm"], 1)
                dve.wait_ge(s["att_p"], nb + 1)
                ch.step(tt(rd[:, :], sm[:, :], es[:, :], ALU.add))
                ch.step(dve.reciprocal(rd[:, :], rd[:, :]))
                for h in range(4):
                    last = ts(sc[:, par, h, k0 * P:], sc[:, par, h, k0 * P:], rd[:, h:h + 1], None, ALU.mult)
                last.then_inc(s["att_pn"], 1)

            def flipped(nb):
                k0 = 1 if isinstance(nb, int) and nb == 0 else 0
                dve.wait_ge(s["att_tp"], nb + 1)
                dve.tensor_copy(ptT[:, 2:4, k0:, :], PS[5][:, :].rearrange("p (h a b) -> p h a b", h=2, b=P)[:, :, k0:, :])\
                    .then_inc(s["att_tpd"], 1)

            dve.wait_ge(s["xn_ready"], NT)
            dve.wait_ge(s["hT_tr"], NT)
            dve.memset(ptT[:, :, 0, :], 0.0)
            dve.memset(vt[:, 0, 0, :], 0.0)
            dve.memset(qz, 0.0).then_inc(s["att_zero"], 1)
            dve.wait_ge(s["pad_ready"], 1)
            for i in range(N_ATT):
                projected(i, i % 2)
            dve.wait_ge(s["ld_misc"], 16 * 8)
            dve.wait_ge(s["gtb_ld"], 32)

            def half_blocks(n, loads):
                if not isinstance(n, int) or n >= 1:
                    dve.wait_ge(s["mod2_ps"], n)
                for par in range(2):
                    dve.wait_ge(s_ada[par], loads)
                    summed(acb[:, par], adb[:, par], "acb_ready")

            def gate_columns(n):
                dve.wait_ge(s["mod2_ps"], n + 1)
                dst = gtb[:, n // 6, (n % 2) * 512:(n % 2 + 1) * 512]
                tt(dst, dst, PS[6][:, :], ALU.add).then_inc(s["mod2_ready"], 1)

            def mod_columns(n):
                dve.wait_ge(s["mod2_ps"], n + 1)
                tt(mod[:, ds(n * 4 + 16, 4)], PS[6][:, 0:4], pc[:, ds(n * 4 + 16, 4)], ALU.add).then_inc(s["mod2_ready"], 1)

            half_blocks(0, 32)
            for n in range(2):
                projected(SLOT0 - 1 + n, n)
                softmax(n, n)
                if n == 1:
                    flipped(0)
                gate_columns(n)
                half_blocks(n + 1, 48 + 16 * n)
            with dve.Fori(0, 2) as g:
                ch.enter(g, 2 * (9 + 2 * (KD - 1)))
                for u in range(2):
                    projected(g * 2 + (6 + u), u, g * 2 + (B_BG + u))
                    attended(g * 2 + u)
                    softmax(g * 2 + (2 + u), u)
                    flipped(g * 2 + (1 + u))
                    mod_columns(g * 2 + (2 + u))
                    half_blocks(g * 2 + (3 + u), g * 32 + 16 * (5 + u))
            ch.leave(2)
            for n in (6, 7):
                projected(n + 4, n % 2)
                attended(n - 2)
                softmax(n, n % 2)
                flipped(n - 1)
                gate_columns(n)
                if n == 6:
                    half_blocks(7, 16 * 9)
            projected(12, 0)
            attended(6)
            flipped(7)
            projected(13, 1)
            attended(7)
            for i in range(14, NB):
                projected(i, i % 2)

            dve.wait_ge(s["pool_y"], 4)
            dve.wait_ge(s["conv_y"], 2)
            dve.wait_ge(s["pad_ready"], 2)
            dve.wait_ge(s["att_y"], NT)
            dve.wait_ge(s["proj_act"], NB)
            dve.wait_ge(s["proj_dve"], NB)
            dve.memset(ct[:, :], 0.0).then_inc(s["w_yT"], 1)
            with dve.Fori(0, NT // 2) as m:
                ch.enter(m, 18)

                def wait(name, per, k):
                    dve.wait_ge(s[name], m * per + k)

                wait("w_yT", 1, 1)
                wait("w_df", 1, 1)
                for b in range(ZB):
                    last = stt(z[:, b, :], df[:, b, :], pc[:, R_MU + b:R_MU + b + 1],
                               pT[:, b, ds(m * W2 + PAD, W2)], ALU.mult, ALU.add)
                last.then_inc(s["w_z"], 1)
                wait("w_z", 1, 1)
                for p in range(2):
                    last = ts(kkr[:, p], z[:, B_K + p, :], pc[:, R_KK + p:R_KK + p + 1], None, ALU.mult)
                last.then_inc(s["w_kkr"], 1)
                wait("w_tanh", 1, 1)
                ts(lt[64:128, :], lt[64:128, :], 0.5, 0.5, ALU.mult, ALU.add).then_inc(s["w_sg"], 1)
                wait("w_ss", 2, 1)
                ts(nrm[:, :], PS[3][:, 0:8], 1e-24, None, ALU.max).then_inc(s["w_nrm"], 1)
                wait("w_th", 1, 1)
                c = -0.5 * float(np.exp(-0.5))
                ch.step(ts(lw, lw, 1.0, c, ALU.add, ALU.mult))
                ch.step(dve.tensor_tensor_scan(flat3(Lc), rmask[:, :], flat3(lw), 0.0, ALU.mult, ALU.add))
                tt(Lm, Lc, lw, ALU.subtract).then_inc(s["w_L"], 1)
                wait("w_nrt", 2, 1)
                dve.tensor_copy(nrT[:, :], PS[3][0:8, P:2 * P]).then_inc(s["w_nrT"], 1)
                wait("w_tha", 1, 1)
                for p in range(2):
                    ch.note(ts(rk[:, p], aa[:, p], hp[:, 4 + p:5 + p], hp[:, 6 + p:7 + p], ALU.mult, ALU.add))
                ch.wait()
                ch.note(tt(z[:, B_K:B_K + 2, :], z[:, B_K:B_K + 2, :], rk, ALU.mult))
                ch.step(ts(aa, aa, 0.5, 0.5, ALU.mult, ALU.add))
                wait("w_nrb", 2, 1)
                ch.step(tt(flat3(kkr), flat3(kkr), PS[4][:, :], ALU.mult))
                wait("w_exp", 1, 1)
                ch.note(tt(KR[:, :, 0, :], kkr, Pm, ALU.mult))
                ch.note(tt(KR[:, :, 1, :], z[:, B_R:B_R + 2, :], Pc, ALU.mult))
                ch.note(tt(Kt, z[:, B_K:B_K + 2, :], iP, ALU.mult))
                ch.note(tt(rk, z[:, B_R:B_R + 2, :], z[:, B_K:B_K + 2, :], ALU.mult))
                ch.step(tt(aa, kkr, aa, ALU.mult))
                tt(Bt, aa, iP, ALU.mult).then_inc(s["w_ops"], 1)
                for n in range(2):
                    t = rw[n]
                    wait("w_tok", 2, n + 1)
                    ch.note(dve.tensor_copy(t["vt"], PS[4 * n + 1][:, 0:256].rearrange("p (h d) -> p h d", h=4)))
                    dve.tensor_copy(t["wk"][:, :, 1, :], PS[4 * n + 1][:, 256:512].rearrange("p (h d) -> p h d", h=4))\
                        .then_inc(s["w_tkd"], 1)
                    wait("w_abp", 2, n + 1)
                    for q in range(2):
                        last = tt(t["ab"][:, q::2].rearrange("p h a t -> p h (a t)"),
                                  PS[4 * n + 2 + q][:, :].rearrange("p (h x) -> p h x", h=2),
                                  mskb(), ALU.mult)
                    last.then_inc(s["w_ab"], 1)
                for n in range(2):
                    wait("w_bl", 12, n + 1)
                    tt(rw[n]["xt"], ident[:, :].unsqueeze(1).to_broadcast([P, 4, P]), rw[n]["bl"], ALU.subtract)\
                        .then_inc(s["w_xt"], 1)
                for n in range(2):
                    wait("w_akp", 2, n + 1)
                    for q in range(2):
                        last = tt(rw[n]["ak"][:, q::2].rearrange("p h a t -> p h (a t)"),
                                  PS[4 * n + q][:, :].rearrange("p (h x) -> p h x", h=2), mskb(), ALU.mult)
                    last.then_inc(s["w_ak"], 1)
                for l in range(1, 6):
                    for n in range(2):
                        wait("w_x2p", 10, 2 * (l - 1) + n + 1)
                        tt(rw[n]["xt"], rw[n]["xt"], PS[4 * n + 2][:, :].rearrange("p (h t) -> p h t", h=4), ALU.subtract)\
                            .then_inc(s["w_xt"], 1)
                for n in range(2):
                    wait("w_rep", 2, n + 1)
                    tt(rw[n]["re"], PS[4 * n + 3][:, 0:256].rearrange("p (a t) -> p a t", a=2),
                       KR[:, :, 1, n * P:(n + 1) * P], ALU.add).then_inc(s["w_re"], 1)
                    wait("w_gp", 2, n + 1)
                    for c in range(2):
                        for h in range(2):
                            r = slice(64 * h, 64 * h + 64)
                            last = tt(G[r, 4 * n + 2 * c:4 * n + 2 * c + 2, r],
                                      PS[4 * n + 2 - c][r, 0:128].rearrange("p (q d) -> p q d", q=2),
                                      ident[r, r].unsqueeze(1).to_broadcast([64, 2, 64]), ALU.add)
                    last.then_inc(s["w_G"], 1)
                for n in range(2):
                    wait("w_yp", 2, n + 1)
                    dve.tensor_copy(yb[:, :, n * P:(n + 1) * P], PS[4 * n + 1][:, 0:256].rearrange("p (a t) -> p a t", a=2))\
                        .then_inc(s["w_y"], 1)
                wait("w_mean", 1, 1)
                stt(flat3(yb), PS[2][:, :], -1.0 / HD, flat3(yb), ALU.mult, ALU.add).then_inc(s["w_yc"], 1)
                wait("w_bonp", 1, 1)
                ch.note(tt(flat3(Lm), PS[5][:, :], flat3(z[:, B_V:B_V + 2, :]), ALU.mult))
                wait("w_ss", 2, 2)
                ts(nrm[:, :], PS[3][:, 0:8], 1.0 / HD, GN_EPS, ALU.mult, ALU.add).then_inc(s["w_nrm"], 1)
                wait("w_nrt", 2, 2)
                dve.tensor_copy(nrT[:, :], PS[3][0:8, P:2 * P]).then_inc(s["w_nrT"], 1)
                wait("w_nrb", 2, 2)
                ch.step(tt(flat3(yb), flat3(yb), PS[4][:, :], ALU.mult))
                for p in range(2):
                    last = ts(yb[:, p], yb[:, p], pc[:, R_LNG + p:R_LNG + p + 1], pc[:, R_LNB + p:R_LNB + p + 1], ALU.mult, ALU.add)
                ch.step(last)
                ch.step(tt(yb, yb, Lm, ALU.add))
                tt(yT[:, 6:8, ds(m * W2, W2)], yb, gg, ALU.mult).then_inc(s["w_yT"], 1)
            ch.leave(NT // 2)

            dve.wait_ge(s["mod2_ready"], 8)
            ch.step(stt(s2[:, :], mod[:, M_SC2:M_SC2 + 8], 1.0, pc[:, R_G2:R_G2 + 8], ALU.add, ALU.mult))

            dve.wait_ge(s["xr_ld"], 16 * NT)

            def modulated(dst, count, tr, done, bank=5):
                dve.wait_ge(s[tr], count)
                for k in range(4, KD):
                    last = ts(dst[:, k, :], PS[bank][:, (k - 4) * P:(k - 3) * P], s2[:, k:k + 1],
                              mod[:, M_SH2 + k:M_SH2 + k + 1], ALU.mult, ALU.add)
                last.then_inc(s[done], 1)

            for j in range(NT):
                dve.wait_ge(s["op_ps"], j + 1)
                if j >= 2:
                    dve.wait_ge(s_st[j % 2], 16 * (j // 2))
                for h in range(2):
                    ch.note(tt(xn2[:, j % 2, h * 512:(h + 1) * 512], PS[2 * (j % 2) + h][:, :], gtb[:, 0, h * 512:(h + 1) * 512],
                               ALU.mult))
                ch.wait()
                tt(x1[:, j], x1[:, j], xn2[:, j % 2], ALU.add).then_inc(s["op_x1"], 1)
                mean_square(j, 1)
                dve.wait_ge(s["rstd_ready"], NT + j + 1)
                ts(xn2[:, j % 2], x1[:, j], rs[:, j % 2:j % 2 + 1], None, ALU.mult).then_inc(s["op_xn"], 1)
                modulated(h2T, j + 1, "op_tp", "op_td")
                dve.wait_ge(s["op_lg"], j + 1)
                tt(lg[:, j], PS[6][:, 0:GROUPS + E], rbias[:, :], ALU.add).then_inc(s["op_lgd"], 1)
            dve.wait_ge(s["op_lgd"], NT)

            q = small

            def b3(ap, n):
                return ap.unsqueeze(2).to_broadcast([P, NT, n])

            def row3(ap, n):
                return ap.unsqueeze(1).to_broadcast([P, NT, n])

            L = lg[:, :, 0:GROUPS]
            X = lg[:, :, GROUPS:]

            def pick(vals, n, top, where, hot):
                ch.step(dve.tensor_reduce(top, vals, AX.X, ALU.max))
                key = rt["ky"][:, :, 0:n]
                ch.step(tt(key, vals, b3(top, n), ALU.is_ge))
                ch.step(ts(key, key, -64.0, 64.0, ALU.mult, ALU.add))
                ch.step(tt(key, key, row3(rt["i32"][:, 0:n], n), ALU.add))
                ch.step(dve.tensor_reduce(where, key, AX.X, ALU.min))
                ch.step(tt(hot, row3(rt["i32"][:, 0:n], n), b3(where, n), ALU.is_equal))

            ch.step(dve.tensor_tensor_scan(rt["i32"], ones[:, 0:E], ones[:, 0:E], -1.0, ALU.mult, ALU.add))
            ch.step(ts(rt["thr"], rt["i32"][:, 0:OVT], float(CAP), float(CAP), ALU.mult, ALU.add))
            pick(L, GROUPS, q["gm"], q["gi"], rt["goh"])
            tt(rt["ga"], L, b3(q["gm"], GROUPS), ALU.subtract).then_inc(s["rt_e1"], 1)
            ch.step(ts(rt["goh"], rt["goh"], 1.0, -NEG, ALU.subtract, ALU.mult))
            for e in range(GROUPS):
                ch.note(tt(rt["xm"][:, :, e * EPG:(e + 1) * EPG], X[:, :, e * EPG:(e + 1) * EPG],
                           rt["goh"][:, :, e:e + 1].to_broadcast([P, NT, EPG]), ALU.add))
            ch.wait()
            pick(rt["xm"], E, q["m1"], q["i1"], rt["oh1"])
            ch.step(ts(rt["tmp"], rt["oh1"], 10 * NEG, None, ALU.mult))
            ch.step(tt(rt["xm"], rt["xm"], rt["tmp"], ALU.add))
            pick(rt["xm"], E, q["m2"], q["i2"], rt["oh2"])
            tt(q["e2"], q["m2"], q["m1"], ALU.subtract).then_inc(s["rt_e1"], 1)
            tt(rt["tmp"], rt["oh1"], rt["oh2"], ALU.add).then_inc(s["rt_oh"], 1)
            dve.wait_ge(s["rt_e2"], 1)
            ch.step(dve.tensor_reduce(q["gp"], rt["gb"], AX.X, ALU.add))
            dve.wait_ge(s["rt_e2"], 2)
            ch.step(ts(q["g1"], q["e2"], 1.0, None, ALU.add))
            ch.step(tt(q["g1"], q["g1"], q["gp"], ALU.mult))
            ch.step(dve.reciprocal(q["g1"], q["g1"]))
            ch.step(tt(q["g2"], q["g1"], q["e2"], ALU.mult))
            dve.wait_ge(s["rt_pos"], 1)
            ch.step(dve.memset(rt["pre"][:, 0], 0.0))
            for j in range(NT):
                ch.step(tt(rt["pre"][:, j + 1], rt["pre"][:, j], PS[7][:, 256 + j * E:256 + (j + 1) * E], ALU.add))
            ch.step(tt(rt["pos"], PS[7][:, 0:256].rearrange("p (j e) -> p j e", e=E), rt["pre"][:, 0:NT], ALU.add))
            n_e = rt["pre"][:, NT]
            cmp = rt["cmp"].rearrange("p (e i) -> p e i", i=OVT)
            ch.step(tt(cmp, n_e.unsqueeze(2).to_broadcast([P, E, OVT]), rt["thr"].unsqueeze(1).to_broadcast([P, E, OVT]), ALU.is_gt))
            ch.step(dve.tensor_reduce(rt["nov"], cmp, AX.X, ALU.add))
            ch.step(dve.tensor_tensor_scan(rt["ci"], ones[:, 0:E], rt["nov"], 0.0, ALU.mult, ALU.add))
            ch.note(tt(rt["ob"], rt["ci"], rt["nov"], ALU.subtract))
            cm2 = rt["cmp"].rearrange("p (i e) -> p i e", e=E)
            ch.step(tt(cm2, rt["ci"].unsqueeze(1).to_broadcast([P, OVT, E]),
                       rt["i32"][:, 0:OVT].unsqueeze(2).to_broadcast([P, OVT, E]), ALU.is_le))
            ch.step(dve.tensor_reduce(rt["thr"], cm2, AX.X, ALU.add))
            ch.note(ts(eidt[:, :], rt["thr"], float(E - 1), None, ALU.min))
            ts(idy[:, 0:1], rt["ci"][:, E - 1:E], 1.0, None, ALU.max).then_inc(s["rt_n"], 1)
            for n in range(2):
                hot, where, g_ = (rt["oh1"], q["i1"], q["g1"]) if n == 0 else (rt["oh2"], q["i2"], q["g2"])
                qq, bb, c_ = (q["q1"], q["b1"], q["c1"]) if n == 0 else (q["q2"], q["b2"], q["c2"])
                ch.step(tt(rt["tmp"], hot, rt["pos"], ALU.mult))
                ch.step(dve.tensor_reduce(qq, rt["tmp"], AX.X, ALU.add))
                ch.step(tt(rt["tmp"], hot, row3(rt["ob"], E), ALU.mult))
                ch.step(dve.tensor_reduce(bb, rt["tmp"], AX.X, ALU.add))
                ch.step(tt(bb, bb, where, ALU.subtract))
                ch.step(ts(bb, bb, float(CAP), float(CAP * (E - 1)), ALU.mult, ALU.add))
                ch.step(ts(c_, qq, float(CAP), None, ALU.is_ge))
                ch.step(tt(bb, bb, c_, ALU.mult))
                ch.step(tt(bb, bb, qq, ALU.add))
                ch.step(ts(c_, where, float(CAP), None, ALU.mult))
                ch.note(tt(slot[:, n * NT:(n + 1) * NT], bb, c_, ALU.add))
                ch.note(dve.tensor_copy(ent[:, n * NT:(n + 1) * NT, 2].bitcast(F32), g_))
            ch.wait()
            dve.memset(ct[:, :], 0.0).then_inc(s["rt_ent"], 1)

            dve.wait_ge(s["rt_n"], 1)
            dve.wait_ge(s["rt_ld"], 16)

            def gate(e):
                if isinstance(e, int):
                    return tbl[:, e, 2:3].bitcast(F32)
                return tbl[:, ds(e, 1), 2:3].rearrange("p o f -> p (o f)").bitcast(F32)

            def hidden(e, par, pre="m_", free=True):
                dve.wait_ge(s[pre + "th"], e + 1)
                ch.step(stt(a1[:, par, :], th[:, par, :], 1.0, PS[2 + par][:, 0:P], ALU.add, ALU.mult))
                if free:
                    dve.wait_ge(s[pre + "dn"], e - 1)
                stt(ac[:, par, :], a1[:, par, :], 0.5, PS[2 + par][:, P:2 * P], ALU.mult, ALU.mult).then_inc(s[pre + "act"], 1)

            def result(e, par, pre="m_", free=None):
                dve.wait_ge(s[pre + "dn"], e + 1)
                if free is not None:
                    dve.wait_ge(s_sc[par], free)
                ts(yo[:, par, 512:], PS[5 + 2 * par][:, :], gate(e), None, ALU.mult).then_inc(s[pre + "yd"], 1)

            modulated(xt[:, 0], 1, "m_tx", "m_xd", 1)
            modulated(xt[:, 1], 2, "m_tx", "m_xd", 1)
            hidden(0, 0, free=False)
            modulated(xt[:, 0], 3, "m_tx", "m_xd", 1)
            hidden(1, 1, free=False)
            result(0, 0)
            modulated(xt[:, 1], 4, "m_tx", "m_xd", 1)
            hidden(2, 0)
            result(1, 1)
            with dve.Fori(0, 7) as g:
                ch.enter(g, 4)
                for u in range(4):
                    modulated(xt[:, (4 + u) % 2], g * 4 + (5 + u), "m_tx", "m_xd", 1)
                    hidden(g * 4 + (3 + u), (3 + u) % 2)
                    result(g * 4 + (2 + u), u % 2, free=g * 32 + 16 * ((2 + u) // 2))
            ch.leave(7)
            hidden(31, 1)
            result(30, 0, free=16 * 15)
            result(31, 1, free=16 * 15)
            n_ov = dve.value_load(idy[0:1, 0:1], min_val=1, max_val=OVT)
            with dve.Fori(0, n_ov) as i:
                ch.enter(i, 1)
                modulated(xt[:, 0], i + (E + 1), "m_tx", "m_xd", 1)
                hidden(i + E, 0, free=False)
                result(i + E, 0)

            dve.wait_ge(s["ld_fg"], 16)
            for j in range(NT):
                dve.wait_ge(s_fy[j % 2], 32 * (j // 2 + 1))
                a_, b_ = yab[:, j % 2, 0], yab[:, j % 2, 1]
                tt(a_, a_, b_, ALU.add).then_inc(s["f_c"], 1)
                dve.wait_ge(s["f_c"], 2 * j + 1)
                tt(a_, a_, gtb[:, 1], ALU.mult).then_inc(s["f_c"], 1)
                dve.wait_ge(s["f_c"], 2 * j + 2)
                tt(x1[:, j], x1[:, j], a_, ALU.add).then_inc(s["f_x2"], 1)
                mean_square(j, 2)
                dve.wait_ge(s["rstd_ready"], 2 * NT + j + 1)
                stt(fo[:, j % 2], x1[:, j], rs[:, j % 2:j % 2 + 1], fg, ALU.mult, ALU.mult).then_inc(s["f_o"], 1)


_INS = ["x", "c", "w_ada", "b_ada", "norm1_g", "norm2_g", "w_in", "w_out", "pool_w", "pool_scale", "attn_sinks", "conv_w",
        "rwkv_mu", "rwkv_w0", "rwkv_w2", "rwkv_a0", "rwkv_a2", "rwkv_g2", "rwkv_k_k", "rwkv_k_a", "rwkv_r_k", "rwkv_ln_g",
        "rwkv_ln_b", "moe_w_grp", "moe_b_grp", "moe_w_exp", "moe_b_exp", "moe_w_gate", "moe_w_up", "moe_w_down", "final_g"]


def kernel(**inputs):
    import numpy as _np
    import concourse.bacc as _bacc
    from concourse import mybir as _mybir
    from concourse.bass_utils import run_bass_kernel_spmd as _run

    nc = _bacc.Bacc("TRN2", target_bir_lowering=False, num_devices=1)
    arrays, args = {}, {}
    for name in _INS:
        a = _np.ascontiguousarray(inputs[name])
        arrays[f"in_{name}"] = a
        args[name] = nc.dram_tensor(f"in_{name}", a.shape, _mybir.dt.from_np(a.dtype), kind="ExternalInput").ap()
    out = nc.dram_tensor("out_dram", (1, T, D), F32, kind="ExternalOutput").ap()
    build(nc, args, out)
    r = _run(nc, [arrays], core_ids=[0])
    return r.results[0]["out_dram"]
```

```python
from contextlib import ExitStack

import numpy as np

import concourse.bass as bass
from concourse import mybir

F32 = mybir.dt.float32
I32 = mybir.dt.int32
U32 = mybir.dt.uint32
ALU = mybir.AluOpType
ACT = mybir.ActivationFunctionType
AX = mybir.AxisListType
ds = bass.ds

P = 128
D = 1024
T = 1024
KD = D // P
NT = T // P
HD = 64
CH = 64
PAD = 16
TW = T + PAD
EPS = 1e-6
GN_EPS = 64e-5
E = 32
GROUPS = 4
EPG = E // GROUPS
FE = 128
CAP = P
OVT = (2 * T - 1) // CAP
TILES = E + OVT
OOB = 1 << 20
NEG = -1e30

B_R, B_K, B_V, B_LORA, B_POOL, B_Q, B_KEY, B_VAL, B_BG, B_CG, B_XI = 0, 2, 4, 6, 7, 9, 11, 12, 13, 15, 17
NB = 19
ORDER = [B_Q, B_Q + 1, B_KEY, B_VAL, B_POOL, B_POOL + 1, *range(B_BG, NB), *range(B_R, B_POOL)]
N_ATT, N_POOL, N_CONV = 4, 6, 12
SLOT0 = 5
COL_POOL, COL_ATT, COL_CONV, COL_RWKV = 0, 256, 768, 1536
ZB = 7

R_ADA, R_G1, R_G2, R_MU, R_W0, R_A0, R_KK, R_KA, R_RK, R_LNG, R_LNB, R_PS, R_CW, NR = \
    0, 48, 56, 64, 71, 73, 75, 77, 79, 81, 83, 85, 87, 93
M_SH1, M_SC1, M_GT1, M_SH2, M_SC2, M_GT2 = 0, 8, 16, 24, 32, 40


TURNS = NT // 2


def front_counts(m):
    if m is None:
        return (lambda per, k: k), 1
    return (lambda per, k: m * per + (per + k)), m * 2 + 2


def tail_norm(m):
    return 2 * TURNS if isinstance(m, int) else m * 2 + 3


class Chain:

    def __init__(self, eng, sem):
        self.eng, self.sem, self.base, self.n, self.loop = eng, sem, 0, 0, None

    def at(self):
        return self.base + self.n if self.loop is None else self.loop[0] * self.loop[1] + (self.base + self.n)

    def note(self, ins):
        ins.then_inc(self.sem, 1)
        self.n += 1

    def wait(self):
        self.eng.wait_ge(self.sem, self.at())

    def step(self, ins):
        self.note(ins)
        self.wait()

    def enter(self, reg, per):
        self.base, self.n, self.loop = self.base + self.n, 0, (reg, per)

    def leave(self, turns):
        per = self.loop[1]
        assert self.n == per, (self.n, per)
        self.base, self.n, self.loop = self.base + per * turns, 0, None


def build(nc, w, out):
    ctx = ExitStack()
    with ctx:
        def sb(name, shape, dt=F32):
            return ctx.enter_context(nc.sbuf_tensor(name, shape, dt))

        def sem(name):
            return ctx.enter_context(nc.semaphore(name))

        PS = [ctx.enter_context(nc.psum_tensor(f"bank{i}", [P, 512], F32)) for i in range(8)]

        xn2_d = nc.dram_tensor("xn2_d", [T, D], F32, kind="Internal")
        y_d = nc.dram_tensor("y_d", [2 * T, D], F32, kind="Internal")

        REG_P = sb("REG_P", [P, NB * TW])
        REG_W = sb("REG_W", [P, 15360])
        REG_Y = sb("REG_Y", [P, 8192])

        def area(reg, at, *shape):
            n = int(np.prod(shape))
            v = reg[:, at:at + n]
            names = "abcd"[:len(shape)]
            if len(shape) > 1:
                v = v.rearrange(f"p ({' '.join(names)}) -> p {' '.join(names)}", **dict(zip(names, shape)))
            return v, at + n

        pT = REG_P[:, :].rearrange("p (b t) -> p b t", b=NB)
        hT, o = area(REG_W, 0, KD, T)
        A_ATT = o
        xin, o = area(REG_W, o, 2, D)
        xn, o = area(REG_W, o, 2, D)
        A_WIN = 15360 - 2 * KD * P
        win, _ = area(REG_W, A_WIN, 2, KD, P)
        ada, _ = area(REG_P, 0, 4, KD, 512)
        yT = REG_Y[:, :].rearrange("p (k t) -> p k t", k=KD)
        qz, o = area(REG_W, A_ATT, 4, P)
        vs, o = area(REG_W, o, 2 * P)
        vt, o = area(REG_W, o, 2, 2, P)
        sc, o = area(REG_W, o, 2, 4, 2 * P)
        assert o <= A_WIN
        ptT, _ = area(REG_Y, 7 * T, 4, 2, P)
        pm1, o = area(REG_Y, 4 * T, TW)
        pm2, o = area(REG_Y, o, TW)
        acb, o = area(REG_Y, o, 2, 256)
        assert o <= 7 * T
        adb, _ = area(REG_P, 0, 2, KD, 256)
        acc, _ = area(REG_Y, 0, 4, 512)
        pmd = yT[:, 0:2, :]
        W2 = 2 * P
        z, o = area(REG_W, 0, ZB, W2)
        df, o = area(REG_W, o, ZB, W2)
        lw, o = area(REG_W, o, 2, W2)
        Lc, o = area(REG_W, o, 2, W2)
        Lm, o = area(REG_W, o, 2, W2)
        Pc, o = area(REG_W, o, 2, W2)
        Pm = Lm
        iP = Lc
        aa, o = area(REG_W, o, 2, W2)
        gg, o = area(REG_W, o, 2, W2)
        kkr, o = area(REG_W, o, 2, W2)
        rk, o = area(REG_W, o, 2, W2)
        yb, o = area(REG_W, o, 2, W2)
        KR, o = area(REG_W, o, 2, 2, W2)
        lt, o = area(REG_W, o, W2)
        ggn, o = area(REG_W, o, 2, W2)
        zv, o = area(REG_W, o, 2, W2)
        bon, o = area(REG_W, o, 2, W2)
        pend, o = area(REG_W, o, 2, 4)
        Bt, _ = area(df.rearrange("p a b -> p (a b)"), 0, 2, W2)
        Kt, _ = area(df.rearrange("p a b -> p (a b)"), 2 * W2, 2, W2)
        sq, _ = area(df.rearrange("p a b -> p (a b)"), 4 * W2, 2, W2)
        rw, rw_at = [], []
        for n in range(2):
            reg, o = (REG_P, TW * 7) if n == 0 else (REG_P, o)
            t = {}
            rw_at.append(o)
            for name, shape in (("bt", (4, HD)), ("kt", (4, HD)), ("vt", (4, HD)), ("wk", (4, 2, HD)), ("uz", (2, 4, HD)),
                                ("ab", (4, 2, P)), ("ak", (4, 2, P)), ("x", (4, P)), ("xt", (4, P)), ("t1", (4, P)),
                                ("bl", (4, P)), ("re", (2, P))):
                t[name], o = area(reg, o, *shape)
            rw.append(t)
        assert o <= NB * TW
        wo, o = area(REG_P, 0, KD, D)
        x1, o = area(REG_P, o, NT, D)
        xn2, o = area(REG_P, o, 2, D)
        h2T, o = area(REG_P, o, KD, P)
        wg, o = area(REG_W, 0, 4, KD, FE)
        wu, o = area(REG_W, o, 4, KD, FE)
        wd, o = area(REG_W, o, 4, D)
        xg, o = area(REG_Y, 0, 2, D)
        xt, o = area(REG_Y, o, 2, KD, P)
        yo, o = area(REG_Y, o, 2, D)
        th, o = area(REG_Y, o, 2, P)
        a1, o = area(REG_Y, o, 2, P)
        ac, o = area(REG_Y, o, 2, P)
        fg, o = area(REG_Y, o, D)
        lanes, o = area(REG_Y, 2 * D, 2 * NT, CAP)
        hots, o = area(REG_Y, o, 2 * NT, 3, TILES)
        i128, o = area(REG_Y, o, CAP)
        tab, o = area(REG_Y, o, 2, TILES)
        tif, o = area(REG_Y, o, 2, 2 * NT)
        tii, o = area(REG_Y, o, 2, 2 * NT)
        tii = tii.bitcast(I32)
        rowf, o = area(REG_Y, o, 2 * NT)
        gatef, o = area(REG_Y, o, 2 * NT)
        assert o <= 8192 - D
        disti, _ = area(REG_W, 0, 2 * P)
        disti = disti.bitcast(I32)
        o = 4 * (2 * KD * FE + D)
        rt = {}
        for name, shape in (("ga", (NT, GROUPS)), ("gb", (NT, GROUPS)), ("goh", (NT, GROUPS)), ("xm", (NT, E)), ("ky", (NT, E)),
                            ("oh1", (NT, E)), ("oh2", (NT, E)), ("pos", (NT, E)), ("pre", (NT + 1, E)), ("tmp", (NT, E)),
                            ("cmp", (E * OVT,)), ("i32", (E,)), ("thr", (OVT,)), ("nov", (E,)), ("ci", (E,)), ("ob", (E,))):
            rt[name], o = area(REG_W, o, *shape)
        small = {}
        for name in ("gm", "gi", "gp", "m1", "i1", "m2", "i2", "e2", "q1", "q2", "b1", "b2", "c1", "c2", "g1", "g2"):
            small[name], o = area(REG_W, o, NT)
        assert o <= 15360
        yab, o = area(REG_W, 0, 4, 2, D)
        fo, _ = area(REG_W, o, 2, D)

        ident = sb("ident", [P, P])
        bones = sb("bones", [P, P])
        tri = sb("tri", [P, P])
        ones = sb("ones", [P, P])
        msk = sb("msk", [P, 2, P])
        lmask = sb("lmask", [P, 6, P])
        adist = sb("adist", [P, 2 * P])
        sel = sb("sel", [8, 4, P])
        rmask = sb("rmask", [P, 512])
        rc16 = sb("rc16", [P, 2, PAD])
        cnti = sb("cnti", [P, PAD], I32)
        mhalf = sb("mhalf", [P, 8])
        prow = sb("prow", [NR, P])
        pc = sb("pc", [P, NR])
        pw = sb("pw", [P, 2, P])
        lor = sb("lor", [P, 256])
        wr = sb("wr", [P, KD, GROUPS + E])
        rbias = sb("rbias", [P, GROUPS + E])
        sink = sb("sink", [P, 4])
        cc = sb("cc", [P, KD])
        ct = sb("ct", [P, KD])
        mod = sb("mod", [P, 48])
        s1 = sb("s1", [P, KD])
        s2 = sb("s2", [P, KD])
        hp = sb("hp", [P, 8])
        brk = sb("brk", [P, 2, P])
        gtb = sb("gtb", [P, 2, D])
        ss = sb("ss", [P, 2])
        rs = sb("rs", [P, 2])
        mx = sb("mx", [P, 4])
        nm = sb("nm", [P, 4])
        es = sb("es", [P, 4])
        sm = sb("sm", [P, 4])
        rd = sb("rd", [P, 4])
        nrm = sb("nrm", [P, 8])
        nrp = sb("nrp", [P, 8])
        nrT = sb("nrT", [8, P])
        S = sb("S", [P, 5, 2, HD])
        G = sb("G", [P, 8, P])
        lg = sb("lg", [P, NT, GROUPS + E])
        tbl = sb("tbl", [P, TILES + 1, 4], I32)
        idx = sb("idx", [P, 4], I32)
        idy = sb("idy", [P, 4], I32)
        junk = sb("junk", [P, 1])

        eidt = sb("eidt", [P, OVT], I32)
        out_row = sb("out_row", [P, 2 * NT], I32)
        slot = sb("slot", [P, 2 * NT], I32)

        def eid_view(i):
            return eidt[0:1, ds(i, 1)]

        def both(n):
            at = rw_at[n]
            return REG_P[:, at:at + 512]

        def mskb():
            return msk[:, :, :].rearrange("p a t -> p (a t)").unsqueeze(1).to_broadcast([P, 2, 2 * P])

        v = {n: w[n] for n in w}
        xd = v["x"].rearrange("b t d -> (b t) d")
        outd = out.rearrange("b t d -> (b t) d")

        names = ("ld_c ld_prm ld_misc ld_wr const_ready sel_ready chain_pool chain_dve  "
                 "prm_t prm_ready silu_t silu_ready mod1_ps mod1_ready mod2_ps mod2_ready "
                 "ss_ready ms_ready rstd_ready xn_ready hT_tr hT_act hT_dve "
                 "proj_ps proj_act proj_dve pad_ready acc_ready acb_ready gtb_ld "
                 "att_q att_qk att_vps att_v  att_nm att_p att_pn att_tp att_tpa att_tpd att_o att_y "
                 "pool_d pool_ps pool_y conv_y  "
                 "w_df w_z w_tanh w_lora w_th w_tha w_sg  w_gg w_L w_exp w_kkr w_sq w_ss w_nrm w_nrp w_nrt w_nrT w_nrb "
                 "w_ops w_tok w_tka w_tkd w_abp w_ab w_akp w_ak w_bl w_xt w_xp w_xa w_t1p w_t1 w_x2p w_w1p w_w1 w_uzp w_uz "
                 "w_gp w_G w_rep w_re w_hp w_S w_yp w_y w_mean w_yc w_bonp  w_yT w_cp "
                 "wo_ld xr_ld op_ps op_x1 op_xn op_tp op_ta op_td op_lg op_lgd "
                 "rt_pos  rt_hot rt_tab rt_ld rt_n "
                 " m_tx m_xa m_xd m_gu m_th m_act m_dn m_ya m_yd "
                 "ov_w ov_g ov_sc "
                 "rt_c rt_e1 rt_e2 rt_oh ld_fg f_go ov_go f_c att_zero f_x2 f_o f_a").split()
        s = {n: sem(n) for n in names}
        s_ada = [sem(f"ld_ada{i}") for i in range(4)]
        s_x = [sem(f"ld_x{i}") for i in range(2)]
        s_win = [sem(f"ld_win{i}") for i in range(2)]
        s_w = [sem(f"ld_expert{i}") for i in range(4)]
        s_gx = [sem(f"gathered{i}") for i in range(2)]
        s_sc = [sem(f"scattered{i}") for i in range(2)]
        s_st = [sem(f"st_xn2_{i}") for i in range(2)]
        s_fo = [sem(f"st_out{i}") for i in range(2)]
        block = ctx.enter_context(nc.Block())

        ada_v = v["w_ada"].rearrange("l (p k) n -> (l p) k n", k=KD)
        win_v = v["w_in"].rearrange("l (k p) n -> (l p) k n", p=P)
        wo_v = v["w_out"].rearrange("l (k p) n -> (l p) k n", p=P)
        wg_v = v["moe_w_gate"].rearrange("l e (k p) f -> p (l e) k f", p=P)
        wu_v = v["moe_w_up"].rearrange("l e (k p) f -> p (l e) k f", p=P)
        wd_v = v["moe_w_down"].rearrange("l e f d -> f (l e) d")

        @block.sync
        def _(sp):
            def row(n, r, k):
                return sp.dma_start(prow[r:r + k, :], v[n])

            sp.dma_start(cc[:, :], v["c"].rearrange("b (p k) -> (b p) k", k=KD)).then_inc(s["ld_c"], 16)

            def load_ada(b):
                sp.dma_start(ada[:, b], ada_v[:, :, b * 512:(b + 1) * 512]).then_inc(s_ada[b], 16)

            def load_x(j):
                sp.dma_start(xin[:, j % 2], xd[j * P:(j + 1) * P, :]).then_inc(s_x[j % 2], 16)

            load_x(0)
            load_ada(0)
            load_x(1)
            load_ada(1)
            rows = [("b_ada", R_ADA, 48), ("norm1_g", R_G1, 8), ("norm2_g", R_G2, 8), ("rwkv_mu", R_MU, 7),
                    ("rwkv_w0", R_W0, 2), ("rwkv_a0", R_A0, 2), ("rwkv_k_k", R_KK, 2), ("rwkv_k_a", R_KA, 2),
                    ("rwkv_r_k", R_RK, 2), ("rwkv_ln_g", R_LNG, 2), ("rwkv_ln_b", R_LNB, 2), ("pool_scale", R_PS, 2)]
            for name, r, k in rows:
                sp.dma_start(prow[r:r + k, :], v[name].rearrange("l (r n) -> (l r) n", n=P)).then_inc(s["ld_prm"], 16)
            sp.dma_start(prow[R_CW:R_CW + 6, :], v["conv_w"].rearrange("l c (r n) -> (l c r) n", n=P)).then_inc(s["ld_prm"], 16)
            load_ada(2)
            load_ada(3)

            def load_win(i):
                b, u = ORDER[i], i % 2
                if B_Q <= b < B_KEY:
                    for n in range(2):
                        c0 = COL_ATT + (b - B_Q + 2 * n) * HD
                        sp.dma_start(win[:, u, :, n * HD:(n + 1) * HD], win_v[:, :, c0:c0 + HD]).then_inc(s_win[u], 16)
                    return
                if b < B_POOL:
                    c0 = COL_RWKV + b * P
                elif b < B_Q:
                    c0 = COL_POOL + (b - B_POOL) * P
                elif b < B_BG:
                    c0 = COL_ATT + 256 + (b - B_KEY) * P
                else:
                    c0 = COL_CONV + (b - B_BG) * P
                sp.dma_start(win[:, u], win_v[:, :, c0:c0 + P]).then_inc(s_win[u], 32)

            load_win(0)
            load_win(1)
            sp.wait_ge(s["const_ready"], 1)
            for g in range(4):
                h = 64 * (g % 2)
                sp.dma_start(pw[h:h + 64, g // 2, h:h + 64], v["pool_w"][0, g]).then_inc(s["ld_misc"], 16)
            sp.dma_start(lor[0:32, :], v["rwkv_w2"][0]).then_inc(s["ld_misc"], 16)
            sp.dma_start(lor[32:64, :], v["rwkv_a2"][0]).then_inc(s["ld_misc"], 16)
            sp.dma_start(lor[64:128, :], v["rwkv_g2"][0]).then_inc(s["ld_misc"], 16)
            sp.dma_start(sink[:, :], v["attn_sinks"].to_broadcast([P, 4])).then_inc(s["ld_misc"], 16)
            for j in range(2, NT):
                sp.wait_ge(s["xn_ready"], j - 1)
                load_x(j)
            sp.dma_start(rbias[:, 0:GROUPS], v["moe_b_grp"].to_broadcast([P, GROUPS])).then_inc(s["ld_wr"], 16)
            sp.dma_start(rbias[:, GROUPS:], v["moe_b_exp"].to_broadcast([P, E])).then_inc(s["ld_wr"], 16)
            sp.dma_start(wr[:, :, 0:GROUPS], v["moe_w_grp"].rearrange("l (k p) n -> (l p) k n", p=P)).then_inc(s["ld_wr"], 16)
            sp.dma_start(wr[:, :, GROUPS:], v["moe_w_exp"].rearrange("l (k p) n -> (l p) k n", p=P)).then_inc(s["ld_wr"], 16)
            for i in range(2):
                sp.dma_start(gtb[:, i], v["b_ada"][:, (2 + 3 * i) * D:(3 + 3 * i) * D].to_broadcast([P, D])).then_inc(s["gtb_ld"], 16)
            sp.wait_ge(s["acc_ready"], 4)
            for i in range(2, NB):
                sp.wait_ge(s["proj_ps"], i - 1)
                load_win(i)
                for h in range(2 * (i - 4), 2 * (i - 4) + 2) if 4 <= i < 12 else ():
                    if h >= 2:
                        sp.wait_ge(s["acb_ready"], h - 1)
                    sp.dma_start(adb[:, h % 2], ada_v[:, :, 2048 + h * 256:2304 + h * 256]).then_inc(s_ada[h % 2], 16)


            sp.wait_ge(s["w_z"], 4)
            sp.dma_start(wo[:, 0:KD - 1], wo_v[:, 0:KD - 1]).then_inc(s["wo_ld"], 16)
            sp.wait_ge(s["w_yT"], 5)
            sp.dma_start(wo[:, KD - 1], wo_v[:, KD - 1]).then_inc(s["ld_wr"], 16)
            for j in range(NT):
                sp.dma_start(x1[:, j], xd[j * P:(j + 1) * P, :]).then_inc(s["xr_ld"], 16)

            def load_expert(u, e):
                for dst, src in ((wg, wg_v), (wu, wu_v), (wd, wd_v)):
                    view = src[:, e] if isinstance(e, int) else src[:, ds(e, 1)]
                    d_ = dst[:, u] if isinstance(e, int) else dst[:, u:u + 1]
                    sp.dma_start(d_, view).then_inc(s_w[u], 16)

            for e in range(4):
                load_expert(e, e)
            for j in range(NT):
                sp.wait_ge(s["op_xn"], j + 1)
                sp.dma_start(xn2_d[j * P:(j + 1) * P, :], xn2[:, j % 2]).then_inc(s_st[j % 2], 16)
            sp.wait_ge(s["op_ps"], NT)
            sp.dma_start(fg, v["final_g"].rearrange("(o n) -> o n", o=1).to_broadcast([P, D])).then_inc(s["ld_fg"], 16)
            with sp.Fori(1, E // 4) as g:
                for u in range(4):
                    sp.wait_ge(s["m_dn"], g * 4 + (u - 3))
                    load_expert(u, g * 4 + u)
            sp.wait_ge(s["rt_n"], 1)
            n_ov = sp.value_load(idy[0:1, 0:1], min_val=1, max_val=OVT)
            with sp.Fori(0, n_ov) as i:
                sp.wait_ge(s["ov_go"], i + 1)
                e = sp.value_load(eid_view(i), min_val=0, max_val=E - 1)
                for dst, src in ((wg, wg_v), (wu, wu_v), (wd, wd_v)):
                    sp.dma_start(dst[:, 0:1], src[:, ds(e, 1)]).then_inc(s["ov_w"], 16)
            sp.wait_ge(s["f_go"], 1)

            def load_outputs(j):
                for n in range(2):
                    sp.dma_start(yab[:, j % 4, n], y_d[n * T + j * P:n * T + (j + 1) * P, :]).then_inc(s_w[j % 4], 16)

            for j in range(4):
                load_outputs(j)
            for j in range(NT):
                sp.wait_ge(s["f_o"], j + 1)
                sp.dma_start(outd[j * P:(j + 1) * P, :], fo[:, j % 2]).then_inc(s_fo[j % 2], 16)
                if j + 4 < NT:
                    load_outputs(j + 4)
            for n in range(2):
                sp.wait_ge(s_fo[n], 16 * NT // 2)


        @block.gpsimd
        def _(gp):
            ch = Chain(gp, s["chain_pool"])

            def keep(o_, in_, pattern, base, cm, op=ALU.is_ge, fill=0.0):
                ch.step(gp.affine_select(out=o_, in_=in_, compare_op=op, fill=fill, base=base, pattern=pattern,
                                         channel_multiplier=cm))

            ch.note(gp.memset(ident[:, :], 0.0))
            ch.note(gp.memset(pw[:, :, :], 0.0))
            ch.note(gp.memset(bones[:, :], 0.0))
            ch.step(gp.memset(ones[:, :], 1.0))
            keep(ident[:, :], ident[:, :], [[-1, P]], 0, 1, ALU.not_equal, 1.0)
            gp.memset(mhalf[:, :], -0.5).then_inc(s["const_ready"], 1)
            keep(tri[:, :], ones[:, :], [[1, P]], -1, -1)
            keep(msk[:, 1, :], ones[:, :], [[1, P]], 0, -1)
            ch.note(gp.memset(bones[0:64, 0:64], 1.0))
            ch.step(gp.memset(bones[64:P, 64:P], 1.0))
            ch.note(gp.tensor_tensor(msk[:, 0, :], tri[:, :], bones[:, :], ALU.mult))
            ch.step(gp.tensor_tensor(msk[:, 1, :], msk[:, 1, :], bones[:, :], ALU.mult))
            ch.step(gp.memset(lmask[:, :, :], 0.0))
            for l in range(6):
                b = 1 << l
                half = lmask[:, l, :].rearrange("p (n h b) -> p n h b", h=2, b=b)[:, :, 1, :]
                ch.step(gp.memset(half, 1.0))
                keep(half, half, [[-2 * b, P // (2 * b)], [0, b]], 0, 1)
                keep(half, half, [[2 * b, P // (2 * b)], [0, b]], b - 1, -1)
            ch.step(gp.iota(disti, pattern=[[1, 2 * P]], base=-P, channel_multiplier=-1))
            ch.step(gp.tensor_copy(adist[:, :], disti))
            keep(adist[:, :], adist[:, :], [[-1, 2 * P]], P, 1, fill=NEG)
            keep(adist[:, :], adist[:, :], [[1, 2 * P]], -1, -1, fill=NEG)
            ch.step(gp.memset(sel[:, :, :], 0.0))
            sv = sel[:, :, :].rearrange("p a (h d) -> p a h d", h=2)
            keep(sv, sv, [[-2, 4], [-1, 2], [0, HD]], 0, 1, ALU.not_equal, 1.0)
            ch.step(gp.memset(rmask[:, :], 1.0))
            ch.step(gp.memset(rmask[:, 0:512:CH], 0.0))
            ch.step(gp.iota(cnti[:, :], pattern=[[1, PAD]], base=1, channel_multiplier=0))
            for c in range(2):
                ch.step(gp.tensor_copy(rc16[:, c, :], cnti[:, :]))
                for h in range(2):
                    rows = rc16[64 * h:64 * h + 64, c, :]
                    ch.step(gp.tensor_scalar(rows, rows, float(2 << (2 * c + h)), None, ALU.min))
            gp.memset(S[:, 4], 0.0)
            gp.memset(G[:, :, :], 0.0)
            ch.note(gp.iota(out_row[:, :], pattern=[[P, 2 * NT]], base=0, channel_multiplier=1))
            gp.memset(tbl[:, :, :], OOB).then_inc(s["sel_ready"], 1)

            def power(out_, in_, n, ready, done, count):
                gp.wait_ge(s[ready], count)
                gp.tensor_tensor(out_, in_, mhalf[:, 0:n], ALU.pow).then_inc(s[done], 1)

            for j in range(NT):
                power(rs[:, j % 2:j % 2 + 1], ss[:, j % 2:j % 2 + 1], 1, "ms_ready", "rstd_ready", j + 1)

            gp.wait_ge(s["acc_ready"], 4)
            gp.memset(pT[:, ZB:, 0:PAD], 0.0).then_inc(s["pad_ready"], 1)

            gp.wait_ge(s["proj_act"], N_POOL)
            gp.wait_ge(s["proj_dve"], N_POOL)
            gp.wait_ge(s["pad_ready"], 1)
            gp.wait_ge(s["rt_c"], 1)
            ch.step(gp.memset(pm1[:, 0:PAD], 0.0))
            ch.step(gp.memset(pm2[:, 0:PAD], 0.0))
            for c in range(2):
                u = pT[:, B_POOL + c]
                src, dst, steps = u, pm1, 2 + 2 * c
                for n in range(steps):
                    sh = 1 << n
                    ch.step(gp.tensor_tensor(dst[:, PAD:], src[:, PAD:], src[:, PAD - sh:TW - sh], ALU.add))
                    if n >= steps - 2:
                        h = n - (steps - 2)
                        r = slice(64 * h, 64 * h + 64)
                        wdt = float(2 * sh)
                        ch.note(gp.tensor_scalar(pmd[r, c, PAD:], dst[r, 2 * PAD:], 1.0 / wdt, None, ALU.mult))
                        ch.step(gp.tensor_tensor(pmd[r, c, 0:PAD], dst[r, PAD:2 * PAD], rc16[r, c, :], ALU.mult))
                    src, dst = dst, (pm2 if dst is pm1 else pm1)
                gp.tensor_tensor(pmd[:, c, :], pmd[:, c, :], u[:, PAD:], ALU.subtract).then_inc(s["pool_d"], 1)
            gp.wait_ge(s["prm_ready"], 1)
            gp.wait_ge(s["proj_act"], N_CONV)
            gp.wait_ge(s["proj_dve"], N_CONV)
            for c in range(2):
                zc, yc, tap = pT[:, B_CG + c], pT[:, B_XI + c], yT[:, 4 + c, :]
                ch.step(gp.tensor_tensor(zc, zc, yc, ALU.mult))
                ch.step(gp.tensor_scalar(yc[:, PAD:], zc[:, PAD - 2:TW - 2], pc[:, R_CW + c:R_CW + c + 1], None, ALU.mult))
                for n in (1, 2):
                    ch.step(gp.tensor_scalar(tap, zc[:, PAD - 2 + n:TW - 2 + n],
                                             pc[:, R_CW + 2 * n + c:R_CW + 2 * n + c + 1], None, ALU.mult))
                    ch.step(gp.tensor_tensor(yc[:, PAD:], yc[:, PAD:], tap, ALU.add))
                gp.tensor_tensor(tap, yc[:, PAD:], pT[:, B_BG + c, PAD:], ALU.mult).then_inc(s["conv_y"], 1)
                gp.wait_ge(s["conv_y"], c + 1)
            gp.wait_ge(s["acb_ready"], 16)
            gp.memset(pT[:, 0:ZB, 0:PAD], 0.0).then_inc(s["pad_ready"], 1)

            def differences(m):
                if m is None:
                    prev, at = PAD - 1, PAD
                    gp.wait_ge(s["w_yT"], 1)
                    src = [pT[:, 0:ZB, c:c + W2] for c in (prev, at)]
                else:
                    prev, at = (gp.snap(m * W2 + (W2 + PAD - 1 + c)) for c in (0, 1))
                    gp.wait_ge(s["w_akp"], m * 2 + 2)
                    src = [pT[:, 0:ZB, ds(c, W2)] for c in (prev, at)]
                gp.tensor_tensor(df, src[0], src[1], ALU.subtract).then_inc(s["w_df"], 1)

            def turn(m, more):
                gp.wait_ge(s["w_yT"], m + 1)
                gp.wait_ge(s["w_gg"], m + 1)
                one = ones[:, 0:1].unsqueeze(2).to_broadcast([P, 2, W2])
                gp.tensor_tensor(zv, z[:, B_V:B_V + 2, :], one, ALU.mult)
                gp.tensor_tensor(gg, ggn, one, ALU.mult).then_inc(s["w_cp"], 1)
                for l in range(6):
                    for n in range(2):
                        if l == 0:
                            gp.wait_ge(s["w_ab"], m * 2 + (n + 1))
                        elif l == 1:
                            gp.wait_ge(s["w_xt"], m * 12 + (n + 1))
                        else:
                            gp.wait_ge(s["w_t1p"], m * 10 + (2 * (l - 2) + n + 1))
                        gp.tensor_tensor(rw[n]["bl"], rw[n]["ab"][:, :, 0, :],
                                         lmask[:, l:l + 1, :].to_broadcast([P, 4, P]), ALU.mult).then_inc(s["w_bl"], 1)
                    if l == 1 and more:
                        differences(m)
                    if l == 4 and more:
                        power(nrp[:, :], nrm[:, :], 8, "w_nrm", "w_nrp", front_counts(m)[1])
                power(nrp[:, :], nrm[:, :], 8, "w_nrm", "w_nrp", tail_norm(m))

            differences(None)
            power(nrp[:, :], nrm[:, :], 8, "w_nrm", "w_nrp", 1)
            with gp.Fori(0, TURNS - 1) as m:
                turn(m, True)
            turn(TURNS - 1, False)

            for j in range(NT):
                power(rs[:, j % 2:j % 2 + 1], ss[:, j % 2:j % 2 + 1], 1, "ms_ready", "rstd_ready", NT + j + 1)
            gp.wait_ge(s["op_ps"], NT)
            ch.step(gp.memset(xg, 0.0))
            gp.wait_ge(s["rt_ld"], 1)
            gp.wait_ge(s_st[0], 16 * NT // 2)
            gp.wait_ge(s_st[1], 16 * NT // 2)

            def tview(e, c):
                if isinstance(e, int):
                    return tbl[:, e, c:c + 1]
                return tbl[:, ds(e, 1), c:c + 1].rearrange("p o f -> p (o f)")

            last_row, last_out = gp.to_reg(T - 1), gp.to_reg(2 * T - 1)

            def pause():
                ch.note(gp.tensor_tensor(junk[:, :], mhalf[:, 0:1], mhalf[:, 0:1], ALU.mult))

            def gather(e, par):
                row_ = e if isinstance(e, int) else gp.snap(e)
                if not isinstance(e, int) or e >= 2:
                    gp.wait_ge(s["m_tx"], e - 1)
                ch.step(gp.tensor_copy(idx[:, par:par + 1], tview(row_, 1)))
                pause()
                gp.indirect_dma_start(out=xg[:, par], out_offset=None, in_=xn2_d[:, :],
                                      in_offset=bass.IndirectOffsetOnAxis(ap=idx[:, par:par + 1], axis=0),
                                      bounds_check=last_row, oob_is_err=False).then_inc(s_gx[par], 16)

            def scatter(e, par):
                row_ = e if isinstance(e, int) else gp.snap(e)
                gp.wait_ge(s["m_ya"], e + 1)
                gp.wait_ge(s["m_yd"], e + 1)
                ch.step(gp.tensor_copy(idx[:, 2 + par:3 + par], tview(row_, 0)))
                pause()
                gp.indirect_dma_start(out=y_d[:, :], out_offset=bass.IndirectOffsetOnAxis(ap=idx[:, 2 + par:3 + par], axis=0),
                                      in_=yo[:, par], in_offset=None, bounds_check=last_out,
                                      oob_is_err=False).then_inc(s_sc[par], 16)

            gather(0, 0)
            gather(1, 1)
            gather(2, 0)
            gather(3, 1)
            with gp.Fori(0, 7) as g:
                ch.enter(g, 16)
                for u in range(4):
                    gather(g * 4 + (4 + u), u % 2)
                    scatter(g * 4 + u, u % 2)
            ch.leave(7)

            def gather_overflow(tile):
                row_ = tile if isinstance(tile, int) else gp.snap(tile)
                ch.step(gp.tensor_copy(idx[:, 0:1], tview(row_, 1)))
                pause()
                gp.indirect_dma_start(out=xg[:, 0], out_offset=None, in_=xn2_d[:, :],
                                      in_offset=bass.IndirectOffsetOnAxis(ap=idx[:, 0:1], axis=0),
                                      bounds_check=last_row, oob_is_err=False).then_inc(s["ov_g"], 16)

            for e in (28, 29):
                scatter(e, e % 2)
            gp.wait_ge(s["m_tx"], E - 1)
            gp.wait_ge(s["m_dn"], E - 3)
            gather_overflow(E)
            gp.sem_inc(s["ov_go"], 1)
            for e in (30, 31):
                scatter(e, e % 2)
            for par in range(2):
                gp.wait_ge(s_sc[par], 16 * E // 2)

            n_ov = gp.value_load(idy[0:1, 0:1], min_val=1, max_val=OVT)
            with gp.Fori(0, n_ov) as i:
                ch.enter(i, 4)
                row_ = gp.snap(i + E)
                ch.step(gp.tensor_copy(idx[:, 2:3], tview(row_, 0)))
                gp.wait_ge(s["m_ya"], i + (E + 1))
                gp.wait_ge(s["m_yd"], i + (E + 1))
                pause()
                gp.indirect_dma_start(out=y_d[:, :], out_offset=bass.IndirectOffsetOnAxis(ap=idx[:, 2:3], axis=0),
                                      in_=yo[:, 0], in_offset=None, bounds_check=last_out,
                                      oob_is_err=False).then_inc(s["ov_sc"], 16)
                gp.wait_ge(s["ov_sc"], i * 16 + 16)
                gather_overflow(i + (E + 1))
                gp.sem_inc(s["ov_go"], 1)
            gp.sem_inc(s["f_go"], 1)

            def add_outputs(j):
                gp.wait_ge(s_w[j % 4], 48 * (E // 4) + 32 * (j // 4 + 1))
                gp.tensor_tensor(yab[:, j % 4, 0], yab[:, j % 4, 0], yab[:, j % 4, 1], ALU.add).then_inc(s["f_a"], 1)

            add_outputs(0)
            add_outputs(1)
            for j in range(NT):
                if j + 2 < NT:
                    add_outputs(j + 2)
                power(rs[:, j % 2:j % 2 + 1], ss[:, j % 2:j % 2 + 1], 1, "ms_ready", "rstd_ready", 2 * NT + j + 1)

        @block.tensor
        def _(pe):
            def mm(o_, l, r, start=True, stop=True):
                return pe.matmul(o_, l, r, start=start, stop=stop, skip_group_check=True)

            def columns(out_, sums, n):
                for q in range(n):
                    last = mm(out_[:, q:q + 1], sums[:, q * P:(q + 1) * P], ones[:, 0:1])
                return last

            pe.wait_ge(s["sel_ready"], 1)
            pe.wait_ge(s["ld_prm"], 16 * 13)
            pe.transpose(PS[7][:, 0:NR], prow[:, :], ident[0:NR, 0:NR]).then_inc(s["prm_t"], 1)
            for b in range(4):
                pe.wait_ge(s["acc_ready"], b + 1)
                last = columns(PS[6][:, 4 * b:4 * b + 4], acc[:, b], 4)
            last.then_inc(s["mod1_ps"], 1)

            for j in range(NT):
                pe.wait_ge(s["xn_ready"], j + 1)
                if j >= 2:
                    pe.wait_ge(s["hT_act"], j - 1)
                    pe.wait_ge(s["hT_dve"], j - 1)
                for k in range(KD):
                    last = pe.transpose(PS[2 * (j % 2) + k // 4][:, (k % 4) * P:(k % 4 + 1) * P],
                                        xn[:, j % 2, k * P:(k + 1) * P], ident[:, :])
                last.then_inc(s["hT_tr"], 1)
            pe.wait_ge(s["hT_act"], NT)
            pe.wait_ge(s["hT_dve"], NT)
            pe.wait_ge(s["mod1_ready"], 1)

            def project(par, loads, done, mid=None):
                pe.wait_ge(s_win[par], loads)
                if done is not None:
                    pe.wait_ge(s["proj_act"], done)
                    pe.wait_ge(s["proj_dve"], done)
                for k in range(KD):
                    if k == KD // 2 and mid is not None:
                        mid()
                    for h in range(2):
                        last = mm(PS[2 * par + h][:, :], win[:, par, k, :], hT[:, k, h * 512:(h + 1) * 512], k == 0, k == KD - 1)
                last.then_inc(s["proj_ps"], 1)

            def scores(nb):
                first = isinstance(nb, int) and nb == 0
                k0 = 1 if first else 0
                ks = slice(nb * P + (PAD - P * (1 - k0)), nb * P + PAD + P) if isinstance(nb, int) else \
                    ds(nb * P + (PAD - P), 2 * P)
                pe.wait_ge(s["att_q"], nb + 1)
                if not isinstance(nb, int) or nb >= 2:
                    pe.wait_ge(s["att_tpa"], nb - 1)
                    pe.wait_ge(s["att_tpd"], nb - 1)
                for h in range(4):
                    last = mm(PS[4 + h // 2][:, (h % 2) * 256 + k0 * P:(h % 2) * 256 + 256], qz[:, h, :], pT[:, B_KEY, ks])
                last.then_inc(s["att_qk"], 1)
                if not first:
                    pe.wait_ge(s["mod2_ready"], nb)
                for kb in range(k0, 2):
                    last = pe.transpose(PS[6][:, kb * P:(kb + 1) * P], vs[:, kb * P:(kb + 1) * P], ident[:, :])
                last.then_inc(s["att_vps"], 1)

            def flip_probs(nb, par, nxt=True):
                k0 = 1 if isinstance(nb, int) and nb == 0 else 0
                pe.wait_ge(s["att_pn"], nb + 1)
                if nxt:
                    pe.wait_ge(s["att_nm"], nb + 2)
                for h in range(4):
                    for kb in range(k0, 2):
                        last = pe.transpose(PS[4 + h // 2][:, ((h % 2) * 2 + kb) * P:((h % 2) * 2 + kb + 1) * P],
                                            sc[:, par, h, kb * P:(kb + 1) * P], ident[:, :])
                last.then_inc(s["att_tp"], 1)

            def outputs(nb, par):
                k0 = 1 if isinstance(nb, int) and nb == 0 else 0
                pe.wait_ge(s["att_v"], nb + 1)
                pe.wait_ge(s["att_tpa"], nb + 1)
                pe.wait_ge(s["att_tpd"], nb + 1)
                if isinstance(nb, int) and nb == NT - 1:
                    pe.wait_ge(s["att_y"], nb)
                for h in range(4):
                    r = 64 * (h % 2)
                    for kb in range(k0, 2):
                        last = mm(PS[7][r:r + 64, (h // 2) * P:(h // 2 + 1) * P], vt[:, par, kb, (h // 2) * HD:(h // 2 + 1) * HD],
                                  ptT[:, h, kb, :], kb == k0, kb == 1)
                last.then_inc(s["att_o"], 1)

            def sums(nb, gates):
                pe.wait_ge(s["acb_ready"], nb * 2 + 2)
                pe.wait_ge(s["att_v"], nb + 1)
                if gates:
                    last = mm(PS[6][:, :], ones[:, :], acb.rearrange("p a b -> p (a b)"))
                else:
                    last = columns(PS[6][:, 0:4], acb.rearrange("p a b -> p (a b)"), 4)
                last.then_inc(s["mod2_ps"], 1)

            for i in range(SLOT0):
                project(i % 2, 32 * (i // 2 + 1), i - 1 if i >= 2 else None)
            scores(0)
            project(1, 32 * 3, 4, lambda: sums(0, True))
            scores(1)
            project(0, 32 * 4, 5, lambda: (flip_probs(0, 0), sums(1, True)))

            def beside(g, u, gates):
                outputs(g * 2 + u, u)
                scores(g * 2 + (2 + u))
                project((1 + u) % 2, g * 32 + 32 * (4 + u), g * 2 + (6 + u),
                        lambda: (flip_probs(g * 2 + (1 + u), (1 + u) % 2), sums(g * 2 + (2 + u), gates)))

            with pe.Fori(0, 2) as g:
                for u in range(2):
                    beside(g, u, False)
            for u in range(2):
                beside(2, u, True)
            outputs(6, 0)
            project(1, 32 * 7, 12, lambda: flip_probs(7, 1, False))
            outputs(7, 1)
            project(0, 32 * 8, 13)
            pe.wait_ge(s["ld_misc"], 16 * 8)
            pe.wait_ge(s["att_y"], NT)
            for c in range(2):
                pe.wait_ge(s["pool_d"], c + 1)
                if c == 1:
                    pe.wait_ge(s["pool_y"], 2)
                for h in range(2):
                    last = mm(PS[6 + h][:, :], pw[:, c, :], pmd[:, c, h * 512:(h + 1) * 512])
                last.then_inc(s["pool_ps"], 1)
                project(1 - c, 32 * (8 + c), 14 + c)
            project(1, 32 * 9, 16)
            project(0, 32 * 10, 17)
            pe.wait_ge(s["proj_act"], NB)
            pe.wait_ge(s["proj_dve"], NB)
            pe.wait_ge(s["pool_y"], 4)

            def hb(h):
                return slice(64 * (h % 2), 64 * (h % 2) + 64)

            def lora_wa(m):
                cnt = front_counts(m)[0]
                pe.wait_ge(s["w_tanh"], cnt(1, 1))
                if m is not None:
                    pe.wait_ge(s["w_w1"], m * 2 + 2)
                for p in range(2):
                    last = mm(PS[0][:, p * W2:(p + 1) * W2], lor[0:32, p * P:(p + 1) * P], lt[0:32, :])
                last.then_inc(s["w_lora"], 1)
                for p in range(2):
                    last = mm(PS[1][:, p * W2:(p + 1) * W2], lor[32:64, p * P:(p + 1) * P], z[32:64, B_LORA, :])
                last.then_inc(s["w_lora"], 1)

            def lora_g(m):
                pe.wait_ge(s["w_sg"], front_counts(m)[0](1, 1))
                for p in range(2):
                    last = mm(PS[4][:, p * W2:(p + 1) * W2], lor[64:128, p * P:(p + 1) * P], lt[64:128, :])
                last.then_inc(s["w_lora"], 1)

            def norm_sums(bank, count):
                pe.wait_ge(s["w_sq"], count)
                for n in range(2):
                    for p in range(2):
                        c = n * 4 + p * 2
                        last = mm(PS[bank][:, c:c + 2], sq[:, p, n * P:(n + 1) * P], bones[:, 0:P:64])
                last.then_inc(s["w_ss"], 1)

            def norm_flip(bank, count):
                pe.wait_ge(s["w_nrp"], count)
                pe.transpose(PS[bank][0:8, P:2 * P], nrp[:, :], ident[:, :]).then_inc(s["w_nrt"], 1)

            def norm_back(bank, count):
                pe.wait_ge(s["w_nrT"], count)
                for p in range(2):
                    for n in range(2):
                        last = mm(PS[bank][:, p * W2 + n * P:p * W2 + (n + 1) * P], sel[:, n * 2 + p, :], nrT[:, :])
                last.then_inc(s["w_nrb"], 1)

            def turn(m, more):
                def wait(name, per, k):
                    pe.wait_ge(s[name], m * per + k)

                cnt, fn_ = front_counts(m)
                wait("w_ops", 1, 1)
                wait("w_gg", 1, 1)
                for n in range(2):
                    tk = slice(n * P, (n + 1) * P)
                    for i, src in enumerate((Bt, Kt)):
                        for p in range(2):
                            pe.transpose(PS[4 * n][:, (2 * i + p) * P:(2 * i + p + 1) * P], src[:, p, tk], ident[:, :])
                    for p in range(2):
                        pe.transpose(PS[4 * n + 1][:, p * P:(p + 1) * P], z[:, B_V + p, tk], ident[:, :])
                        last = pe.transpose(PS[4 * n + 1][:, (2 + p) * P:(3 + p) * P], KR[:, p, 0, tk], ident[:, :])
                    last.then_inc(s["w_tok"], 1)
                    for h in range(4):
                        last = mm(PS[4 * n + 2 + h % 2][:, (h // 2) * 256:(h // 2) * 256 + 256].rearrange("p (a t) -> p a t", a=2),
                                  Bt[hb(h), h // 2, tk], KR[hb(h), h // 2, :, tk])
                    last.then_inc(s["w_abp"], 1)
                for n in range(2):
                    tk = slice(n * P, (n + 1) * P)
                    wait("w_tka", 2, n + 1)
                    wait("w_tkd", 2, n + 1)
                    for h in range(4):
                        last = mm(PS[4 * n + h % 2][:, (h // 2) * 256:(h // 2) * 256 + 256].rearrange("p (a t) -> p a t", a=2),
                                  Kt[hb(h), h // 2, tk], KR[hb(h), h // 2, :, tk])
                    last.then_inc(s["w_akp"], 1)

                def four(n, bank, l, r, sem_name):
                    for h in range(4):
                        last = mm(PS[4 * n + bank][:, h * P:(h + 1) * P], l[:, h, :], r[:, h, :])
                    last.then_inc(s[sem_name], 1)

                def flip(n, bank):
                    for h in range(4):
                        last = pe.transpose(PS[4 * n + bank][:, h * P:(h + 1) * P], rw[n]["xt"][:, h, :], ident[:, :])
                    last.then_inc(s["w_xp"], 1)

                for n in range(2):
                    wait("w_xt", 12, n + 1)
                    flip(n, 2)
                for n in range(2):
                    wait("w_ak", 2, n + 1)
                    for h in range(4):
                        last = mm(PS[4 * n][:, h * HD:(h + 1) * HD], rw[n]["ak"][:, h, 0, :], rw[n]["vt"][:, h, :])
                    last.then_inc(s["w_w1p"], 1)
                for l in range(1, 6):
                    for n in range(2):
                        wait("w_xa", 10, 2 * (l - 1) + n + 1)
                        wait("w_bl", 12, 2 * l + n + 1)
                        four(n, 3, rw[n]["bl"], rw[n]["x"], "w_t1p")
                    if more and l == 3:
                        lora_wa(m)
                        norm_sums(5, fn_)
                    if more and l == 4:
                        lora_g(m)
                    for n in range(2):
                        wait("w_t1", 10, 2 * (l - 1) + n + 1)
                        four(n, 2, rw[n]["t1"], rw[n]["xt"], "w_x2p")
                    if l < 5:
                        for n in range(2):
                            wait("w_xt", 12, 2 * l + n + 1)
                            flip(n, 3)
                    if more and l == 4:
                        norm_flip(5, fn_)
                if more:
                    pe.wait_ge(s["w_th"], cnt(1, 1))
                    norm_back(0, fn_)
                    pe.wait_ge(s["w_tha"], cnt(1, 1))
                for n in range(2):
                    wait("w_xt", 12, 10 + n + 1)
                    wait("w_w1", 2, n + 1)
                    for h in range(4):
                        last = mm(PS[4 * n + 1][:, h * P:(h + 1) * P], rw[n]["xt"][:, h, :],
                                  rw[n]["wk"][:, h].rearrange("p a d -> p (a d)"))
                    last.then_inc(s["w_uzp"], 1)
                for n in range(2):
                    wait("w_uz", 2, n + 1)
                    if n == 1 and more:
                        wait("w_re", 2, 1)
                        pe.wait_ge(s["w_gg"], cnt(1, 1))
                    uz, bt = rw[n]["uz"], rw[n]["bt"]
                    for h in range(4):
                        last = mm(PS[4 * n + 3][hb(h), (h // 2) * P:(h // 2 + 1) * P], uz[:, 1, h, :], rw[n]["ab"][:, h, 1, :])
                    last.then_inc(s["w_rep"], 1)
                    for c in range(2):
                        rr = slice(64 * c, 64 * c + 64)
                        for h in range(4):
                            last = mm(PS[4 * n + 2 - c][hb(h), (h // 2) * HD:(h // 2 + 1) * HD], uz[rr, 1, h, :], bt[rr, h, :])
                    last.then_inc(s["w_gp"], 1)
                for n in range(2):
                    t = rw[n]
                    for c in range(2):
                        rr = slice(64 * c, 64 * c + 64)
                        for p in range(2):
                            o_ = PS[4 * n + 3 * c][:, p * HD:(p + 1) * HD]
                            for h in (2 * p, 2 * p + 1):
                                mm(o_[hb(h), :], t["bt"][rr, h, :], t["uz"][rr, 0, h, :], True, False)
                                mm(o_[hb(h), :], t["kt"][rr, h, :], t["vt"][rr, h, :], False, False)
                            if p == 0:
                                if c == 0:
                                    wait("w_G", 2, n + 1)
                                wait("w_S", 5, 2 * n + c + 1)
                            last = mm(o_, G[:, 4 * n + c * 2 + p, :], S[:, 2 * n + c, p, :], False, True)
                        last.then_inc(s["w_hp"], 1)
                for n in range(2):
                    wait("w_re", 2, n + 1)
                    t = rw[n]
                    for h in range(4):
                        p = h // 2
                        o_ = PS[4 * n + 1][hb(h), p * P:(p + 1) * P]
                        mm(o_, t["uz"][:, 0, h, :], t["ab"][:, h, 1, :], True, False)
                        mm(o_, t["vt"][:, h, :], t["ak"][:, h, 1, :], False, False)
                        for c in range(2):
                            cs = slice(64 * c, 64 * c + 64)
                            last = mm(o_[:, cs], S[hb(h), 2 * n + c, p, :], t["re"][hb(h), p, cs], False, c == 1)
                    last.then_inc(s["w_yp"], 1)
                wait("w_y", 2, 2)
                mm(PS[2][:, :], bones[:, :], yb.rearrange("p a t -> p (a t)")).then_inc(s["w_mean"], 1)
                for p in range(2):
                    last = mm(PS[5][:, p * W2:(p + 1) * W2], brk[:, p, :], rk[:, p, :])
                last.then_inc(s["w_bonp"], 1)
                norm_sums(3, tail_norm(m))
                norm_flip(3, tail_norm(m))
                norm_back(4, tail_norm(m))

            lora_wa(None)
            norm_sums(5, 1)
            lora_g(None)
            norm_flip(5, 1)
            pe.wait_ge(s["w_th"], 1)
            norm_back(0, 1)
            with pe.Fori(0, TURNS - 1) as m:
                turn(m, True)
            turn(TURNS - 1, False)

            pe.wait_ge(s["w_yT"], 5)
            pe.wait_ge(s["wo_ld"], 16)
            pe.wait_ge(s["ld_wr"], 16 * 4)

            def out_main(j):
                if j >= 2:
                    pe.wait_ge(s["op_x1"], j - 1)
                for k in range(KD):
                    if j == 0 and k == KD - 1:
                        pe.wait_ge(s["ld_wr"], 16 * 5)
                    for h in range(2):
                        last = mm(PS[2 * (j % 2) + h][:, :], yT[:, k, j * P:(j + 1) * P], wo[:, k, h * 512:(h + 1) * 512],
                                  k == 0, k == KD - 1)
                last.then_inc(s["op_ps"], 1)

            out_main(0)
            for j in range(NT):
                if j + 1 < NT:
                    out_main(j + 1)
                pe.wait_ge(s["op_xn"], j + 1)
                if j >= 1:
                    pe.wait_ge(s["op_ta"], j)
                    pe.wait_ge(s["op_td"], j)
                for k in range(KD):
                    last = pe.transpose(PS[4 + k // 4][:, (k % 4) * P:(k % 4 + 1) * P], xn2[:, j % 2, k * P:(k + 1) * P],
                                        ident[:, :])
                last.then_inc(s["op_tp"], 1)
                pe.wait_ge(s["op_ta"], j + 1)
                pe.wait_ge(s["op_td"], j + 1)
                if j >= 1:
                    pe.wait_ge(s["op_lgd"], j)
                for k in range(KD):
                    last = mm(PS[6][:, 0:GROUPS + E], h2T[:, k, :], wr[:, k, :], k == 0, k == KD - 1)
                last.then_inc(s["op_lg"], 1)

            pe.wait_ge(s["rt_oh"], 1)
            flat = rt["tmp"].rearrange("p a b -> p (a b)")
            mm(PS[7][:, 0:NT * E], tri[:, :], flat)
            mm(PS[7][:, 256:256 + NT * E], ones[:, :], flat).then_inc(s["rt_pos"], 1)
            for a in range(2 * NT):
                if a % 4 == 0:
                    pe.wait_ge(s["rt_hot"], a // 4 + 1)
                last = mm(PS[7][:, 0:3 * TILES], lanes[:, a, :], hots[:, a].rearrange("p q t -> p (q t)"), a == 0, a == 2 * NT - 1)
            last.then_inc(s["rt_tab"], 1)

            def ex_t(e, par, pre="m_", gsem=None, gcount=None, wait_free=True):
                pe.wait_ge(gsem, gcount)
                if wait_free:
                    pe.wait_ge(s[pre + "xa"], e)
                    pe.wait_ge(s[pre + "xd"], e)
                for k in range(KD):
                    last = pe.transpose(PS[k // 4][:, (k % 4) * P:(k % 4 + 1) * P], xg[:, par, k * P:(k + 1) * P], ident[:, :])
                last.then_inc(s[pre + "tx"], 1)

            def ex_gu(e, par, u, pre="m_", wsem=None, wcount=None, wait_free=True):
                pe.wait_ge(s[pre + "xa"], e + 1)
                pe.wait_ge(s[pre + "xd"], e + 1)
                pe.wait_ge(wsem, wcount)
                if wait_free:
                    pe.wait_ge(s[pre + "act"], e - 1)
                for i, wt in enumerate((wg, wu)):
                    for k in range(KD):
                        last = mm(PS[2 + par][:, i * P:(i + 1) * P], wt[:, u, k, :], xt[:, par, k, :], k == 0, k == KD - 1)
                last.then_inc(s[pre + "gu"], 1)

            def ex_dn(e, par, u, pre="m_", wait_free=True):
                pe.wait_ge(s[pre + "act"], e + 1)
                if wait_free:
                    pe.wait_ge(s[pre + "ya"], e - 1)
                    pe.wait_ge(s[pre + "yd"], e - 1)
                for h in range(2):
                    last = mm(PS[4 + 2 * par + h][:, :], ac[:, par, :], wd[:, u, h * 512:(h + 1) * 512])
                last.then_inc(s[pre + "dn"], 1)

            ex_t(0, 0, gsem=s_gx[0], gcount=16, wait_free=False)
            ex_t(1, 1, gsem=s_gx[1], gcount=16)
            ex_gu(0, 0, 0, wsem=s_w[0], wcount=48, wait_free=False)

            def turn(e, u1, gcount_, wcount_, first):
                ex_t(e + 1, (u1 + 1) % 2, gsem=s_gx[(u1 + 1) % 2], gcount=gcount_)
                ex_gu(e, u1 % 2, u1 % 4, wsem=s_w[u1 % 4], wcount=wcount_, wait_free=not first)
                ex_dn(e - 1, (u1 - 1) % 2, (u1 - 1) % 4, wait_free=not first)

            turn(1, 1, 32, 48, True)
            ex_t(3, 1, gsem=s_gx[1], gcount=32)
            ex_gu(2, 0, 2, wsem=s_w[2], wcount=48)
            ex_dn(1, 1, 1, wait_free=False)
            with pe.Fori(0, 7) as g:
                for u in range(4):
                    turn(g * 4 + (3 + u), 3 + u, g * 32 + 16 * ((4 + u) // 2 + 1), g * 48 + 48 * ((3 + u) // 4 + 1), False)
            ex_gu(31, 1, 3, wsem=s_w[3], wcount=48 * 8)
            ex_dn(30, 0, 2)
            ex_dn(31, 1, 3)

            n_ov = pe.value_load(idy[0:1, 0:1], min_val=1, max_val=OVT)
            pe.wait_ge(s["m_ya"], E)
            pe.wait_ge(s["m_yd"], E)
            with pe.Fori(0, n_ov) as i:
                ex_t(i + E, 0, "m_", s["ov_g"], i * 16 + 16, False)
                ex_gu(i + E, 0, 0, "m_", s["ov_w"], i * 48 + 48, False)
                ex_dn(i + E, 0, 0, "m_", False)

        @block.scalar
        def _(act):
            def fn(o_, i_, f=ACT.Copy, **kw):
                return act.activation(o_, i_, f, **kw)

            act.wait_ge(s["ld_c"], 16)
            fn(ct[:, :], cc[:, :], ACT.Tanh, scale=0.5).then_inc(s["silu_t"], 1)

            def square(j):
                act.wait_ge(s_x[j % 2], 16 * (j // 2 + 1))
                fn(xn[:, j % 2], xin[:, j % 2], ACT.Square, accum_out=ss[:, j % 2:j % 2 + 1]).then_inc(s["ss_ready"], 1)

            square(0)
            square(1)
            act.wait_ge(s["mod1_ready"], 1)
            for j in range(NT):
                act.wait_ge(s["hT_tr"], j + 1)
                for k in range(4):
                    last = fn(hT[:, k, j * P:(j + 1) * P], PS[2 * (j % 2)][:, k * P:(k + 1) * P], ACT.Identity,
                              scale=s1[:, k:k + 1], bias=mod[:, M_SH1 + k:M_SH1 + k + 1])
                last.then_inc(s["hT_act"], 1)
                if j + 2 < NT:
                    square(j + 2)

            def projected(i, par, blk=None):
                act.wait_ge(s["proj_ps"], i + 1)
                dst = pT[:, ORDER[i], PAD:PAD + 512] if blk is None else \
                    pT[:, ds(blk, 1), PAD:PAD + 512].rearrange("p o t -> p (o t)")
                fn(dst, PS[2 * par][:, :]).then_inc(s["proj_act"], 1)

            def queries(nb):
                first = isinstance(nb, int) and nb == 0
                k0 = 1 if first else 0
                tok = slice(nb * P + PAD, nb * P + PAD + P) if isinstance(nb, int) else ds(nb * P + PAD, P)
                at = slice(nb * P + PAD - P * (1 - k0), nb * P + PAD + P) if isinstance(nb, int) else ds(nb * P + (PAD - P), 2 * P)
                if not first:
                    act.wait_ge(s["att_qk"], nb)
                    act.wait_ge(s["att_vps"], nb)
                for kv in range(2):
                    r = slice(64 * kv, 64 * kv + 64)
                    fn(qz[r, 2 * kv:2 * kv + 2, :], pT[r, B_Q:B_Q + 2, tok], scale=float(HD) ** -0.5)
                fn(vs[:, k0 * P:], pT[:, B_VAL, at]).then_inc(s["att_q"], 1)

            def values(nb, par):
                k0 = 1 if isinstance(nb, int) and nb == 0 else 0
                act.wait_ge(s["att_vps"], nb + 1)
                fn(vt[:, par, k0:, :], PS[6][:, k0 * P:256].rearrange("p (a b) -> p a b", b=P)).then_inc(s["att_v"], 1)

            def exps(nb, par):
                k0 = 1 if isinstance(nb, int) and nb == 0 else 0
                act.wait_ge(s["att_nm"], nb + 1)
                for h in range(4):
                    fn(sc[:, par, h, k0 * P:], sc[:, par, h, k0 * P:], ACT.Exp, bias=nm[:, h:h + 1], accum_out=sm[:, h:h + 1])
                fn(es[:, :], es[:, :], ACT.Exp).then_inc(s["att_p"], 1)

            def flipped(nb):
                k0 = 1 if isinstance(nb, int) and nb == 0 else 0
                act.wait_ge(s["att_tp"], nb + 1)
                fn(ptT[:, 0:2, k0:, :], PS[4][:, :].rearrange("p (h a b) -> p h a b", h=2, b=P)[:, :, k0:, :])\
                    .then_inc(s["att_tpa"], 1)

            act.wait_ge(s["pad_ready"], 1)
            for i in range(N_ATT):
                projected(i, i % 2)
            act.wait_ge(s["att_zero"], 1)
            act.wait_ge(s["proj_dve"], N_ATT)
            act.wait_ge(s["proj_act"], N_ATT)
            for n in range(2):
                queries(n)
                projected(SLOT0 - 1 + n, n)
                values(n, n)
                exps(n, n)
                if n == 1:
                    flipped(0)
            with act.Fori(0, 3) as g:
                for u in range(2):
                    queries(g * 2 + (2 + u))
                    projected(g * 2 + (6 + u), u, g * 2 + (B_BG + u))
                    values(g * 2 + (2 + u), u)
                    exps(g * 2 + (2 + u), u)
                    flipped(g * 2 + (1 + u))
            projected(12, 0)
            flipped(7)
            for i in (13, 14):
                projected(i, i % 2)

            for i in range(4):
                c, h = i // 2, i % 2
                act.wait_ge(s["pool_ps"], c + 1)
                fn(yT[:, c, h * 512:(h + 1) * 512], PS[6 + h][:, :], scale=pc[:, R_PS + c:R_PS + c + 1]).then_inc(s["pool_y"], 1)
                if h == 1:
                    projected(15 + c, 1 - c)
            projected(17, 1)
            projected(18, 0)

            def squash(m):
                cnt = front_counts(m)[0]
                act.wait_ge(s["w_z"], cnt(1, 1))
                fn(lt[0:32, :], z[0:32, B_LORA, :], ACT.Tanh)
                fn(lt[64:128, :], z[64:128, B_LORA, :], ACT.Tanh, scale=0.5).then_inc(s["w_tanh"], 1)
                act.wait_ge(s["w_kkr"], cnt(1, 1))
                fn(sq, kkr, ACT.Square).then_inc(s["w_sq"], 1)

            def rates(m):
                cnt = front_counts(m)[0]
                for i, (dst, done) in enumerate(((lw, "w_th"), (aa, "w_tha"))):
                    act.wait_ge(s["w_lora"], cnt(3, i + 1))
                    for p in range(2):
                        last = fn(dst[:, p], PS[i][:, p * W2:(p + 1) * W2], ACT.Tanh, scale=0.5,
                                  bias=hp[:, 2 * i + p:2 * i + p + 1])
                    last.then_inc(s[done], 1)

            def out_gate(m):
                act.wait_ge(s["w_lora"], front_counts(m)[0](3, 3))
                fn(ggn.rearrange("p a t -> p (a t)"), PS[4][:, :]).then_inc(s["w_gg"], 1)

            def decays(m):
                act.wait_ge(s["w_L"], front_counts(m)[0](1, 1))
                fn(Pc, Lc, ACT.Exp)
                fn(Pm, Lm, ACT.Exp)
                fn(iP, Lc, ACT.Exp, scale=-1.0).then_inc(s["w_exp"], 1)

            def turn(m, more):
                def wait(name, per, k):
                    act.wait_ge(s[name], m * per + k)

                wait("w_yT", 1, 1)
                fn(S[:, 0], S[:, 4]).then_inc(s["w_S"], 1)
                for n in range(2):
                    wait("w_tok", 2, n + 1)
                    fn(both(n), PS[4 * n][:, :]).then_inc(s["w_tka"], 1)
                for n in range(2):
                    wait("w_xp", 10, n + 1)
                    fn(rw[n]["x"], PS[4 * n + 2][:, :].rearrange("p (h t) -> p h t", h=4)).then_inc(s["w_xa"], 1)
                for n in range(2):
                    wait("w_w1p", 2, n + 1)
                    fn(rw[n]["wk"][:, :, 0, :], PS[4 * n][:, 0:256].rearrange("p (h d) -> p h d", h=4)).then_inc(s["w_w1"], 1)
                for l in range(1, 6):
                    for n in range(2):
                        wait("w_t1p", 10, 2 * (l - 1) + n + 1)
                        fn(rw[n]["t1"], PS[4 * n + 3][:, :].rearrange("p (h t) -> p h t", h=4)).then_inc(s["w_t1"], 1)
                    if more and l == 2:
                        squash(m)
                    if more and l == 4:
                        out_gate(m)
                    if l < 5:
                        for n in range(2):
                            wait("w_xp", 10, 2 * l + n + 1)
                            fn(rw[n]["x"], PS[4 * n + 3][:, :].rearrange("p (h t) -> p h t", h=4)).then_inc(s["w_xa"], 1)
                    if more and l == 3:
                        rates(m)
                for n in range(2):
                    wait("w_uzp", 2, n + 1)
                    fn(rw[n]["uz"].rearrange("p a h d -> p h a d"),
                       PS[4 * n + 1][:, :].rearrange("p (h a d) -> p h a d", h=4, a=2), scale=-1.0).then_inc(s["w_uz"], 1)
                if more:
                    decays(m)
                for n in range(2):
                    for c in range(2):
                        wait("w_hp", 4, 2 * n + c + 1)
                        i = 2 * n + c
                        for p in range(2):
                            last = fn(S[:, i + 1, p, :], PS[4 * n + 3 * c][:, p * HD:(p + 1) * HD], scale=pend[:, p, i:i + 1])
                        last.then_inc(s["w_S"], 1)
                wait("w_yc", 1, 1)
                fn(sq, yb, ACT.Square).then_inc(s["w_sq"], 1)

            squash(None)
            rates(None)
            out_gate(None)
            decays(None)
            with act.Fori(0, TURNS - 1) as m:
                turn(m, True)
            turn(TURNS - 1, False)

            def modulated(dst, j, count, tr, done, bank=4):
                act.wait_ge(s[tr], count)
                for k in range(4):
                    last = fn(dst[:, k, :], PS[bank][:, k * P:(k + 1) * P], ACT.Identity, scale=s2[:, k:k + 1],
                              bias=mod[:, M_SH2 + k:M_SH2 + k + 1])
                last.then_inc(s[done], 1)

            for j in range(NT):
                act.wait_ge(s["op_x1"], j + 1)
                fn(xn2[:, j % 2], x1[:, j], ACT.Square, accum_out=ss[:, j % 2:j % 2 + 1]).then_inc(s["ss_ready"], 1)
                modulated(h2T, j, j + 1, "op_tp", "op_ta")

            act.wait_ge(s["rt_e1"], 1)
            fn(rt["gb"], rt["ga"], ACT.Exp).then_inc(s["rt_e2"], 1)
            act.wait_ge(s["rt_e1"], 2)
            fn(small["e2"], small["e2"], ACT.Exp).then_inc(s["rt_e2"], 1)

            act.wait_ge(s["rt_n"], 1)
            act.wait_ge(s["rt_ld"], 1)

            def gate(e):
                if isinstance(e, int):
                    return tbl[:, e, 2:3].bitcast(F32)
                return tbl[:, ds(e, 1), 2:3].rearrange("p o f -> p (o f)").bitcast(F32)

            def hidden(e, par, pre="m_", free=True):
                act.wait_ge(s[pre + "gu"], e + 1)
                if free:
                    act.wait_ge(s[pre + "act"], e - 1)
                fn(th[:, par, :], PS[2 + par][:, 0:P], ACT.Tanh, scale=0.5).then_inc(s[pre + "th"], 1)

            def result(e, par, pre="m_", free=None):
                act.wait_ge(s[pre + "dn"], e + 1)
                if free is not None:
                    act.wait_ge(s_sc[par], free)
                fn(yo[:, par, 0:512], PS[4 + 2 * par][:, :], scale=gate(e)).then_inc(s[pre + "ya"], 1)

            act.wait_ge(s["op_ps"], NT)
            modulated(xt[:, 0], 0, 1, "m_tx", "m_xa", 0)
            modulated(xt[:, 1], 1, 2, "m_tx", "m_xa", 0)
            hidden(0, 0, free=False)
            modulated(xt[:, 0], 2, 3, "m_tx", "m_xa", 0)
            hidden(1, 1, free=False)
            result(0, 0)
            modulated(xt[:, 1], 3, 4, "m_tx", "m_xa", 0)
            hidden(2, 0)
            result(1, 1)
            with act.Fori(0, 7) as g:
                for u in range(4):
                    modulated(xt[:, (4 + u) % 2], 0, g * 4 + (5 + u), "m_tx", "m_xa", 0)
                    hidden(g * 4 + (3 + u), (3 + u) % 2)
                    result(g * 4 + (2 + u), u % 2, free=g * 32 + 16 * ((2 + u) // 2))
            hidden(31, 1)
            result(30, 0, free=16 * 15)
            result(31, 1, free=16 * 15)
            act.wait_ge(s_sc[0], 16 * E // 2)
            n_ov = act.value_load(idy[0:1, 0:1], min_val=1, max_val=OVT)
            with act.Fori(0, n_ov) as i:
                modulated(xt[:, 0], 0, i + (E + 1), "m_tx", "m_xa", 0)
                hidden(i + E, 0, free=False)
                result(i + E, 0)

            for j in range(NT):
                act.wait_ge(s["f_x2"], j + 1)
                if j >= 2:
                    act.wait_ge(s_fo[j % 2], 16 * (j // 2))
                fn(fo[:, j % 2], x1[:, j], ACT.Square, accum_out=ss[:, j % 2:j % 2 + 1]).then_inc(s["ss_ready"], 1)

        @block.vector
        def _(dve):
            ch = Chain(dve, s["chain_dve"])
            tt, ts, stt = dve.tensor_tensor, dve.tensor_scalar, dve.scalar_tensor_tensor

            def flat3(ap):
                return ap.rearrange("p a t -> p (a t)")

            dve.wait_ge(s["ld_c"], 16)
            dve.wait_ge(s["silu_t"], 1)
            ch.step(ts(ct[:, :], ct[:, :], 0.5, 0.5, ALU.mult, ALU.add))
            tt(cc[:, :], cc[:, :], ct[:, :], ALU.mult).then_inc(s["silu_ready"], 1)
            def mean_square(j, phase):
                dve.wait_ge(s["ss_ready"], phase * NT + j + 1)
                ts(ss[:, j % 2:j % 2 + 1], ss[:, j % 2:j % 2 + 1], 1.0 / D, EPS, ALU.mult, ALU.add).then_inc(s["ms_ready"], 1)

            def normed(j):
                mean_square(j, 0)
                dve.wait_ge(s["rstd_ready"], j + 1)
                dve.wait_ge(s_x[j % 2], 16 * (j // 2 + 1))
                ts(xn[:, j % 2], xin[:, j % 2], rs[:, j % 2:j % 2 + 1], None, ALU.mult).then_inc(s["xn_ready"], 1)

            def summed(dst, src, done):
                ch.step(ts(dst, src[:, 0], cc[:, 0:1], None, ALU.mult))
                for k in range(1, KD):
                    last = stt(dst, src[:, k], cc[:, k:k + 1], dst, ALU.mult, ALU.add)
                    if k < KD - 1:
                        ch.step(last)
                last.then_inc(s[done], 1)

            dve.wait_ge(s["silu_ready"], 1)
            for b in range(4):
                dve.wait_ge(s_ada[b], 16)
                summed(acc[:, b], ada[:, b], "acc_ready")
            dve.wait_ge(s["sel_ready"], 1)
            dve.reciprocal(rc16[:, :, :], rc16[:, :, :]).then_inc(s["rt_c"], 1)
            normed(0)
            normed(1)
            dve.wait_ge(s["prm_t"], 1)
            dve.tensor_copy(pc[:, :], PS[7][:, 0:NR]).then_inc(s["prm_ready"], 1)
            dve.wait_ge(s["prm_ready"], 1)
            ch.note(ts(hp[:, 0:4], pc[:, R_W0:R_W0 + 4], 0.5, None, ALU.mult))
            ch.note(ts(hp[:, 4:6], pc[:, R_KA:R_KA + 2], 0.5, None, ALU.mult))
            ch.note(ts(hp[:, 6:8], pc[:, R_KA:R_KA + 2], -0.5, 1.0, ALU.mult, ALU.add))
            for p in range(2):
                ch.note(ts(brk[:, p, :], bones[:, :], pc[:, R_RK + p:R_RK + p + 1], None, ALU.mult))
            dve.wait_ge(s["mod1_ps"], 1)
            ch.step(tt(mod[:, 0:16], PS[6][:, 0:16], pc[:, 0:16], ALU.add))
            stt(s1[:, :], mod[:, M_SC1:M_SC1 + 8], 1.0, pc[:, R_G1:R_G1 + 8], ALU.add, ALU.mult).then_inc(s["mod1_ready"], 1)
            dve.wait_ge(s["mod1_ready"], 1)
            for j in range(NT):
                dve.wait_ge(s["hT_tr"], j + 1)
                for k in range(4, KD):
                    last = ts(hT[:, k, j * P:(j + 1) * P], PS[2 * (j % 2) + 1][:, (k - 4) * P:(k - 3) * P],
                              s1[:, k:k + 1], mod[:, M_SH1 + k:M_SH1 + k + 1], ALU.mult, ALU.add)
                last.then_inc(s["hT_dve"], 1)
                if j + 2 < NT:
                    normed(j + 2)

            def projected(i, par, blk=None):
                dve.wait_ge(s["proj_ps"], i + 1)
                dst = pT[:, ORDER[i], PAD + 512:PAD + 1024] if blk is None else \
                    pT[:, ds(blk, 1), PAD + 512:PAD + 1024].rearrange("p o t -> p (o t)")
                dve.tensor_copy(dst, PS[2 * par + 1][:, :]).then_inc(s["proj_dve"], 1)

            def attended(nb):
                dve.wait_ge(s["att_o"], nb + 1)
                tok = slice(nb * P, nb * P + P) if isinstance(nb, int) else ds(nb * P, P)
                dve.tensor_copy(yT[:, 2:4, tok], PS[7][:, 0:2 * P].rearrange("p (a t) -> p a t", a=2)).then_inc(s["att_y"], 1)

            def softmax(nb, par):
                k0 = 1 if isinstance(nb, int) and nb == 0 else 0
                dve.wait_ge(s["att_qk"], nb + 1)
                for h in range(4):
                    slope = 2.0 ** (-8.0 * (h + 1) / 4)
                    ch.note(stt(sc[:, par, h, k0 * P:], adist[:, k0 * P:], slope,
                                PS[4 + h // 2][:, (h % 2) * 256 + k0 * P:(h % 2 + 1) * 256], ALU.mult, ALU.add))
                ch.wait()
                ch.step(dve.tensor_reduce(mx[:, :], sc[:, par, :, k0 * P:], AX.X, ALU.max))
                ch.step(tt(mx[:, :], mx[:, :], sink[:, :], ALU.max))
                ch.note(tt(es[:, :], sink[:, :], mx[:, :], ALU.subtract))
                ts(nm[:, :], mx[:, :], -1.0, None, ALU.mult).then_inc(s["att_nm"], 1)
                dve.wait_ge(s["att_p"], nb + 1)
                ch.step(tt(rd[:, :], sm[:, :], es[:, :], ALU.add))
                ch.step(dve.reciprocal(rd[:, :], rd[:, :]))
                for h in range(4):
                    last = ts(sc[:, par, h, k0 * P:], sc[:, par, h, k0 * P:], rd[:, h:h + 1], None, ALU.mult)
                last.then_inc(s["att_pn"], 1)

            def flipped(nb):
                k0 = 1 if isinstance(nb, int) and nb == 0 else 0
                dve.wait_ge(s["att_tp"], nb + 1)
                dve.tensor_copy(ptT[:, 2:4, k0:, :], PS[5][:, :].rearrange("p (h a b) -> p h a b", h=2, b=P)[:, :, k0:, :])\
                    .then_inc(s["att_tpd"], 1)

            dve.wait_ge(s["xn_ready"], NT)
            dve.wait_ge(s["hT_tr"], NT)
            dve.memset(ptT[:, :, 0, :], 0.0)
            dve.memset(vt[:, 0, 0, :], 0.0)
            dve.memset(qz, 0.0).then_inc(s["att_zero"], 1)
            dve.wait_ge(s["pad_ready"], 1)
            for i in range(N_ATT):
                projected(i, i % 2)
            dve.wait_ge(s["ld_misc"], 16 * 8)
            dve.wait_ge(s["gtb_ld"], 32)

            def half_blocks(n, loads):
                if not isinstance(n, int) or n >= 1:
                    dve.wait_ge(s["mod2_ps"], n)
                for par in range(2):
                    dve.wait_ge(s_ada[par], loads)
                    summed(acb[:, par], adb[:, par], "acb_ready")

            def gate_columns(n):
                dve.wait_ge(s["mod2_ps"], n + 1)
                dst = gtb[:, n // 6, (n % 2) * 512:(n % 2 + 1) * 512]
                tt(dst, dst, PS[6][:, :], ALU.add).then_inc(s["mod2_ready"], 1)

            def mod_columns(n):
                dve.wait_ge(s["mod2_ps"], n + 1)
                tt(mod[:, ds(n * 4 + 16, 4)], PS[6][:, 0:4], pc[:, ds(n * 4 + 16, 4)], ALU.add).then_inc(s["mod2_ready"], 1)

            half_blocks(0, 32)
            for n in range(2):
                projected(SLOT0 - 1 + n, n)
                softmax(n, n)
                if n == 1:
                    flipped(0)
                gate_columns(n)
                half_blocks(n + 1, 48 + 16 * n)
            with dve.Fori(0, 2) as g:
                ch.enter(g, 2 * (9 + 2 * (KD - 1)))
                for u in range(2):
                    projected(g * 2 + (6 + u), u, g * 2 + (B_BG + u))
                    attended(g * 2 + u)
                    softmax(g * 2 + (2 + u), u)
                    flipped(g * 2 + (1 + u))
                    mod_columns(g * 2 + (2 + u))
                    half_blocks(g * 2 + (3 + u), g * 32 + 16 * (5 + u))
            ch.leave(2)
            for n in (6, 7):
                projected(n + 4, n % 2)
                attended(n - 2)
                softmax(n, n % 2)
                flipped(n - 1)
                gate_columns(n)
                if n == 6:
                    half_blocks(7, 16 * 9)
            projected(12, 0)
            attended(6)
            flipped(7)
            projected(13, 1)
            attended(7)
            for i in range(14, NB):
                projected(i, i % 2)

            dve.wait_ge(s["pool_y"], 4)
            dve.wait_ge(s["conv_y"], 2)
            dve.wait_ge(s["pad_ready"], 2)
            dve.wait_ge(s["att_y"], NT)
            dve.wait_ge(s["proj_act"], NB)
            dve.wait_ge(s["proj_dve"], NB)
            dve.memset(ct[:, :], 0.0).then_inc(s["w_yT"], 1)

            def mixed(m):
                cnt = front_counts(m)[0]
                dve.wait_ge(s["w_df"], cnt(1, 1))
                for b in range(ZB):
                    tok = pT[:, b, PAD:PAD + W2] if m is None else pT[:, b, ds(m * W2 + (W2 + PAD), W2)]
                    last = stt(z[:, b, :], df[:, b, :], pc[:, R_MU + b:R_MU + b + 1], tok, ALU.mult, ALU.add)
                last.then_inc(s["w_z"], 1)
                dve.wait_ge(s["w_z"], cnt(1, 1))
                for p in range(2):
                    last = ts(kkr[:, p], z[:, B_K + p, :], pc[:, R_KK + p:R_KK + p + 1], None, ALU.mult)
                last.then_inc(s["w_kkr"], 1)

            def sigmoid(m):
                dve.wait_ge(s["w_tanh"], front_counts(m)[0](1, 1))
                ts(lt[64:128, :], lt[64:128, :], 0.5, 0.5, ALU.mult, ALU.add).then_inc(s["w_sg"], 1)

            def key_norm(m):
                dve.wait_ge(s["w_ss"], front_counts(m)[1])
                ts(nrm[:, :], PS[5][:, 0:8], 1e-24, None, ALU.max).then_inc(s["w_nrm"], 1)

            def log_decays(m):
                dve.wait_ge(s["w_th"], front_counts(m)[0](1, 1))
                c = -0.5 * float(np.exp(-0.5))
                ch.step(ts(lw, lw, 1.0, c, ALU.add, ALU.mult))
                ch.step(dve.tensor_tensor_scan(flat3(Lc), rmask[:, :], flat3(lw), 0.0, ALU.mult, ALU.add))
                tt(Lm, Lc, lw, ALU.subtract).then_inc(s["w_L"], 1)

            def keys(m):
                dve.wait_ge(s["w_tha"], front_counts(m)[0](1, 1))
                for p in range(2):
                    ch.note(ts(Kt[:, p], aa[:, p], hp[:, 4 + p:5 + p], hp[:, 6 + p:7 + p], ALU.mult, ALU.add))
                ch.wait()
                ch.note(tt(z[:, B_K:B_K + 2, :], z[:, B_K:B_K + 2, :], Kt, ALU.mult))
                ch.note(ts(aa, aa, 0.5, 0.5, ALU.mult, ALU.add))

            def key_power(m):
                dve.wait_ge(s["w_nrt"], front_counts(m)[1])
                dve.tensor_copy(nrT[:, :], PS[5][0:8, P:2 * P]).then_inc(s["w_nrT"], 1)

            def normed_keys(m):
                dve.wait_ge(s["w_nrb"], front_counts(m)[1])
                ch.step(tt(flat3(kkr), flat3(kkr), PS[0][:, :], ALU.mult))

            def turn(m, more):
                def wait(name, per, k):
                    dve.wait_ge(s[name], m * per + k)

                wait("w_exp", 1, 1)
                ch.note(dve.tensor_copy(pend, Pc[:, :, CH - 1::CH]))
                ch.note(tt(KR[:, :, 0, :], kkr, Pm, ALU.mult))
                ch.note(tt(KR[:, :, 1, :], z[:, B_R:B_R + 2, :], Pc, ALU.mult))
                ch.note(tt(Kt, z[:, B_K:B_K + 2, :], iP, ALU.mult))
                ch.note(tt(rk, z[:, B_R:B_R + 2, :], z[:, B_K:B_K + 2, :], ALU.mult))
                ch.step(tt(aa, kkr, aa, ALU.mult))
                tt(Bt, aa, iP, ALU.mult).then_inc(s["w_ops"], 1)
                for n in range(2):
                    t = rw[n]
                    wait("w_tok", 2, n + 1)
                    ch.note(dve.tensor_copy(t["vt"], PS[4 * n + 1][:, 0:256].rearrange("p (h d) -> p h d", h=4)))
                    dve.tensor_copy(t["wk"][:, :, 1, :], PS[4 * n + 1][:, 256:512].rearrange("p (h d) -> p h d", h=4))\
                        .then_inc(s["w_tkd"], 1)
                    wait("w_abp", 2, n + 1)
                    for q in range(2):
                        last = tt(t["ab"][:, q::2].rearrange("p h a t -> p h (a t)"),
                                  PS[4 * n + 2 + q][:, :].rearrange("p (h x) -> p h x", h=2),
                                  mskb(), ALU.mult)
                    last.then_inc(s["w_ab"], 1)
                for n in range(2):
                    wait("w_bl", 12, n + 1)
                    tt(rw[n]["xt"], ident[:, :].unsqueeze(1).to_broadcast([P, 4, P]), rw[n]["bl"], ALU.subtract)\
                        .then_inc(s["w_xt"], 1)
                for n in range(2):
                    wait("w_akp", 2, n + 1)
                    for q in range(2):
                        last = tt(rw[n]["ak"][:, q::2].rearrange("p h a t -> p h (a t)"),
                                  PS[4 * n + q][:, :].rearrange("p (h x) -> p h x", h=2), mskb(), ALU.mult)
                    last.then_inc(s["w_ak"], 1)
                for l in range(1, 6):
                    for n in range(2):
                        wait("w_x2p", 10, 2 * (l - 1) + n + 1)
                        tt(rw[n]["xt"], rw[n]["xt"], PS[4 * n + 2][:, :].rearrange("p (h t) -> p h t", h=4), ALU.subtract)\
                            .then_inc(s["w_xt"], 1)
                    if more:
                        for step in ((mixed,), (sigmoid,), (key_norm,), (log_decays, keys), (key_power,))[l - 1]:
                            step(m)
                if more:
                    normed_keys(m)
                for n in range(2):
                    wait("w_rep", 2, n + 1)
                    tt(rw[n]["re"], PS[4 * n + 3][:, 0:256].rearrange("p (a t) -> p a t", a=2),
                       KR[:, :, 1, n * P:(n + 1) * P], ALU.add).then_inc(s["w_re"], 1)
                    wait("w_gp", 2, n + 1)
                    for c in range(2):
                        for h in range(2):
                            r = slice(64 * h, 64 * h + 64)
                            last = tt(G[r, 4 * n + 2 * c:4 * n + 2 * c + 2, r],
                                      PS[4 * n + 2 - c][r, 0:128].rearrange("p (q d) -> p q d", q=2),
                                      ident[r, r].unsqueeze(1).to_broadcast([64, 2, 64]), ALU.add)
                    last.then_inc(s["w_G"], 1)
                for n in range(2):
                    wait("w_yp", 2, n + 1)
                    dve.tensor_copy(yb[:, :, n * P:(n + 1) * P], PS[4 * n + 1][:, 0:256].rearrange("p (a t) -> p a t", a=2))\
                        .then_inc(s["w_y"], 1)
                wait("w_mean", 1, 1)
                stt(flat3(yb), PS[2][:, :], -1.0 / HD, flat3(yb), ALU.mult, ALU.add).then_inc(s["w_yc"], 1)
                wait("w_bonp", 1, 1)
                wait("w_cp", 1, 1)
                ch.note(tt(flat3(bon), PS[5][:, :], flat3(zv), ALU.mult))
                count = tail_norm(m)
                dve.wait_ge(s["w_ss"], count)
                ts(nrm[:, :], PS[3][:, 0:8], 1.0 / HD, GN_EPS, ALU.mult, ALU.add).then_inc(s["w_nrm"], 1)
                dve.wait_ge(s["w_nrt"], count)
                dve.tensor_copy(nrT[:, :], PS[3][0:8, P:2 * P]).then_inc(s["w_nrT"], 1)
                dve.wait_ge(s["w_nrb"], count)
                ch.step(tt(flat3(yb), flat3(yb), PS[4][:, :], ALU.mult))
                for p in range(2):
                    last = ts(yb[:, p], yb[:, p], pc[:, R_LNG + p:R_LNG + p + 1], pc[:, R_LNB + p:R_LNB + p + 1], ALU.mult, ALU.add)
                ch.step(last)
                ch.step(tt(yb, yb, bon, ALU.add))
                tok = slice(m * W2, (m + 1) * W2) if isinstance(m, int) else ds(m * W2, W2)
                tt(yT[:, 6:8, tok], yb, gg, ALU.mult).then_inc(s["w_yT"], 1)

            for step in (mixed, sigmoid, key_norm, log_decays, keys, key_power, normed_keys):
                step(None)
            with dve.Fori(0, TURNS - 1) as m:
                ch.enter(m, 19)
                turn(m, True)
            ch.leave(TURNS - 1)
            turn(TURNS - 1, False)

            dve.wait_ge(s["mod2_ready"], 8)
            ch.step(stt(s2[:, :], mod[:, M_SC2:M_SC2 + 8], 1.0, pc[:, R_G2:R_G2 + 8], ALU.add, ALU.mult))

            ch.step(dve.tensor_tensor_scan(rt["i32"], ones[:, 0:E], ones[:, 0:E], -1.0, ALU.mult, ALU.add))
            ch.step(ts(rt["thr"], rt["i32"][:, 0:OVT], float(CAP), float(CAP), ALU.mult, ALU.add))

            dve.wait_ge(s["xr_ld"], 16 * NT)

            def modulated(dst, count, tr, done, bank=5):
                dve.wait_ge(s[tr], count)
                for k in range(4, KD):
                    last = ts(dst[:, k, :], PS[bank][:, (k - 4) * P:(k - 3) * P], s2[:, k:k + 1],
                              mod[:, M_SH2 + k:M_SH2 + k + 1], ALU.mult, ALU.add)
                last.then_inc(s[done], 1)

            for j in range(NT):
                dve.wait_ge(s["op_ps"], j + 1)
                if j >= 2:
                    dve.wait_ge(s_st[j % 2], 16 * (j // 2))
                for h in range(2):
                    ch.note(tt(xn2[:, j % 2, h * 512:(h + 1) * 512], PS[2 * (j % 2) + h][:, :], gtb[:, 0, h * 512:(h + 1) * 512],
                               ALU.mult))
                ch.wait()
                tt(x1[:, j], x1[:, j], xn2[:, j % 2], ALU.add).then_inc(s["op_x1"], 1)
                mean_square(j, 1)
                dve.wait_ge(s["rstd_ready"], NT + j + 1)
                ts(xn2[:, j % 2], x1[:, j], rs[:, j % 2:j % 2 + 1], None, ALU.mult).then_inc(s["op_xn"], 1)
                modulated(h2T, j + 1, "op_tp", "op_td")
                dve.wait_ge(s["op_lg"], j + 1)
                tt(lg[:, j], PS[6][:, 0:GROUPS + E], rbias[:, :], ALU.add).then_inc(s["op_lgd"], 1)
            dve.wait_ge(s["op_lgd"], NT)

            q = small

            def b3(ap, n):
                return ap.unsqueeze(2).to_broadcast([P, NT, n])

            def row3(ap, n):
                return ap.unsqueeze(1).to_broadcast([P, NT, n])

            L = lg[:, :, 0:GROUPS]
            X = lg[:, :, GROUPS:]

            def pick(vals, n, top, where, hot):
                ch.step(dve.tensor_reduce(top, vals, AX.X, ALU.max))
                key = rt["ky"][:, :, 0:n]
                ch.step(tt(key, vals, b3(top, n), ALU.is_ge))
                ch.step(ts(key, key, -64.0, 64.0, ALU.mult, ALU.add))
                ch.step(tt(key, key, row3(rt["i32"][:, 0:n], n), ALU.add))
                ch.step(dve.tensor_reduce(where, key, AX.X, ALU.min))
                ch.step(tt(hot, row3(rt["i32"][:, 0:n], n), b3(where, n), ALU.is_equal))

            pick(L, GROUPS, q["gm"], q["gi"], rt["goh"])
            tt(rt["ga"], L, b3(q["gm"], GROUPS), ALU.subtract).then_inc(s["rt_e1"], 1)
            ch.step(ts(rt["goh"], rt["goh"], 1.0, -NEG, ALU.subtract, ALU.mult))
            for e in range(GROUPS):
                ch.note(tt(rt["xm"][:, :, e * EPG:(e + 1) * EPG], X[:, :, e * EPG:(e + 1) * EPG],
                           rt["goh"][:, :, e:e + 1].to_broadcast([P, NT, EPG]), ALU.add))
            ch.wait()
            pick(rt["xm"], E, q["m1"], q["i1"], rt["oh1"])
            ch.step(ts(rt["tmp"], rt["oh1"], 10 * NEG, None, ALU.mult))
            ch.step(tt(rt["xm"], rt["xm"], rt["tmp"], ALU.add))
            pick(rt["xm"], E, q["m2"], q["i2"], rt["oh2"])
            tt(q["e2"], q["m2"], q["m1"], ALU.subtract).then_inc(s["rt_e1"], 1)
            tt(rt["tmp"], rt["oh1"], rt["oh2"], ALU.add).then_inc(s["rt_oh"], 1)
            ch.note(dve.tensor_tensor_scan(i128, ones[:, :], ones[:, :], -1.0, ALU.mult, ALU.add))
            ch.note(dve.tensor_copy(rowf, out_row[:, :]))
            dve.wait_ge(s["rt_e2"], 1)
            ch.step(dve.tensor_reduce(q["gp"], rt["gb"], AX.X, ALU.add))
            dve.wait_ge(s["rt_e2"], 2)
            ch.step(ts(q["g1"], q["e2"], 1.0, None, ALU.add))
            ch.step(tt(q["g1"], q["g1"], q["gp"], ALU.mult))
            ch.step(dve.reciprocal(q["g1"], q["g1"]))
            ch.step(tt(q["g2"], q["g1"], q["e2"], ALU.mult))
            dve.wait_ge(s["rt_pos"], 1)
            ch.step(dve.memset(rt["pre"][:, 0], 0.0))
            for j in range(NT):
                ch.step(tt(rt["pre"][:, j + 1], rt["pre"][:, j], PS[7][:, 256 + j * E:256 + (j + 1) * E], ALU.add))
            ch.step(tt(rt["pos"], PS[7][:, 0:256].rearrange("p (j e) -> p j e", e=E), rt["pre"][:, 0:NT], ALU.add))
            n_e = rt["pre"][:, NT]
            cmp = rt["cmp"].rearrange("p (e i) -> p e i", i=OVT)
            ch.step(tt(cmp, n_e.unsqueeze(2).to_broadcast([P, E, OVT]), rt["thr"].unsqueeze(1).to_broadcast([P, E, OVT]), ALU.is_gt))
            ch.step(dve.tensor_reduce(rt["nov"], cmp, AX.X, ALU.add))
            ch.step(dve.tensor_tensor_scan(rt["ci"], ones[:, 0:E], rt["nov"], 0.0, ALU.mult, ALU.add))
            ch.note(tt(rt["ob"], rt["ci"], rt["nov"], ALU.subtract))
            cm2 = rt["cmp"].rearrange("p (i e) -> p i e", e=E)
            ch.step(tt(cm2, rt["ci"].unsqueeze(1).to_broadcast([P, OVT, E]),
                       rt["i32"][:, 0:OVT].unsqueeze(2).to_broadcast([P, OVT, E]), ALU.is_le))
            ch.step(dve.tensor_reduce(rt["thr"], cm2, AX.X, ALU.add))
            ch.note(ts(eidt[:, :], rt["thr"], float(E - 1), None, ALU.min))
            ts(idy[:, 0:1], rt["ci"][:, E - 1:E], 1.0, None, ALU.max).then_inc(s["rt_n"], 1)
            sides = [(rt["oh1"], q["i1"], q["g1"], q["q1"], q["b1"], q["c1"], rt["tmp"]),
                     (rt["oh2"], q["i2"], q["g2"], q["q2"], q["b2"], q["c2"], rt["ky"])]

            def step(f):
                for n, side in enumerate(sides):
                    ch.note(f(n, *side))
                ch.wait()

            step(lambda n, hot, at, g_, pos, base, c_, tmp: tt(tmp, hot, rt["pos"], ALU.mult))
            step(lambda n, hot, at, g_, pos, base, c_, tmp: dve.tensor_reduce(pos, tmp, AX.X, ALU.add))
            step(lambda n, hot, at, g_, pos, base, c_, tmp: tt(tmp, hot, row3(rt["ob"], E), ALU.mult))
            step(lambda n, hot, at, g_, pos, base, c_, tmp: dve.tensor_reduce(base, tmp, AX.X, ALU.add))
            step(lambda n, hot, at, g_, pos, base, c_, tmp: tt(base, base, at, ALU.subtract))
            step(lambda n, hot, at, g_, pos, base, c_, tmp: ts(base, base, float(CAP), float(CAP * (E - 1)), ALU.mult, ALU.add))
            step(lambda n, hot, at, g_, pos, base, c_, tmp: ts(c_, pos, float(CAP), None, ALU.is_ge))
            step(lambda n, hot, at, g_, pos, base, c_, tmp: tt(base, base, c_, ALU.mult))
            step(lambda n, hot, at, g_, pos, base, c_, tmp: tt(base, base, pos, ALU.add))
            step(lambda n, hot, at, g_, pos, base, c_, tmp: ts(c_, at, float(CAP), None, ALU.mult))
            step(lambda n, hot, at, g_, pos, base, c_, tmp: tt(slot[:, n * NT:(n + 1) * NT], base, c_, ALU.add))
            step(lambda n, hot, at, g_, pos, base, c_, tmp: dve.tensor_copy(gatef[:, n * NT:(n + 1) * NT], g_))
            ch.note(ts(tii[:, 0], slot[:, :], 7, None, ALU.logical_shift_right))
            ch.step(ts(tii[:, 1], slot[:, :], CAP - 1, None, ALU.bitwise_and))
            ch.step(dve.tensor_copy(tif, tii))
            across = [P, 2 * NT, TILES]
            ch.step(tt(hots[:, :, 0, :], i128[:, 0:TILES].unsqueeze(1).to_broadcast(across),
                       tif[:, 0].unsqueeze(2).to_broadcast(across), ALU.is_equal))
            ch.note(tt(hots[:, :, 1, :], hots[:, :, 0, :], rowf.unsqueeze(2).to_broadcast(across), ALU.mult))
            ch.note(tt(hots[:, :, 2, :], hots[:, :, 0, :], gatef.unsqueeze(2).to_broadcast(across), ALU.mult))
            for c in range(4):
                r = slice(4 * c, 4 * c + 4)
                tt(lanes[:, r], i128.unsqueeze(1).to_broadcast([P, 4, CAP]),
                   tif[:, 1, r].unsqueeze(2).to_broadcast([P, 4, CAP]), ALU.is_equal).then_inc(s["rt_hot"], 1)
            dve.wait_ge(s["rt_tab"], 1)
            filled, row_, gate_ = (PS[7][:, q_ * TILES:(q_ + 1) * TILES] for q_ in range(3))
            ch.note(ts(tab[:, 0], filled, -float(OOB), float(OOB), ALU.mult, ALU.add))
            ch.step(ts(tab[:, 1], row_, float(T), -float(T), ALU.is_ge, ALU.mult))
            ch.note(tt(tab[:, 1], tab[:, 1], tab[:, 0], ALU.add))
            ch.note(dve.tensor_copy(tbl[:, 0:TILES, 2].bitcast(F32), gate_))
            ch.note(tt(tbl[:, 0:TILES, 0], row_, tab[:, 0], ALU.add))
            ch.wait()
            tt(tbl[:, 0:TILES, 1], row_, tab[:, 1], ALU.add).then_inc(s["rt_ld"], 1)

            dve.wait_ge(s["rt_n"], 1)
            dve.wait_ge(s["rt_ld"], 1)

            def gate(e):
                if isinstance(e, int):
                    return tbl[:, e, 2:3].bitcast(F32)
                return tbl[:, ds(e, 1), 2:3].rearrange("p o f -> p (o f)").bitcast(F32)

            def hidden(e, par, pre="m_", free=True):
                dve.wait_ge(s[pre + "th"], e + 1)
                ch.step(stt(a1[:, par, :], th[:, par, :], 1.0, PS[2 + par][:, 0:P], ALU.add, ALU.mult))
                if free:
                    dve.wait_ge(s[pre + "dn"], e - 1)
                stt(ac[:, par, :], a1[:, par, :], 0.5, PS[2 + par][:, P:2 * P], ALU.mult, ALU.mult).then_inc(s[pre + "act"], 1)

            def result(e, par, pre="m_", free=None):
                dve.wait_ge(s[pre + "dn"], e + 1)
                if free is not None:
                    dve.wait_ge(s_sc[par], free)
                ts(yo[:, par, 512:], PS[5 + 2 * par][:, :], gate(e), None, ALU.mult).then_inc(s[pre + "yd"], 1)

            modulated(xt[:, 0], 1, "m_tx", "m_xd", 1)
            modulated(xt[:, 1], 2, "m_tx", "m_xd", 1)
            hidden(0, 0, free=False)
            modulated(xt[:, 0], 3, "m_tx", "m_xd", 1)
            hidden(1, 1, free=False)
            result(0, 0)
            modulated(xt[:, 1], 4, "m_tx", "m_xd", 1)
            hidden(2, 0)
            result(1, 1)
            with dve.Fori(0, 7) as g:
                ch.enter(g, 4)
                for u in range(4):
                    modulated(xt[:, (4 + u) % 2], g * 4 + (5 + u), "m_tx", "m_xd", 1)
                    hidden(g * 4 + (3 + u), (3 + u) % 2)
                    result(g * 4 + (2 + u), u % 2, free=g * 32 + 16 * ((2 + u) // 2))
            ch.leave(7)
            hidden(31, 1)
            result(30, 0, free=16 * 15)
            result(31, 1, free=16 * 15)
            dve.wait_ge(s_sc[0], 16 * E // 2)
            n_ov = dve.value_load(idy[0:1, 0:1], min_val=1, max_val=OVT)
            with dve.Fori(0, n_ov) as i:
                ch.enter(i, 1)
                modulated(xt[:, 0], i + (E + 1), "m_tx", "m_xd", 1)
                hidden(i + E, 0, free=False)
                result(i + E, 0)

            dve.wait_ge(s["ld_fg"], 16)
            def sums(j):
                a_ = yab[:, j % 4, 0]
                dve.wait_ge(s["f_a"], j + 1)
                tt(a_, a_, gtb[:, 1], ALU.mult).then_inc(s["f_c"], 1)
                dve.wait_ge(s["f_c"], j + 1)
                tt(x1[:, j], x1[:, j], a_, ALU.add).then_inc(s["f_x2"], 1)

            sums(0)
            for j in range(NT):
                if j + 1 < NT:
                    sums(j + 1)
                mean_square(j, 2)
                dve.wait_ge(s["rstd_ready"], 2 * NT + j + 1)
                dve.wait_ge(s["f_x2"], j + 1)
                stt(fo[:, j % 2], x1[:, j], rs[:, j % 2:j % 2 + 1], fg, ALU.mult, ALU.mult).then_inc(s["f_o"], 1)


_INS = ["x", "c", "w_ada", "b_ada", "norm1_g", "norm2_g", "w_in", "w_out", "pool_w", "pool_scale", "attn_sinks", "conv_w",
        "rwkv_mu", "rwkv_w0", "rwkv_w2", "rwkv_a0", "rwkv_a2", "rwkv_g2", "rwkv_k_k", "rwkv_k_a", "rwkv_r_k", "rwkv_ln_g",
        "rwkv_ln_b", "moe_w_grp", "moe_b_grp", "moe_w_exp", "moe_b_exp", "moe_w_gate", "moe_w_up", "moe_w_down", "final_g"]


def kernel(**inputs):
    import numpy as _np
    import concourse.bacc as _bacc
    from concourse import mybir as _mybir
    from concourse.bass_utils import run_bass_kernel_spmd as _run

    nc = _bacc.Bacc("TRN2", target_bir_lowering=False, num_devices=1)
    arrays, args = {}, {}
    for name in _INS:
        a = _np.ascontiguousarray(inputs[name])
        arrays[f"in_{name}"] = a
        args[name] = nc.dram_tensor(f"in_{name}", a.shape, _mybir.dt.from_np(a.dtype), kind="ExternalInput").ap()
    out = nc.dram_tensor("out_dram", (1, T, D), F32, kind="ExternalOutput").ap()
    build(nc, args, out)
    r = _run(nc, [arrays], core_ids=[0])
    return r.results[0]["out_dram"]
```
